# Optimizing a Trainium2 kernel written in Bass

```python
import math
import jax
import jax.numpy as jnp
from jax import lax
import numpy as np
import jax, jax.numpy as jnp

D_MODEL = 1024
BATCH = 1
SEQ = 1024
DEPTH = 2

GRID_W = 64
CTX_LEN = 256
EPS = 1e-6
POOL_GROUPS = 4
POOL_WINDOWS = (2, 4, 8, 16)
POOL_WIDTH = D_MODEL // 4
POOL_GROUP_DIM = POOL_WIDTH // POOL_GROUPS
HEAD_DIM = 128
N_Q_HEADS = (D_MODEL - POOL_WIDTH) // HEAD_DIM
N_KV_HEADS = 2
ATT_WIDTH = N_Q_HEADS * HEAD_DIM
KV_WIDTH = N_KV_HEADS * HEAD_DIM
Q_BLOCK = 128
ROPE_THETA = 10000.0
ROPE_FREQS = HEAD_DIM // 4
EVEN_SPLITS = (POOL_WIDTH, 2 * POOL_WIDTH, 2 * POOL_WIDTH + ATT_WIDTH,
               2 * POOL_WIDTH + ATT_WIDTH + KV_WIDTH, 2 * POOL_WIDTH + ATT_WIDTH + 2 * KV_WIDTH)
EVEN_IN = 2 * POOL_WIDTH + 2 * ATT_WIDTH + 2 * KV_WIDTH
EVEN_MIX = POOL_WIDTH + ATT_WIDTH
HY_ORDER = 2
HY_WIDTH = 3 * D_MODEL // 4
HY_EMB = 33
HY_BANDS = (HY_EMB - 1) // 2
HY_HIDDEN = 64
HY_DECAY_TARGET = 1e-2
HY_FAST_DECAY = 0.3
HY_SLOW_DECAY = 1.5
FN_WIDTH = D_MODEL - HY_WIDTH
ODD_SPLITS = ((HY_ORDER + 1) * HY_WIDTH, (HY_ORDER + 2) * HY_WIDTH,
              (HY_ORDER + 2) * HY_WIDTH + FN_WIDTH)
ODD_IN = (HY_ORDER + 2) * HY_WIDTH + 2 * FN_WIDTH
ODD_MIX = HY_WIDTH + FN_WIDTH
N_EVEN = (DEPTH + 1) // 2
N_ODD = DEPTH // 2


def rmsnorm(x, g):
    xf = x.astype(jnp.float32)
    y = xf * lax.rsqrt(jnp.mean(xf * xf, axis=-1, keepdims=True) + EPS)
    return y.astype(x.dtype) * g

def modulation(cond, w_mod, b_mod):
    m = jax.nn.silu(cond) @ w_mod + b_mod
    return jnp.split(m, 3, axis=-1)

def to_heads(t, n_heads):
    return t.reshape(t.shape[:2] + (n_heads, HEAD_DIM))

def axial_rope_tables(row_idx, col_idx):
    inv_freq = ROPE_THETA ** (-jnp.arange(ROPE_FREQS, dtype=jnp.float32) / ROPE_FREQS)
    ang = jnp.stack([row_idx[:, None] * inv_freq, col_idx[:, None] * inv_freq], axis=1)
    ang = ang[:, None, :, None, :]
    return jnp.cos(ang), jnp.sin(ang)

def apply_rope(x, cos, sin):
    xr = x.reshape(x.shape[:-1] + (2, 2, ROPE_FREQS)).astype(jnp.float32)
    rot = jnp.concatenate([-xr[..., 1:, :], xr[..., :1, :]], axis=-2)
    return (xr * cos + rot * sin).astype(x.dtype).reshape(x.shape)

def blocked_attention(q, k, v):
    b, lq, hq, dh = q.shape
    hkv = k.shape[2]
    grp = hq // hkv
    nb = lq // Q_BLOCK
    qb = q.reshape(b, nb, Q_BLOCK, hkv, grp, dh).transpose(1, 0, 2, 3, 4, 5)
    scale = dh ** -0.5

    def one_block(qblk):
        s = jnp.einsum('bqhgd,bkhd->bhgqk', qblk, k, preferred_element_type=jnp.float32) * scale
        p = jax.nn.softmax(s, axis=-1).astype(v.dtype)
        return jnp.einsum('bhgqk,bkhd->bqhgd', p, v)

    o = lax.map(one_block, qb)
    return o.transpose(1, 0, 2, 3, 4, 5).reshape(b, lq, hq * dh)

def pool_mixer(u, w_grp, scale):
    b, L, _ = u.shape
    ug = u.reshape(b, L, POOL_GROUPS, POOL_GROUP_DIM).astype(jnp.float32)
    cs = jnp.concatenate([jnp.zeros((b, 1, POOL_GROUPS, POOL_GROUP_DIM), jnp.float32),
                          jnp.cumsum(ug, axis=1)], axis=1)
    t = jnp.arange(L)
    outs = []
    for gi, w in enumerate(POOL_WINDOWS):
        lo = jnp.clip(t - w // 2, 0, L)
        hi = jnp.clip(t + w // 2, 0, L)
        csg = cs[:, :, gi]
        win_sum = jnp.take(csg, hi, axis=1) - jnp.take(csg, lo, axis=1)
        cnt = (hi - lo).astype(jnp.float32)[None, :, None]
        outs.append(win_sum / cnt - ug[:, :, gi])
    d = jnp.stack(outs, axis=2).astype(u.dtype)
    y = jnp.einsum('blgc,gcd->blgd', d, w_grp)
    return y.reshape(b, L, POOL_WIDTH) * scale

def even_mix(a_val, a_gate, q, b_gate, k_all, v_all, pool_w, pool_scale, w_out):
    ya = pool_mixer(a_val, pool_w, pool_scale)
    yb = blocked_attention(q, k_all, v_all)
    y = jnp.concatenate([ya * jax.nn.silu(a_gate), yb * jax.nn.silu(b_gate)], axis=-1)
    return y @ w_out

def short_conv3(u, w, b):
    up = jnp.pad(u, ((0, 0), (1, 1), (0, 0)))
    return up[:, :-2] * w[0] + up[:, 1:-1] * w[1] + up[:, 2:] * w[2] + b

def hyena_filters(L, w1, b1, w2, b2, w3, freq):
    f32 = jnp.float32
    t = jnp.linspace(0.0, 1.0, L, dtype=f32)[:, None]
    w = 2.0 * math.pi * jnp.arange(L, dtype=f32)[:, None] / L
    f = jnp.linspace(1e-4, HY_BANDS - 1, HY_BANDS, dtype=f32)[None, :]
    emb = jnp.concatenate([t, jnp.cos(f * w), -jnp.sin(f * w)], axis=-1)
    fr = freq.astype(f32)
    hdn = jnp.sin(fr * (emb @ w1.astype(f32) + b1.astype(f32)))
    hdn = jnp.sin(fr * (hdn @ w2.astype(f32) + b2.astype(f32)))
    h = (hdn @ w3.astype(f32)).reshape(L, HY_ORDER, 2, HY_WIDTH)
    max_decay = math.log(HY_DECAY_TARGET) / HY_FAST_DECAY
    min_decay = math.log(HY_DECAY_TARGET) / HY_SLOW_DECAY
    deltas = jnp.linspace(min_decay, max_decay, HY_WIDTH, dtype=f32)
    decay = jnp.exp(-t * jnp.abs(deltas))
    h = h * decay[:, None, None, :]
    h = h / (jnp.sum(jnp.abs(h), axis=(0, 2), keepdims=True) + EPS)
    zero = jnp.zeros((1, HY_ORDER, HY_WIDTH), f32)
    return jnp.concatenate([h[:, :, 0], zero, h[:0:-1, :, 1]], axis=0)

def fft_long_conv(z, kfull):
    L = z.shape[1]
    zf = jnp.fft.rfft(z, n=2 * L, axis=1)
    kf = jnp.fft.rfft(kfull, n=2 * L, axis=0)
    return jnp.fft.irfft(zf * kf[None], n=2 * L, axis=1)[:, :L]

def hyena_mixer(u, conv_w, conv_b, w1, b1, w2, b2, w3, freq, skip):
    L = u.shape[1]
    uc = short_conv3(u, conv_w, conv_b)
    v, x1, x2 = jnp.split(uc, HY_ORDER + 1, axis=-1)
    k = hyena_filters(L, w1, b1, w2, b2, w3, freq)
    z = v.astype(jnp.float32)
    for o, gate_o in enumerate((x1, x2)):
        z = gate_o.astype(jnp.float32) * (fft_long_conv(z, k[:, o]) + skip[o].astype(jnp.float32) * z)
    return z.astype(u.dtype)

def fourier_mixer(u, w):
    y = jnp.fft.fft2(u.astype(jnp.float32), axes=(1, 2), norm='ortho').real
    return y.astype(u.dtype) @ w

def odd_mix(h, w_in, w_out, fn_w, conv_w, conv_b, w1, b1, w2, b2, w3, freq, skip):
    hy_in, hy_gate, fn_in, fn_gate = jnp.split(h @ w_in, ODD_SPLITS, axis=-1)
    yc = hyena_mixer(hy_in, conv_w, conv_b, w1, b1, w2, b2, w3, freq, skip)
    yd = fourier_mixer(fn_in, fn_w)
    y = jnp.concatenate([yc * jax.nn.silu(hy_gate), yd * jax.nn.silu(fn_gate)], axis=-1)
    return y @ w_out

def first_inputs(seed: int = 0) -> dict:
    key = jax.random.key(seed)
    ks = jax.random.split(key, 26)

    def nrm(k, shape, s):
        return jax.random.normal(k, shape, jnp.float32) * s

    return {
        'x': nrm(ks[0], (BATCH, SEQ, D_MODEL), 1.0),
        'c': nrm(ks[1], (BATCH, D_MODEL), 1.0),
        'ctx': nrm(ks[2], (BATCH, CTX_LEN, D_MODEL), 1.0),
        'c_ctx': nrm(ks[3], (D_MODEL,), 1.0),
        'w_mod': nrm(ks[4], (DEPTH, D_MODEL, 3 * D_MODEL), 0.5 * D_MODEL ** -0.5),
        'b_mod': nrm(ks[5], (DEPTH, 3 * D_MODEL), 0.01),
        'norm_g': 1.0 + nrm(ks[6], (DEPTH, D_MODEL), 0.05),
        'ev_w_in': nrm(ks[7], (N_EVEN, D_MODEL, EVEN_IN), D_MODEL ** -0.5),
        'ev_w_out': nrm(ks[8], (N_EVEN, EVEN_MIX, D_MODEL), EVEN_MIX ** -0.5),
        'pool_w': nrm(ks[9], (N_EVEN, POOL_GROUPS, POOL_GROUP_DIM, POOL_GROUP_DIM), POOL_GROUP_DIM ** -0.5),
        'pool_scale': 1.0 + nrm(ks[10], (N_EVEN, POOL_WIDTH), 0.1),
        'q_norm_g': 1.0 + nrm(ks[11], (N_EVEN, HEAD_DIM), 0.05),
        'k_norm_g': 1.0 + nrm(ks[12], (N_EVEN, HEAD_DIM), 0.05),
        'od_w_in': nrm(ks[13], (N_ODD, D_MODEL, ODD_IN), D_MODEL ** -0.5),
        'od_w_out': nrm(ks[14], (N_ODD, ODD_MIX, D_MODEL), ODD_MIX ** -0.5),
        'hy_conv_w': nrm(ks[15], (N_ODD, 3, (HY_ORDER + 1) * HY_WIDTH), 3 ** -0.5),
        'hy_conv_b': nrm(ks[16], (N_ODD, (HY_ORDER + 1) * HY_WIDTH), 0.01),
        'hy_w1': nrm(ks[17], (N_ODD, HY_EMB, HY_HIDDEN), HY_EMB ** -0.5),
        'hy_b1': nrm(ks[18], (N_ODD, HY_HIDDEN), 0.1),
        'hy_w2': nrm(ks[19], (N_ODD, HY_HIDDEN, HY_HIDDEN), HY_HIDDEN ** -0.5),
        'hy_b2': nrm(ks[20], (N_ODD, HY_HIDDEN), 0.1),
        'hy_w3': nrm(ks[21], (N_ODD, HY_HIDDEN, HY_ORDER * 2 * HY_WIDTH), HY_HIDDEN ** -0.5),
        'hy_freq': 1.0 + nrm(ks[22], (N_ODD, HY_HIDDEN), 0.1),
        'hy_skip': nrm(ks[23], (N_ODD, HY_ORDER, HY_WIDTH), 1.0),
        'fn_w': nrm(ks[24], (N_ODD, FN_WIDTH, FN_WIDTH), FN_WIDTH ** -0.5),
        'final_g': 1.0 + nrm(ks[25], (D_MODEL,), 0.05),
    }

def first_block(x, c, ctx, c_ctx, w_mod, b_mod, norm_g, ev_w_in, ev_w_out, pool_w, pool_scale,
              q_norm_g, k_norm_g, od_w_in, od_w_out, hy_conv_w, hy_conv_b, hy_w1, hy_b1, hy_w2, hy_b2,
              hy_w3, hy_freq, hy_skip, fn_w, final_g):
    n_tok = x.shape[1]
    rows = n_tok // GRID_W
    row_idx = jnp.broadcast_to(jnp.arange(rows, dtype=jnp.float32)[:, None], (rows, GRID_W)).reshape(-1)
    col_idx = jnp.broadcast_to(jnp.arange(GRID_W, dtype=jnp.float32)[None, :], (rows, GRID_W)).reshape(-1)
    cos, sin = axial_rope_tables(row_idx, col_idx)

    for i in range(DEPTH):
        li = i // 2
        is_even = i % 2 == 0
        ctx_needed = any(j % 2 == 0 for j in range(i + 1, DEPTH))
        shift, scale, gate = modulation(c[:, None, :], w_mod[i], b_mod[i])
        h = rmsnorm(x, norm_g[i]) * (1 + scale) + shift
        if is_even or ctx_needed:
            cshift, cscale, cgate = modulation(c_ctx[None, None, :], w_mod[i], b_mod[i])
            hc = rmsnorm(ctx, norm_g[i]) * (1 + cscale) + cshift
        if is_even:
            w_in = ev_w_in[li]
            a_val, a_gate, q, k, v, b_gate = jnp.split(h @ w_in, EVEN_SPLITS, axis=-1)
            q = apply_rope(rmsnorm(to_heads(q, N_Q_HEADS), q_norm_g[li]), cos, sin)
            k = apply_rope(rmsnorm(to_heads(k, N_KV_HEADS), k_norm_g[li]), cos, sin)
            if ctx_needed:
                ca_val, ca_gate, cq, ck, cv, cb_gate = jnp.split(hc @ w_in, EVEN_SPLITS, axis=-1)
            else:
                ck, cv = jnp.split(hc @ w_in[:, EVEN_SPLITS[2]:EVEN_SPLITS[4]], 2, axis=-1)
            ck = rmsnorm(to_heads(ck, N_KV_HEADS), k_norm_g[li])
            cv = to_heads(cv, N_KV_HEADS)
            k_all = jnp.concatenate([ck, k], axis=1)
            v_all = jnp.concatenate([cv, to_heads(v, N_KV_HEADS)], axis=1)
            y = even_mix(a_val, a_gate, q, b_gate, k_all, v_all, pool_w[li], pool_scale[li], ev_w_out[li])
            if ctx_needed:
                cq = rmsnorm(to_heads(cq, N_Q_HEADS), q_norm_g[li])
                yc = even_mix(ca_val, ca_gate, cq, cb_gate, ck, cv, pool_w[li], pool_scale[li], ev_w_out[li])
                ctx = ctx + cgate * yc
            x = x + gate * y
        else:
            y = odd_mix(h, od_w_in[li], od_w_out[li], fn_w[li], hy_conv_w[li], hy_conv_b[li],
                        hy_w1[li], hy_b1[li], hy_w2[li], hy_b2[li], hy_w3[li], hy_freq[li], hy_skip[li])
            if ctx_needed:
                yc = odd_mix(hc, od_w_in[li], od_w_out[li], fn_w[li], hy_conv_w[li], hy_conv_b[li],
                             hy_w1[li], hy_b1[li], hy_w2[li], hy_b2[li], hy_w3[li], hy_freq[li], hy_skip[li])
                ctx = ctx + cgate * yc
            x = x + gate * y
    return rmsnorm(x, final_g)


N_MIXERS = 2
SSM_GROUP = 16
SSM_GROUPS = D_MODEL // SSM_GROUP
SSM_STATE = 64
DT_MIN = 1e-3
DT_MAX = 1e-1
SSM_C_STD = 0.5
SB_HEADS = 16
SB_HEAD_DIM = D_MODEL // SB_HEADS
FFN_HIDDEN = -(-8 * D_MODEL // (3 * 256)) * 256
DEEPNORM_ALPHA = (2 * DEPTH) ** 0.25
DEEPNORM_BETA = (8 * DEPTH) ** -0.25
LN_EPS = 1e-5
N_SSM_LAYERS = (DEPTH + 1) // 2
N_SB_LAYERS = DEPTH // 2


def layer_norm(x, g, b):
    xf = x.astype(jnp.float32)
    mu = jnp.mean(xf, axis=-1, keepdims=True)
    var = jnp.mean(jnp.square(xf - mu), axis=-1, keepdims=True)
    y = (xf - mu) * lax.rsqrt(var + LN_EPS) * g.astype(jnp.float32) + b.astype(jnp.float32)
    return y.astype(x.dtype)

def _cmul(ar, ai, br, bi):
    return ar * br - ai * bi, ar * bi + ai * br

def _ssm_combine(left, right):
    alr, ali, blr, bli = left
    arr, ari, brr, bri = right
    ar, ai = _cmul(arr, ari, alr, ali)
    br, bi = _cmul(arr, ari, blr, bli)
    return ar, ai, br + brr, bi + bri

def s5_mixer(x, a_re, a_im, log_dt, b_re, b_im, c_re, c_im, d_skip, w_glu, w_out):
    bsz, seq, _ = x.shape
    f32 = jnp.float32
    u = x.astype(f32).reshape(bsz, seq, SSM_GROUPS, SSM_GROUP)
    dt = jnp.exp(log_dt.astype(f32))[:, None]
    lam_re = jnp.minimum(a_re.astype(f32), -1e-4)
    lam_im = a_im.astype(f32)
    mag = jnp.exp(lam_re * dt)
    lbar_re = mag * jnp.cos(lam_im * dt)
    lbar_im = mag * jnp.sin(lam_im * dt)
    den = lam_re * lam_re + lam_im * lam_im
    num_re = lbar_re - 1.0
    num_im = lbar_im
    coef_re = (num_re * lam_re + num_im * lam_im) / den
    coef_im = (num_im * lam_re - num_re * lam_im) / den
    bb_re, bb_im = _cmul(coef_re[..., None], coef_im[..., None],
                         b_re.astype(f32), b_im.astype(f32))
    bu_re = jnp.einsum('blgh,gph->lbgp', u, bb_re)
    bu_im = jnp.einsum('blgh,gph->lbgp', u, bb_im)
    a_seq_re = jnp.broadcast_to(lbar_re, (seq, 1, SSM_GROUPS, SSM_STATE))
    a_seq_im = jnp.broadcast_to(lbar_im, (seq, 1, SSM_GROUPS, SSM_STATE))
    _, _, s_re, s_im = lax.associative_scan(
        _ssm_combine, (a_seq_re, a_seq_im, bu_re, bu_im), axis=0)
    y = (jnp.einsum('lbgp,ghp->blgh', s_re, c_re.astype(f32))
         - jnp.einsum('lbgp,ghp->blgh', s_im, c_im.astype(f32)))
    y = y.reshape(bsz, seq, D_MODEL) + d_skip.astype(f32) * x.astype(f32)
    h = jax.nn.gelu(y).astype(x.dtype)
    val, gate = jnp.split(h @ w_glu, 2, axis=-1)
    z = val * jax.nn.sigmoid(gate)
    return (z @ w_out).astype(x.dtype)

def stick_breaking_mixer(x, w_qkv, w_o):
    bsz, seq, _ = x.shape
    f32 = jnp.float32
    q, k, v = jnp.split(x @ w_qkv, 3, axis=-1)
    to_heads = lambda t: t.reshape(bsz, seq, SB_HEADS, SB_HEAD_DIM).transpose(0, 2, 1, 3)
    q, k, v = to_heads(q), to_heads(k), to_heads(v)
    scale = SB_HEAD_DIM ** -0.5
    outs = []
    for blk in range(seq // Q_BLOCK):
        q0 = blk * Q_BLOCK
        kv_len = q0 + Q_BLOCK
        qb = q[:, :, q0:kv_len].astype(f32)
        kb = k[:, :, :kv_len].astype(f32)
        vb = v[:, :, :kv_len]
        z = jnp.einsum('bhqd,bhkd->bhqk', qb, kb) * scale
        t_idx = q0 + jnp.arange(Q_BLOCK)[:, None]
        s_idx = jnp.arange(kv_len)[None, :]
        past = s_idx < t_idx
        log_beta = jax.nn.log_sigmoid(z)
        log_1m_beta = jnp.where(past, jax.nn.log_sigmoid(-z), 0.0)
        between = lax.cumsum(log_1m_beta, axis=3, reverse=True) - log_1m_beta
        weights = jnp.where(past, jnp.exp(log_beta + between), 0.0)
        outs.append(jnp.einsum('bhqk,bhkd->bhqd', weights.astype(vb.dtype), vb))
    o = jnp.concatenate(outs, axis=2)
    o = o.transpose(0, 2, 1, 3).reshape(bsz, seq, D_MODEL)
    return (o @ w_o).astype(x.dtype)

def swiglu_ffn(x, w_gu, w_down):
    g, u = jnp.split(x @ w_gu, 2, axis=-1)
    return (jax.nn.silu(g) * u) @ w_down

def second_inputs(seed: int = 0) -> dict:
    key = jax.random.key(seed)
    ks = jax.random.split(key, 24)
    f32 = jnp.float32
    nrm = lambda k, shape, std: jax.random.normal(k, shape, f32) * std
    G, P, H, D, F = SSM_GROUPS, SSM_STATE, SSM_GROUP, D_MODEL, FFN_HIDDEN
    x = jax.random.normal(ks[0], (BATCH, SEQ, D), f32)
    ssm_a_re = -0.5 + nrm(ks[1], (N_SSM_LAYERS, G, P), 0.01)
    ssm_a_im = (math.pi * jnp.arange(P, dtype=f32))[None, None, :] + nrm(ks[2], (N_SSM_LAYERS, G, P), 0.01)
    ssm_log_dt = jax.random.uniform(ks[3], (N_SSM_LAYERS, G), f32,
                                    minval=math.log(DT_MIN), maxval=math.log(DT_MAX))
    ssm_b_re = nrm(ks[4], (N_SSM_LAYERS, G, P, H), (2 * H) ** -0.5)
    ssm_b_im = nrm(ks[5], (N_SSM_LAYERS, G, P, H), (2 * H) ** -0.5)
    ssm_c_re = nrm(ks[6], (N_SSM_LAYERS, G, H, P), SSM_C_STD)
    ssm_c_im = nrm(ks[7], (N_SSM_LAYERS, G, H, P), SSM_C_STD)
    ssm_d = nrm(ks[8], (N_SSM_LAYERS, D), 1.0)
    ssm_w_glu = nrm(ks[9], (N_SSM_LAYERS, D, 2 * D), D ** -0.5)
    ssm_w_out = nrm(ks[10], (N_SSM_LAYERS, D, D), D ** -0.5 * DEEPNORM_BETA)
    sb_w_qkv = nrm(ks[11], (N_SB_LAYERS, D, 3 * D), D ** -0.5)
    sb_w_o = nrm(ks[12], (N_SB_LAYERS, D, D), D ** -0.5 * DEEPNORM_BETA)
    ffn_w_gu = nrm(ks[13], (DEPTH, D, 2 * F), D ** -0.5)
    ffn_w_down = nrm(ks[14], (DEPTH, F, D), F ** -0.5 * DEEPNORM_BETA)
    ln_mix_g = 1.0 + nrm(ks[15], (DEPTH, D), 0.02)
    ln_mix_b = nrm(ks[16], (DEPTH, D), 0.02)
    ln_ffn_g = 1.0 + nrm(ks[17], (DEPTH, D), 0.02)
    ln_ffn_b = nrm(ks[18], (DEPTH, D), 0.02)
    return {"x": x,
            "ssm_a_re": ssm_a_re, "ssm_a_im": ssm_a_im, "ssm_log_dt": ssm_log_dt,
            "ssm_b_re": ssm_b_re, "ssm_b_im": ssm_b_im,
            "ssm_c_re": ssm_c_re, "ssm_c_im": ssm_c_im, "ssm_d": ssm_d,
            "ssm_w_glu": ssm_w_glu, "ssm_w_out": ssm_w_out,
            "sb_w_qkv": sb_w_qkv, "sb_w_o": sb_w_o,
            "ffn_w_gu": ffn_w_gu, "ffn_w_down": ffn_w_down,
            "ln_mix_g": ln_mix_g, "ln_mix_b": ln_mix_b,
            "ln_ffn_g": ln_ffn_g, "ln_ffn_b": ln_ffn_b}

def second_block(x, ssm_a_re, ssm_a_im, ssm_log_dt, ssm_b_re, ssm_b_im, ssm_c_re, ssm_c_im,
              ssm_d, ssm_w_glu, ssm_w_out, sb_w_qkv, sb_w_o, ffn_w_gu, ffn_w_down,
              ln_mix_g, ln_mix_b, ln_ffn_g, ln_ffn_b):
    h = x
    for i in range(DEPTH):
        j = i // N_MIXERS
        if i % N_MIXERS == 0:
            mix = s5_mixer(h, ssm_a_re[j], ssm_a_im[j], ssm_log_dt[j], ssm_b_re[j], ssm_b_im[j],
                           ssm_c_re[j], ssm_c_im[j], ssm_d[j], ssm_w_glu[j], ssm_w_out[j])
        else:
            mix = stick_breaking_mixer(h, sb_w_qkv[j], sb_w_o[j])
        h = layer_norm(DEEPNORM_ALPHA * h + mix, ln_mix_g[i], ln_mix_b[i])
        h = layer_norm(DEEPNORM_ALPHA * h + swiglu_ffn(h, ffn_w_gu[i], ffn_w_down[i]),
                       ln_ffn_g[i], ln_ffn_b[i])
    return h


def setup_inputs(seed=0):
    out = dict(first_inputs(seed))
    for name, value in second_inputs(seed + 1).items():
        if name != "x":
            out[name + "_2"] = value
    return out


def reference(
    x, c, ctx, c_ctx, w_mod, b_mod, norm_g, ev_w_in, ev_w_out, pool_w, pool_scale, q_norm_g,
    k_norm_g, od_w_in, od_w_out, hy_conv_w, hy_conv_b, hy_w1, hy_b1, hy_w2, hy_b2, hy_w3,
    hy_freq, hy_skip, fn_w, final_g, ssm_a_re_2, ssm_a_im_2, ssm_log_dt_2, ssm_b_re_2,
    ssm_b_im_2, ssm_c_re_2, ssm_c_im_2, ssm_d_2, ssm_w_glu_2, ssm_w_out_2, sb_w_qkv_2, sb_w_o_2,
    ffn_w_gu_2, ffn_w_down_2, ln_mix_g_2, ln_mix_b_2, ln_ffn_g_2, ln_ffn_b_2,
):
    x = first_block(
        x, c, ctx, c_ctx, w_mod, b_mod, norm_g, ev_w_in, ev_w_out, pool_w, pool_scale, q_norm_g,
        k_norm_g, od_w_in, od_w_out, hy_conv_w, hy_conv_b, hy_w1, hy_b1, hy_w2, hy_b2, hy_w3,
        hy_freq, hy_skip, fn_w, final_g,
    )
    return second_block(
        x, ssm_a_re_2, ssm_a_im_2, ssm_log_dt_2, ssm_b_re_2, ssm_b_im_2, ssm_c_re_2, ssm_c_im_2,
        ssm_d_2, ssm_w_glu_2, ssm_w_out_2, sb_w_qkv_2, sb_w_o_2, ffn_w_gu_2, ffn_w_down_2,
        ln_mix_g_2, ln_mix_b_2, ln_ffn_g_2, ln_ffn_b_2,
    )


_drawn_inputs = setup_inputs


def setup_inputs(seed=0):
    import zlib

    import numpy as np

    out = dict(_drawn_inputs(seed))
    spreads = {}
    factors = {'ctx': 8.0,
     'c_ctx': 5.512,
     'b_mod': 5.807,
     'norm_g': 2.7,
     'pool_scale': 5.599,
     'q_norm_g': 8.0,
     'k_norm_g': 8.0,
     'hy_conv_b': 8.0,
     'hy_b1': 7.104,
     'hy_b2': 5.239,
     'hy_freq': 8.0,
     'ssm_a_re_2': 200.0,
     'ssm_a_im_2': 28.344,
     'ssm_log_dt_2': 30.288,
     'ssm_b_re_2': 39.384,
     'ssm_b_im_2': 39.648,
     'ssm_c_re_2': 39.376,
     'ssm_c_im_2': 39.736}
    for name, (base, spread) in spreads.items():
        noise = np.random.default_rng([zlib.crc32(name.encode()), seed]).standard_normal(out[name].shape)
        drawn = base * np.exp(spread * noise) if base else spread * noise
        out[name] = jnp.asarray(drawn.astype(out[name].dtype))
    for name, factor in factors.items():
        out[name] = (out[name] * factor).astype(out[name].dtype)
    return out
```

```python
from contextlib import ExitStack

import numpy as np

import concourse.bass as bass
from concourse import mybir

F32 = mybir.dt.float32
F32R = mybir.dt.float32r
ALU = mybir.AluOpType
ACT = mybir.ActivationFunctionType
AX_X = mybir.AxisListType.X

P = 128
D = 1024
T = 1024
H = 512
KB = D // P
CTX = 256
N_HEADS, N_KV, HD = 6, 2, 128
POOLW = 256
KEYS = CTX + T
HYW = 768
FFN = 2816
FB = FFN // P
RING = 4
TILE = KB * P
RMS_EPS, LN_EPS = 1e-6, 1e-5
ALPHA = (2 * 2) ** 0.25
SCALE0 = HD ** -0.5
TWO_PI = 2 * np.pi


class Linear:

    def __init__(self, name, t0, tiles, n0, dram):
        self.name, self.t0, self.tiles, self.n0, self.dram = name, t0, tiles, n0, dram


def plan():
    stages, t, n, dram = {}, 0, 0, 0
    for name, tiles, outs in (
        ("mod", 48, 0),
        ("ev_in", 24, 24),
        ("ev_out", 8, 8),
        ("fn_in", 4, 4),
        ("od_in", 24, 24),
        ("od_out", 8, 8),
        ("glu", 16, 16),
        ("s5_out", 8, 8),
        ("gu0a", 44, 44),
        ("down0a", 24, 8),
        ("gu0b", 44, 44),
        ("down0b", 24, 8),
        ("qkv", 24, 0),
        ("sb_out", 8, 8),
        ("gu1a", 44, 44),
        ("down1a", 24, 8),
        ("gu1b", 44, 44),
        ("down1b", 24, 8),
    ):
        if name.endswith("b"):
            stages[name] = Linear(name, t, tiles, n, stages[name[:-1] + "a"].dram)
        else:
            stages[name] = Linear(name, t, tiles, n, dram)
            dram += tiles
        t += tiles
        n += outs
    return stages


PLAN = plan()

VECS = {}
for _name, _n in (("cond", 16), ("b_mod", 48), ("norm_g", 16), ("pool_scale", 2), ("q_g", 1), ("k_g", 1),
                  ("conv_w", 54), ("conv_b", 18), ("hy_b1", 1), ("hy_b2", 1), ("hy_freq", 1), ("final_g", 8),
                  ("ssm_d", 8), ("ln_mix_g", 16), ("ln_mix_b", 16), ("ln_ffn_g", 16), ("ln_ffn_b", 16)):
    VECS[_name] = (sum(n for _, n in VECS.values()), _n)
N_VECS = sum(n for _, n in VECS.values())


class Stage:
    pe = act = dve = pool = also = None


def span(base, it, step):
    return it * step + base if step else base


def build(nc, ins, out, stop=None):
    ctx = ExitStack()
    with ctx:
        _build(nc, ctx, ins, out, stop)


def _build(nc, ctx, ins, out, stop):
    def sb(name, words):
        return ctx.enter_context(nc.sbuf_tensor(name, [P, words], F32))

    def sem(name):
        return ctx.enter_context(nc.semaphore(name))

    XT_ = sb("resid", KB * T)
    WR = sb("w_ring", RING * TILE)
    with ExitStack() as first_use:
        HT_ = first_use.enter_context(nc.sbuf_tensor("hidden", [P, KB * T], F32))
        AR = first_use.enter_context(nc.sbuf_tensor("arena", [P, 29184], F32))
    WPART = ctx.enter_context(nc.sbuf_tensor("w_parts", [P, 2, 2, TILE], F32R))
    XPART = ctx.enter_context(nc.sbuf_tensor("x_parts", [P, 2, KB, H], F32R))
    HPART = ctx.enter_context(nc.sbuf_tensor("hidden_parts", [P, 2, FB, H], F32R))
    FTMP = sb("ffn_temps", KB * T + 29184 - 4 * TILE - 2 * KB * H - 2 * FB * H)
    RINV = sb("rinv", T)
    SQ = sb("squares", 2 * H)
    IDENT = sb("ident", P)
    ONES = sb("ones", P)
    VEC = sb("vectors", N_VECS)
    MOD = sb("mods", 96)
    PS = ctx.enter_context(nc.psum_tensor("banks", [P, 8, H], F32))

    def ar(at, words, pattern=None, **kw):
        v = AR[:, at:at + words]
        return v.rearrange(pattern, **kw) if pattern else v

    def three(t, blocks, width):
        return t[:, 0:blocks * width].rearrange("p (k t) -> p k t", k=blocks)

    XT, HT = three(XT_, KB, T), three(HT_, KB, T)
    W = WR[:, :].rearrange("p (s k n) -> p s k n", s=RING, k=KB)

    def vec(name, i=0, n=1):
        c = VECS[name][0] + i
        return VEC[:, c:c + n]

    def bank2(pair):
        return PS[:, 2 * pair:2 * pair + 2, :].rearrange("p b t -> p (b t)")

    w_full = [sem(f"w_full{s}") for s in range(RING)]
    w_done = [sem(f"w_done{s}") for s in range(RING)]
    evicted = [sem(f"evicted{p}") for p in range(2)]
    link_s = {k: sem(f"link_{k}") for k in ("act", "dve", "pool")}

    class Link:

        def __init__(self, eng, key):
            self.eng, self.sem, self.n, self.it, self.per = eng, link_s[key], 0, None, 0

        def __call__(self, ins):
            ins.then_inc(self.sem, 1)
            self.n += 1
            self.eng.wait_ge(self.sem, self.n if self.it is None else span(self.n, self.it, self.per))

        def enter(self, it, per):
            self.it, self.per, self.at = it, per, self.n

        def leave(self, trips):
            assert self.n - self.at == self.per, (self.n - self.at, self.per)
            self.n = self.at + trips * self.per
            self.it = None

    def slot(st, j):
        return (st.t0 + j) % RING

    def loads(st, j):
        return (st.t0 + j) // RING + 1

    def wait_tile(eng, st, j, it=None, tiles=0):
        eng.wait_ge(w_full[slot(st, j)], span(16 * loads(st, j), it, 16 * tiles // RING) if it is not None
                    else 16 * loads(st, j))

    def wait_sums(eng, st, j, it=None, tiles=0):
        eng.wait_ge(w_done[slot(st, j)], span(loads(st, j), it, tiles // RING) if it is not None
                    else loads(st, j))

    def wait_pair(eng, st, n, it=None, outs=0):
        used = (st.n0 + n) // 2
        if it is not None:
            eng.wait_ge(evicted[(st.n0 + n) % 2], span(used, it, outs // 2))
        elif used:
            eng.wait_ge(evicted[(st.n0 + n) % 2], used)

    def pair(st, n):
        return (st.n0 + n) % 2

    def wait_done(eng, done):
        for s, v in done:
            eng.wait_ge(s, v)

    def pairs_done(st, outs):
        return [(evicted[p], (st.n0 + outs + 1 - p) // 2) for p in range(2)]

    def matmul_tile(pe, st, j, n, src, it=None, tiles=0, outs=0, width=T):
        wait_tile(pe, st, j, it, tiles)
        wait_pair(pe, st, n, it, outs)
        s, b = slot(st, j), 2 * pair(st, n)
        for k in range(KB):
            for h in range(0, width, H):
                w = min(H, width - h)
                mm = nc.tensor.matmul(PS[:, b + h // H, 0:w], W[:, s, k, :], src[:, k, h:h + w],
                                      start=(k == 0), stop=(k == KB - 1))
        mm.then_inc(w_done[s], 1)

    S = []


    n_sem = {key: sem("n_" + key) for key in ("sq_ready", "sq_free", "stat", "mean_in", "centred", "root",
                                              "scaled", "shifted")}
    n_count = dict.fromkeys(n_sem, 0)

    def norm_stage(name, kind, src, dst, tokens, eps, gain, shift, after, scratch=0):
        base = dict(n_count)
        segs = [(i, min(H, tokens - i)) for i in range(0, tokens, H)]
        layer = kind == "layer"
        uses = {"sq_ready": KB, "sq_free": KB, "stat": layer, "mean_in": layer, "centred": KB * layer,
                "root": 1, "scaled": KB, "shifted": KB * (shift is not None)}
        for key, per_seg in uses.items():
            n_count[key] += len(segs) * per_seg

        def wait(eng, key, n):
            eng.wait_ge(n_sem[key], base[key] + n)

        class St(Stage):
            pass

        St.done = [(n_sem[key], n_count[key]) for key in ("shifted", "root", "scaled") if uses[key]]

        def pe(pe_):
            wait_done(pe_, after)
            if layer:
                for i, (a, w) in enumerate(segs):
                    for k in range(KB):
                        mm = nc.tensor.matmul(PS[:, 4 + i, 0:w], ONES[:, :], src[:, k, a:a + w],
                                              start=(k == 0), stop=(k == KB - 1))
                    mm.then_inc(n_sem["mean_in"], 1)
            for i, (a, w) in enumerate(segs):
                for k in range(KB):
                    j = i * KB + k
                    wait(pe_, "sq_ready", j + 1)
                    mm = nc.tensor.matmul(PS[:, 6 + i, 0:w], ONES[:, :], SQ[:, (j % 2) * H:(j % 2) * H + w],
                                          start=(k == 0), stop=(k == KB - 1))
                    mm.then_inc(n_sem["sq_free"], 1)

        def act(a_, link):
            wait_done(a_, after)
            if layer:
                for i, (a, w) in enumerate(segs):
                    wait(a_, "mean_in", i + 1)
                    nc.scalar.activation(AR[:, scratch + a:scratch + a + w], PS[:, 4 + i, 0:w], ACT.Identity,
                                         scale=1.0 / D).then_inc(n_sem["stat"], 1)
            for i, (a, w) in enumerate(segs):
                for k in range(KB):
                    j = i * KB + k
                    if layer:
                        wait(a_, "centred", j + 1)
                    if j >= 2:
                        wait(a_, "sq_free", j - 1)
                    nc.scalar.activation(SQ[:, (j % 2) * H:(j % 2) * H + w], src[:, k, a:a + w],
                                         ACT.Square).then_inc(n_sem["sq_ready"], 1)
            for i, (a, w) in enumerate(segs):
                wait(a_, "sq_free", (i + 1) * KB)
                nc.scalar.activation(RINV[:, a:a + w], PS[:, 6 + i, 0:w], ACT.Sqrt, scale=1.0 / D,
                                     bias=EPS(eps)).then_inc(n_sem["root"], 1)

        def dve(v_, link):
            wait_done(v_, after)
            if layer:
                for i, (a, w) in enumerate(segs):
                    wait(v_, "stat", i + 1)
                    for k in range(KB):
                        nc.vector.tensor_tensor(src[:, k, a:a + w], src[:, k, a:a + w],
                                                AR[:, scratch + a:scratch + a + w],
                                                ALU.subtract).then_inc(n_sem["centred"], 1)
            for i, (a, w) in enumerate(segs):
                wait(v_, "root", i + 1)
                link(nc.vector.reciprocal(RINV[:, a:a + w], RINV[:, a:a + w]))
                for k in range(KB):
                    nc.vector.scalar_tensor_tensor(dst[:, k, a:a + w], src[:, k, a:a + w], gain(k),
                                                   RINV[:, a:a + w], ALU.mult, ALU.mult).then_inc(n_sem["scaled"], 1)

        def pool(g_, link):
            wait_done(g_, after)
            for i, (a, w) in enumerate(segs):
                for k in range(KB):
                    wait(g_, "scaled", i * KB + k + 1)
                    nc.gpsimd.tensor_scalar(dst[:, k, a:a + w], dst[:, k, a:a + w], shift(k), None,
                                            ALU.add).then_inc(n_sem["shifted"], 1)

        St.pe, St.act, St.dve = pe, act, dve
        if shift is not None:
            St.pool = pool
        St.name = name
        S.append(St)
        return St.done

    EPSV = sb("eps", 2)

    def EPS(e):
        return EPSV[:, 0:1] if e == RMS_EPS else EPSV[:, 1:2]

    vec_in, x_in, ctx_in, tab_in = sem("vec_in"), sem("x_in"), sem("ctx_in"), sem("tab_in")
    consts = sem("consts")
    cond_ready, mod_ready, mod_done = sem("cond_ready"), sem("mod_ready"), sem("mod_done")
    A_AV, A_AG, A_Q, A_K, A_BG, A_V = 0, 2080, 4128, 10272, 12832, 18976
    A_S0 = 21536
    CT = ar(A_Q, KB * CTX, "p (k t) -> p k t", k=KB)
    COS, SIN = ar(A_S0, T), ar(A_S0 + T, T)
    QN, RT = A_S0 + 2 * T, A_S0 + 2 * T + 2 * H
    CTN = ar(A_S0 + 2 * T + 4 * H, KB * CTX, "p (k t) -> p k t", k=KB)
    INVCNT = ar(A_BG, 2 * T, "p (b t) -> p b t", b=2)
    PA, PB = A_BG + 2 * T, A_BG + 2 * T + 1040
    AV = ar(A_AV, 2080, "p (b t) -> p b t", b=2)
    AG = ar(A_AG, 2 * T, "p (b t) -> p b t", b=2)

    class Setup(Stage):
        name = "mod"
        st = PLAN["mod"]
        done = [(mod_done, 3)]

        def sp(s):
            s.dma_start(VEC[:, :], ins["vecs"]).then_inc(vec_in, 16)
            s.dma_start(CT, ins["ctxT"].rearrange("(k p) t -> p k t", p=P)).then_inc(ctx_in, 16)
            s.dma_start(XT, ins["xT"].rearrange("(k p) t -> p k t", p=P)).then_inc(x_in, 16)
            s.dma_start(COS, ins["rope"][0]).then_inc(tab_in, 16)
            s.dma_start(SIN, ins["rope"][1]).then_inc(tab_in, 16)
            s.dma_start(INVCNT, ins["invcnt"].rearrange("b p t -> p b t")).then_inc(tab_in, 16)
            s.dma_start(IDENT[:, :], ins["ident"]).then_inc(tab_in, 16)

        def act(a, link):
            a.wait_ge(vec_in, 16)
            nc.scalar.activation(vec("cond", 0, 16), vec("cond", 0, 16), ACT.Silu).then_inc(cond_ready, 1)

        def pe(p):
            st = PLAN["mod"]
            p.wait_ge(cond_ready, 1)
            with p.Fori(0, 12) as it:
                for j in range(4):
                    wait_tile(p, st, j, it, 4)
                    s = slot(st, j)
                    for k in range(KB):
                        mm = nc.tensor.matmul(PS[:, 4, bass.ds(it * 8 + 2 * j, 2)], W[:, s, k, :],
                                              vec("cond", 2 * k, 2), start=(k == 0), stop=(k == KB - 1))
                    mm.then_inc(w_done[s], 1)

        def dve(v, link):
            nc.vector.memset(ONES[:, :], 1.0).then_inc(consts, 1)
            nc.vector.memset(EPSV[:, 0:1], RMS_EPS).then_inc(consts, 1)
            nc.vector.memset(EPSV[:, 1:2], LN_EPS).then_inc(consts, 1)
            for s in range(RING):
                v.wait_ge(w_done[s], 12)
            m = MOD[:, :].rearrange("p (n c) -> p n c", c=2)
            link(nc.vector.tensor_tensor(m, PS[:, 4, 0:96].rearrange("p (n c) -> p n c", c=2),
                                         vec("b_mod", 0, 48).unsqueeze(2).broadcast_to([P, 48, 2]), ALU.add))
            for layer in range(2):
                sc = m[:, 24 * layer + 8:24 * layer + 16, :]
                ins_ = nc.vector.scalar_tensor_tensor(
                    sc, sc, 1.0, vec("norm_g", 8 * layer, 8).unsqueeze(2).broadcast_to([P, 8, 2]),
                    ALU.add, ALU.mult)
                ins_.then_inc(mod_done, 1)
            v.wait_ge(tab_in, 64)
            v.wait_ge(x_in, 16)
            v.wait_ge(ctx_in, 16)
            nc.vector.memset(AR[:, A_AV:A_AV + 2080], 0.0).then_inc(mod_done, 1)

    S.append(Setup)

    def mod(layer, what, k, c=0):
        i = 2 * (24 * layer + 8 * what + k) + c
        return MOD[:, i:i + 1]

    done = norm_stage("n_ctx", "rms", CT, CTN, CTX, RMS_EPS, lambda k: mod(0, 1, k, 1), lambda k: mod(0, 0, k, 1),
                      Setup.done)
    h0_done = norm_stage("n_x0", "rms", XT, HT, T, RMS_EPS, lambda k: mod(0, 1, k), lambda k: mod(0, 0, k), done)

    ROT = sb("rope_swap", P)
    Q0, BG = ar(A_Q, 6 * T), ar(A_BG, 6 * T)
    K0 = ar(A_K, N_KV * KEYS, "p (h t) -> p h t", h=N_KV)
    V0 = ar(A_V, (KEYS // P) * N_KV * HD, "p (b n) -> p b n", b=KEYS // P)
    POOLW_T = ar(A_S0 + 6144, 2 * P, "p (b n) -> p b n", b=2)
    rot_in, pw_in = sem("rot_in"), sem("pw_in")
    e_sq, e_ss, e_root, e_qn = sem("e_sq"), sem("e_ss"), sem("e_root"), sem("e_qn")
    e_rot, e_rt, e_cos, e_head = sem("e_rot"), sem("e_rt"), sem("e_cos"), sem("e_head")
    pool_mix = sem("pool_mix")

    EV = ([("val", 0), ("val", 1), ("gate", 0), ("gate", 1), ("k", 0), ("k", 1), ("kctx", 0), ("kctx", 1),
           ("v", 0), ("v", 1), ("vctx", 0), ("vctx", 1)] + [("q", i) for i in range(6)]
          + [("bgate", i) for i in range(6)])
    SEGS = []
    for _j, (_kind, _i) in enumerate(EV):
        if _kind in ("k", "q"):
            SEGS += [(_j, 0, H, True), (_j, 1, H, True)]
        if _kind == "kctx":
            SEGS += [(_j, 0, CTX, False)]
    N_ROT = sum(s[3] for s in SEGS)

    def segs_of(j):
        out_ = []
        for g, (jj, h, w, r) in enumerate(SEGS):
            if jj == j:
                out_.append((g, sum(s[3] for s in SEGS[:g]), h, w, r))
        return out_

    def head_dst(kind, i, h, w):
        if kind == "q":
            return Q0[:, i * T + h * H:i * T + h * H + w]
        if kind == "k":
            return K0[:, i, CTX + h * H:CTX + h * H + w]
        return K0[:, i, 0:CTX]

    class EvIn(Stage):
        name = "ev_in"
        st = PLAN["ev_in"]
        after = h0_done
        done = pairs_done(PLAN["ev_in"], 24) + [(e_head, N_ROT), (pool_mix, 2), (e_qn, len(SEGS))]

        def sp(s):
            s.dma_start(ROT[:, :], ins["rope_swap"]).then_inc(rot_in, 16)
            s.dma_start(POOLW_T, ins["pool_w"].rearrange("b p n -> p b n")).then_inc(pw_in, 16)

        def pe(p):
            st = EvIn.st
            wait_done(p, EvIn.after)
            p.wait_ge(rot_in, 16)
            for j in range(len(EV) + 2):
                if j < len(EV):
                    kind, i = EV[j]
                    src = CTN if kind in ("kctx", "vctx") else HT
                    width = CTX if kind in ("kctx", "vctx") else T
                    if kind in ("v", "vctx"):
                        wait_tile(p, st, j)
                        wait_pair(p, st, j)
                        s, b = slot(st, j), 2 * pair(st, j)
                        for tb in range(width // P):
                            for k in range(KB):
                                mm = nc.tensor.matmul(PS[:, b + tb // 4, (tb % 4) * P:(tb % 4 + 1) * P],
                                                      src[:, k, tb * P:(tb + 1) * P], W[:, s, k, :],
                                                      start=(k == 0), stop=(k == KB - 1))
                        mm.then_inc(w_done[s], 1)
                    else:
                        matmul_tile(p, st, j, j, src, width=width)
                for g, _, h, w, _r in segs_of(j - 1):
                    p.wait_ge(e_sq, g + 1)
                    if g >= 2:
                        p.wait_ge(e_root, g - 1)
                    nc.tensor.matmul(PS[:, 4 + g % 2, 0:w], ONES[:, :], SQ[:, (g % 2) * H:(g % 2) * H + w],
                                     start=True, stop=True).then_inc(e_ss, 1)
                for g, r, h, w, rotated in segs_of(j - 2):
                    if rotated:
                        p.wait_ge(e_qn, g + 1)
                        if r >= 2:
                            p.wait_ge(e_rt, r - 1)
                        nc.tensor.matmul(PS[:, 6 + r % 2, 0:w], ROT[:, :],
                                         AR[:, QN + (r % 2) * H:QN + (r % 2) * H + w],
                                         start=True, stop=True).then_inc(e_rot, 1)

        def act(a, link):
            st = EvIn.st
            wait_done(a, EvIn.after)
            for j in range(len(EV) + 1):
                if j < len(EV):
                    kind, i = EV[j]
                    wait_sums(a, st, j)
                    pr = pair(st, j)
                    ev = None
                    if kind == "val":
                        ev = nc.scalar.activation(AV[:, i, 8:8 + T], bank2(pr), ACT.Identity)
                    elif kind == "gate":
                        ev = nc.scalar.activation(AG[:, i, :], bank2(pr), ACT.Silu)
                    elif kind == "v":
                        ev = nc.scalar.activation(V0[:, 2:10, i * HD:(i + 1) * HD],
                                                  bank2(pr).rearrange("p (b n) -> p b n", n=HD), ACT.Identity)
                    elif kind == "vctx":
                        ev = nc.scalar.activation(V0[:, 0:2, i * HD:(i + 1) * HD],
                                                  bank2(pr)[:, 0:CTX].rearrange("p (b n) -> p b n", n=HD),
                                                  ACT.Identity)
                    elif kind == "bgate":
                        if i == 0:
                            a.wait_ge(pool_mix, 2)
                        ev = nc.scalar.activation(BG[:, i * T:(i + 1) * T], bank2(pr), ACT.Silu)
                    if ev is not None:
                        ev.then_inc(evicted[pr], 1)
                    for g, _, h, w, _r in segs_of(j):
                        if g >= 2:
                            a.wait_ge(e_ss, g - 1)
                        nc.scalar.activation(SQ[:, (g % 2) * H:(g % 2) * H + w], PS[:, 2 * pr + h, 0:w],
                                             ACT.Square).then_inc(e_sq, 1)
                for g, _, h, w, _r in segs_of(j - 1):
                    a.wait_ge(e_ss, g + 1)
                    if g >= 2:
                        a.wait_ge(e_qn, g - 1)
                    nc.scalar.activation(RINV[:, (g % 2) * H:(g % 2) * H + w], PS[:, 4 + g % 2, 0:w], ACT.Sqrt,
                                         scale=1.0 / HD, bias=EPS(RMS_EPS)).then_inc(e_root, 1)

        def dve(v, link):
            st = EvIn.st
            wait_done(v, EvIn.after)
            for j in range(len(EV) + 2):
                ss = segs_of(j - 1)
                for n, (g, r, h, w, rotated) in enumerate(ss):
                    kind, i = EV[j - 1]
                    pr = pair(st, j - 1)
                    rv = RINV[:, (g % 2) * H:(g % 2) * H + w]
                    v.wait_ge(e_root, g + 1)
                    link(nc.vector.reciprocal(rv, rv))
                    gain = vec("q_g" if kind == "q" else "k_g")
                    if rotated and r >= 2:
                        v.wait_ge(e_rot, r - 1)
                        v.wait_ge(e_cos, r - 1)
                    dst = AR[:, QN + (r % 2) * H:QN + (r % 2) * H + w] if rotated else head_dst(kind, i, h, w)
                    nc.vector.scalar_tensor_tensor(dst, PS[:, 2 * pr + h, 0:w], gain, rv,
                                                   ALU.mult, ALU.mult).then_inc(e_qn, 1)
                    if n == len(ss) - 1:
                        v.wait_ge(e_qn, g + 1)
                        nc.vector.memset(FLAG[:, 0:1], 0.0).then_inc(evicted[pr], 1)
                for g, r, h, w, rotated in segs_of(j - 2):
                    if rotated:
                        kind, i = EV[j - 2]
                        v.wait_ge(e_rot, r + 1)
                        rt = AR[:, RT + (r % 2) * H:RT + (r % 2) * H + w]
                        if r >= 2:
                            v.wait_ge(e_head, r - 1)
                        nc.vector.tensor_tensor(rt, PS[:, 6 + r % 2, 0:w], SIN[:, h * H:h * H + w],
                                                ALU.mult).then_inc(e_rt, 1)
                        v.wait_ge(e_rt, r + 1)
                        v.wait_ge(e_cos, r + 1)
                        dst = head_dst(kind, i, h, w)
                        nc.vector.tensor_tensor(dst, dst, rt, ALU.add).then_inc(e_head, 1)

        def pool(g_, link):
            st = EvIn.st
            wait_done(g_, EvIn.after)
            g_.wait_ge(tab_in, 64)
            pa, pb = ar(PA, 1040), ar(PB, 1040)
            tt = nc.gpsimd.tensor_tensor
            for b in range(2):
                g_.wait_ge(evicted[pair(st, b)], (st.n0 + b) // 2 + 1)
                x = AV[:, b, :]
                link(tt(pa[:, 1:1040], x[:, 0:1039], x[:, 1:1040], ALU.add))
                link(tt(pb[:, 2:1039], pa[:, 1:1038], pa[:, 3:1040], ALU.add))
                if b == 1:
                    link(tt(pa[:, 4:1037], pb[:, 2:1035], pb[:, 6:1039], ALU.add))
                    link(tt(pb[:, 8:1032], pa[:, 4:1028], pa[:, 12:1036], ALU.add))
                for lo, s in ((0, pa), (64, pb)):
                    m = s[lo:lo + 64, 8:8 + T]
                    link(tt(m, m, INVCNT[lo:lo + 64, b, :], ALU.mult))
                    y = x[lo:lo + 64, 8:8 + T]
                    i_ = tt(y, m, y, ALU.subtract)
                    link(i_)
                nc.gpsimd.memset(FLAG[:, 1:2], 0.0).then_inc(pool_mix, 1)
            for g, (j, h, w, rotated) in enumerate(SEGS):
                if not rotated:
                    continue
                r = sum(s[3] for s in SEGS[:g])
                kind, i = EV[j]
                g_.wait_ge(e_qn, g + 1)
                nc.gpsimd.tensor_tensor(head_dst(kind, i, h, w), AR[:, QN + (r % 2) * H:QN + (r % 2) * H + w],
                                        COS[:, h * H:h * H + w], ALU.mult).then_inc(e_cos, 1)

    FLAG = sb("flags", 4)
    S.append(EvIn)

    MT = HT
    A_P, A_PT, A_QC = A_S0, A_S0 + 2 * KEYS, A_S0 + 4 * KEYS
    NEG, RS = sb("neg_max", 2), sb("row_sum", 2)
    a_qc, a_s, a_mx, a_neg, a_p, a_rs = (sem("a_" + x) for x in ("qc", "s", "mx", "neg", "p", "rs"))
    a_pn, a_t, a_pta, a_ptb, a_pv, a_o = (sem("a_" + x) for x in ("pn", "t", "pta", "ptb", "pv", "o"))
    pm, pme = sem("pool_mm"), sem("pool_out")
    UNITS = N_HEADS * (T // P)
    HALF_U = UNITS // N_KV

    def kv_of(u):
        return min(u, UNITS - 1) // HALF_U

    class Attention(Stage):
        name = "attention"
        after = EvIn.done
        done = [(a_o, UNITS), (pme, 4)]

        def cycles(eng, fn, link=None, per=0):
            def run(lo, hi, loop):
                if not loop:
                    for i in range(lo, hi):
                        fn(None, i)
                    return
                with eng.Fori(0, (hi - lo) // 2) as it:
                    if link:
                        link.enter(it, per)
                    fn(it, lo)
                    fn(it, lo + 1)
                if link:
                    link.leave((hi - lo) // 2)

            run(0, 4, False)
            run(4, 20, True)
            run(20, 28, False)
            run(28, 44, True)
            run(44, UNITS + 1, False)

        def pe(p):
            wait_done(p, Attention.after)
            p.wait_ge(pw_in, 16)
            p.wait_ge(tab_in, 64)
            for b in range(2):
                for h in range(2):
                    if b:
                        p.wait_ge(pme, h + 1)
                    nc.tensor.matmul(PS[:, 6 + h, :], POOLW_T[:, b, :], AV[:, b, 8 + h * H:8 + h * H + H],
                                     start=True, stop=True).then_inc(pm, 1)
            p.wait_ge(pme, 4)

            def scores(it, u):
                par, kv = u % 2, kv_of(u)
                p.wait_ge(a_qc, span(u + 1, it, 2) if it is not None else u + 1)
                if u >= 2:
                    p.wait_ge(a_pta, span(u - 1, it, 2) if it is not None else u - 1)
                    p.wait_ge(a_ptb, span(u - 1, it, 2) if it is not None else u - 1)
                q = AR[:, A_QC + par * P:A_QC + par * P + P]
                for c in range(0, KEYS, H):
                    w = min(H, KEYS - c)
                    mm = nc.tensor.matmul(PS[:, 3 * par + c // H, 0:w], q, K0[:, kv, c:c + w],
                                          start=True, stop=True)
                mm.then_inc(a_s, 1)

            def cycle(it, i):
                v_ = lambda n: span(n, it, 2) if it is not None else n
                par = i % 2
                if i < UNITS:
                    p.wait_ge(a_pn, v_(i + 1))
                    pw = A_P + par * KEYS
                    for b in range(KEYS // P):
                        mm = nc.tensor.transpose(PS[:, 3 * par + b // 4, (b % 4) * P:(b % 4 + 1) * P],
                                                 AR[:, pw + b * P:pw + (b + 1) * P], IDENT[:, :])
                    mm.then_inc(a_t, 1)
                if i >= 1:
                    q = (i - 1) % 2
                    p.wait_ge(a_pta, v_(i))
                    p.wait_ge(a_ptb, v_(i))
                    if i >= 3:
                        p.wait_ge(a_o, v_(i - 2))
                    for b in range(KEYS // P):
                        mm = nc.tensor.matmul(PS[:, 6 + q, 0:P],
                                              V0[:, b, kv_of(i - 1) * HD:(kv_of(i - 1) + 1) * HD],
                                              AR[:, A_PT + q * KEYS + b * P:A_PT + q * KEYS + (b + 1) * P],
                                              start=(b == 0), stop=(b == KEYS // P - 1))
                    mm.then_inc(a_pv, 1)
                if i + 2 < UNITS:
                    scores(it, i + 2)

            scores(None, 0)
            scores(None, 1)
            Attention.cycles(p, cycle)

        def act(a, link):
            wait_done(a, Attention.after)

            def softexp(it, u):
                par = u % 2
                v_ = lambda n: span(n, it, 2) if it is not None else n
                a.wait_ge(a_neg, v_(u + 1))
                if u >= 2:
                    a.wait_ge(a_t, v_(u - 1))
                nc.scalar.activation(AR[:, A_P + par * KEYS:A_P + (par + 1) * KEYS],
                                     PS[:, 3 * par:3 * par + 3, :].rearrange("p b t -> p (b t)")[:, 0:KEYS],
                                     ACT.Exp, bias=NEG[:, par:par + 1], scale=SCALE0,
                                     accum_out=RS[:, par:par + 1]).then_inc(a_p, 1)

            def cycle(it, i):
                par = i % 2
                v_ = lambda n: span(n, it, 2) if it is not None else n
                if i < UNITS:
                    a.wait_ge(a_t, v_(i + 1))
                    if i >= 2:
                        a.wait_ge(a_pv, v_(i - 1))
                    nc.scalar.activation(AR[:, A_PT + par * KEYS + H:A_PT + par * KEYS + 2 * H],
                                         PS[:, 3 * par + 1, :], ACT.Identity).then_inc(a_ptb, 1)
                if i + 2 < UNITS:
                    softexp(it, i + 2)

            softexp(None, 0)
            softexp(None, 1)
            Attention.cycles(a, cycle)

        def dve(v, link):
            wait_done(v, Attention.after)
            for b in range(2):
                for h in range(2):
                    v.wait_ge(pm, 2 * b + h + 1)
                    nc.vector.scalar_tensor_tensor(MT[:, b, h * H:(h + 1) * H], PS[:, 6 + h, :],
                                                   vec("pool_scale", b), AG[:, b, h * H:(h + 1) * H],
                                                   ALU.mult, ALU.mult).then_inc(pme, 1)

            def top(it, u):
                par = u % 2
                v_ = lambda n: span(n, it, 2) if it is not None else n
                v.wait_ge(a_s, v_(u + 1))
                if u >= 2:
                    v.wait_ge(a_p, v_(u - 1))
                sc = PS[:, 3 * par:3 * par + 3, :].rearrange("p b t -> p (b t)")[:, 0:KEYS]
                nc.vector.reduce_max(NEG[:, par:par + 1], sc, AX_X).then_inc(a_mx, 1)
                v.wait_ge(a_mx, v_(u + 1))
                nc.vector.tensor_scalar(NEG[:, par:par + 1], NEG[:, par:par + 1], -SCALE0, None,
                                        ALU.mult).then_inc(a_neg, 1)

            def cycle(it, i):
                par = i % 2
                v_ = lambda n: span(n, it, 2) if it is not None else n
                if i < UNITS:
                    v.wait_ge(a_p, v_(i + 1))
                    rs = RS[:, par:par + 1]
                    nc.vector.reciprocal(rs, rs).then_inc(a_rs, 1)
                    v.wait_ge(a_rs, v_(i + 1))
                    pw = AR[:, A_P + par * KEYS:A_P + (par + 1) * KEYS]
                    nc.vector.tensor_scalar(pw, pw, rs, None, ALU.mult).then_inc(a_pn, 1)
                    v.wait_ge(a_t, v_(i + 1))
                    if i >= 2:
                        v.wait_ge(a_pv, v_(i - 1))
                    pt = A_PT + par * KEYS
                    nc.vector.tensor_copy(AR[:, pt:pt + H], PS[:, 3 * par, :])
                    nc.vector.tensor_copy(AR[:, pt + 2 * H:pt + KEYS],
                                          PS[:, 3 * par + 2, 0:KEYS - 2 * H]).then_inc(a_pta, 1)
                if i >= 1:
                    q = (i - 1) % 2
                    v.wait_ge(a_pv, v_(i))
                    at = span((i - 1) * P, it, 2 * P) if it is not None else (i - 1) * P
                    nc.vector.tensor_tensor(HT_[:, bass.ds(at + 2 * T, P)], PS[:, 6 + q, 0:P],
                                            BG[:, bass.ds(at, P)], ALU.mult).then_inc(a_o, 1)
                if i + 2 < UNITS:
                    top(it, i + 2)

            top(None, 0)
            top(None, 1)
            Attention.cycles(v, cycle)

        def pool(g, link):
            wait_done(g, Attention.after)

            def copy(it, u):
                v_ = lambda n: span(n, it, 2) if it is not None else n
                if u >= 2:
                    g.wait_ge(a_s, v_(u - 1))
                at = span(u * P, it, 2 * P) if it is not None else u * P
                nc.gpsimd.tensor_copy(AR[:, A_QC + (u % 2) * P:A_QC + (u % 2 + 1) * P],
                                      Q0[:, bass.ds(at, P)]).then_inc(a_qc, 1)

            copy(None, 0)
            copy(None, 1)
            with g.Fori(0, UNITS // 2 - 1) as it:
                copy(it, 2)
                copy(it, 3)

    S.append(Attention)

    def residual_linear(name, src, after, gate=None, keep=1.0):
        class St(Stage):
            pass
        st = PLAN[name]
        St.name, St.st = name, st
        St.done = pairs_done(st, 8)

        def pe(p):
            wait_done(p, after)
            for n in range(8):
                matmul_tile(p, st, n, n, src)

        def dve(v, link):
            wait_done(v, after)
            for n in range(8):
                wait_sums(v, st, n)
                pr = pair(st, n)
                if gate is not None:
                    i_ = nc.vector.scalar_tensor_tensor(XT[:, n, :], bank2(pr), gate(n), XT[:, n, :],
                                                        ALU.mult, ALU.add)
                else:
                    i_ = nc.vector.scalar_tensor_tensor(XT[:, n, :], XT[:, n, :], keep, bank2(pr),
                                                        ALU.mult, ALU.add)
                i_.then_inc(evicted[pr], 1)

        St.pe, St.dve = pe, dve
        S.append(St)
        return St.done

    done = residual_linear("ev_out", MT, Attention.done, gate=lambda n: mod(0, 2, n))

    spill = nc.dram_tensor("resid_spill", (D, T), F32, kind="Internal").ap().rearrange("(k p) t -> p k t", p=P)
    spilled, unspilled = sem("spilled"), sem("unspilled")
    ev_out_done = done
    h1_done = norm_stage("n_x1", "rms", XT, HT, T, RMS_EPS, lambda k: mod(1, 1, k), lambda k: mod(1, 0, k),
                         ev_out_done)

    B_Z, B_X1, B_X2, B_K, B_Y, B_TMP = 0, 2048, 4096, 6144, 10240, 14336
    B_COLS, B_INVN, B_TAB = 16386, 16397, 16896
    COLS = ar(B_COLS, 11)
    INVN = ar(B_INVN, 256)
    TAB = ar(B_TAB, 6 * 4 * H, "p (i b n) -> p i b n", i=6, b=4)
    FCE, FCO, FSE, FSO, ICE, ISE = (TAB[:, i] for i in range(6))
    W3S = sb("w3_slice", H)
    HDN = RINV
    CWSW = SQ[:, :].rearrange("p (m n) -> p m n", m=2)
    Z1 = ar(B_Z, 2048, "p (b c) -> p b c", b=8)
    XO = [ar(B_X1, 2048, "p (b c) -> p b c", b=8), ar(B_X2, 2048, "p (b c) -> p b c", b=8)]
    M1 = XT

    C1 = float(np.float32(6.28125))
    C2 = float(np.float32(TWO_PI - 6.28125))
    C3 = float(TWO_PI - 6.28125 - C2)
    ROUND = 1.5 * 2.0 ** 23
    PI_DOWN = float(np.nextafter(np.float32(np.pi), np.float32(0)))

    def reduce_angle(v, link, x, n):
        link(nc.vector.tensor_scalar(n, x, 1.0 / TWO_PI, ROUND, ALU.mult, ALU.add))
        link(nc.vector.tensor_scalar(n, n, -ROUND, None, ALU.add))
        for c in (C1, C2, C3):
            link(nc.vector.scalar_tensor_tensor(x, n, -c, x, ALU.mult, ALU.add))
        link(nc.vector.tensor_scalar(x, x, PI_DOWN, -PI_DOWN, ALU.min, ALU.max))

    mlp_in, hp_mm, hp_arg, hp_sin = sem("mlp_in"), sem("hp_mm"), sem("hp_arg"), sem("hp_sin")
    dft_in, seq_in, ch_in = sem("dft_in"), sem("seq_in"), sem("ch_in")
    E0 = 8192
    EMB, W1, W2 = AR[0:33, E0:E0 + T], AR[0:33, E0 + T:E0 + T + 64], AR[0:64, E0 + T + 64:E0 + T + 128]
    ANG, ROT_N = AR[0:64, E0 + T + 128:E0 + 2 * T + 128], AR[0:64, E0 + 2 * T + 128:E0 + 3 * T + 128]
    HDN1 = AR[0:64, E0 + 3 * T + 128:E0 + 4 * T + 128]

    class HyPrep(Stage):
        name = "hy_prep"
        done = [(hp_sin, 2)]

        def pool(g, link):
            wait_done(g, ev_out_done)
            g.dma_start(spill, XT).then_inc(spilled, 16)
            g.dma_start(EMB, ins["hy_emb"]).then_inc(mlp_in, 16)
            g.dma_start(W1, ins["hy_w1"]).then_inc(mlp_in, 16)
            g.dma_start(W2, ins["hy_w2"]).then_inc(mlp_in, 16)
            g.dma_start(COLS, ins["hy_cols"]).then_inc(dft_in, 16)
            g.dma_start(ar(0, 8192, "p (i b t) -> p i b t", i=2, b=8),
                        ins["fn_seq"].rearrange("i (b p) t -> p i b t", p=P)).then_inc(seq_in, 16)
            for i in range(6):
                g.dma_start(TAB[:, i], ins["hy_dft"][i].rearrange("(b p) n -> p b n", p=P)).then_inc(dft_in, 16)

        def pe(p):
            wait_done(p, h1_done)
            p.wait_ge(mlp_in, 48)
            for i, (w, src) in enumerate(((W1, EMB), (W2, HDN1))):
                if i:
                    p.wait_ge(hp_sin, 1)
                for h in range(2):
                    nc.tensor.matmul(PS[0:64, 4 + 2 * i + h, :], w, src[:, h * H:(h + 1) * H],
                                     start=True, stop=True).then_inc(hp_mm, 1)

        def dve(v, link):
            wait_done(v, h1_done)
            for i in range(2):
                v.wait_ge(hp_mm, 2 * (i + 1))
                if i:
                    v.wait_ge(hp_sin, 1)
                ps = PS[0:64, 4 + 2 * i:6 + 2 * i, :].rearrange("p b t -> p (b t)")
                link(nc.vector.tensor_scalar(ANG, ps, vec("hy_b%d" % (i + 1))[0:64], vec("hy_freq")[0:64],
                                             ALU.add, ALU.mult))
                reduce_angle(v, link, ANG, ROT_N)
                nc.vector.memset(FLAG[:, 0:1], 0.0).then_inc(hp_arg, 1)

        def act(a, link):
            wait_done(a, h1_done)
            for i, dst in enumerate((HDN1, HDN[0:64, :])):
                a.wait_ge(hp_arg, i + 1)
                nc.scalar.activation(dst, ANG, ACT.Sin).then_inc(hp_sin, 1)

    S.append(HyPrep)

    SEQ = ar(0, 8192, "p (i b t) -> p i b t", i=2, b=8)
    FAB = ar(8192, 4096, "p (b n) -> p b n", b=8)
    FIN, FGT = ar(12288, 2048, "p (k t) -> p k t", k=2), ar(14336, 2048, "p (k t) -> p k t", k=2)
    CH = ar(8192, 1024, "p (i k n) -> p i k n", i=2, k=2)
    FNW = ar(9216, 512, "p (k n) -> p k n", k=2)
    YS = ar(12288, 2048, "p (i t) -> p i t", i=4)
    f_cw, f_cwv, f_ab, f_aba, f_abd = (sem("f_" + x) for x in ("cw", "cwv", "ab", "aba", "abd"))
    f_y, f_ys, f_out = sem("f_y"), sem("f_ys"), sem("f_out")

    class Fourier(Stage):
        name = "fn_in"
        st = PLAN["fn_in"]
        done = pairs_done(PLAN["fn_in"], 4) + [(f_out, 2)]

        def pool(g, link):
            wait_done(g, HyPrep.done)
            g.dma_start(CH, ins["fn_ch"].rearrange("i (k p) n -> p i k n", p=P)).then_inc(ch_in, 16)
            g.dma_start(FNW, ins["fn_w"].rearrange("(k p) n -> p k n", p=P)).then_inc(ch_in, 16)

        def pe(p):
            st = Fourier.st
            wait_done(p, HyPrep.done)
            for n in range(4):
                matmul_tile(p, st, n, n, HT)
            p.wait_ge(ch_in, 32)
            for m in range(2):
                for i in range(2):
                    for k in range(2):
                        mm = nc.tensor.matmul(PS[:, 4 + m, i * 256:(i + 1) * 256], CH[:, i, k, m * P:(m + 1) * P],
                                              FNW[:, k, :], start=(k == 0), stop=(k == 1))
                mm.then_inc(f_cw, 1)
            p.wait_ge(f_cwv, 2)
            wait_done(p, pairs_done(st, 4))
            for b in range(8):
                if b >= 4:
                    p.wait_ge(f_aba if b % 2 else f_abd, (b - 4) // 2 + 1)
                for k in range(2):
                    mm = nc.tensor.matmul(PS[:, 4 + b % 4, :], FIN[:, k, b * P:(b + 1) * P], CWSW[:, k, :],
                                          start=(k == 0), stop=(k == 1))
                mm.then_inc(f_ab, 1)
            p.wait_ge(f_aba, 4)
            p.wait_ge(f_abd, 4)
            p.wait_ge(seq_in, 16)
            p.wait_ge(dft_in, 16 * 7)
            for i in range(2):
                for ty in range(2):
                    for b in range(8):
                        mm = nc.tensor.matmul(PS[:, 4 + 2 * i + ty, :], FAB[:, b, ty * 256 + i * P:ty * 256 + (i + 1) * P],
                                              SEQ[:, ty, b, :], start=(b == 0), stop=(b == 7))
                for b in range(8):
                    mm = nc.tensor.matmul(PS[:, i, 0:1], FAB[:, b, i * P:(i + 1) * P], COLS[:, 10:11],
                                          start=(b == 0), stop=(b == 7))
                mm.then_inc(f_y, 1)

        def act(a, link):
            st = Fourier.st
            wait_done(a, HyPrep.done)
            for n in range(4):
                wait_sums(a, st, n)
                dst = FIN[:, n, :] if n < 2 else FGT[:, n - 2, :]
                nc.scalar.activation(dst, bank2(pair(st, n)),
                                     ACT.Identity if n < 2 else ACT.Silu).then_inc(evicted[pair(st, n)], 1)
            for b in range(1, 8, 2):
                a.wait_ge(f_ab, b + 1)
                nc.scalar.activation(FAB[:, b, :], PS[:, 4 + b % 4, :], ACT.Identity).then_inc(f_aba, 1)
            for i in range(2):
                a.wait_ge(f_y, i + 1)
                nc.scalar.activation(YS[:, i, :], PS[:, 5 + 2 * i, :], ACT.Identity).then_inc(f_ys, 1)

        def dve(v, link):
            wait_done(v, HyPrep.done)
            for m in range(2):
                v.wait_ge(f_cw, m + 1)
                nc.vector.tensor_copy(CWSW[:, m, :], PS[:, 4 + m, :]).then_inc(f_cwv, 1)
            for b in range(0, 8, 2):
                v.wait_ge(f_ab, b + 1)
                nc.vector.tensor_copy(FAB[:, b, :], PS[:, 4 + b % 4, :]).then_inc(f_abd, 1)
            v.wait_ge(spilled, 16)
            for i in range(2):
                y, yc = M1[:, 6 + i, :], PS[:, 4 + 2 * i, :]
                v.wait_ge(f_ys, i + 1)
                link(nc.vector.tensor_tensor(y[:, 0:H], yc, YS[:, i, :], ALU.subtract))
                link(nc.vector.tensor_tensor(y[:, T - 1:H:-1], yc[:, 1:H], YS[:, i, 1:H], ALU.add))
                link(nc.vector.tensor_copy(y[:, H:H + 1], PS[:, i, 0:1]))
                nc.vector.tensor_tensor(y, y, FGT[:, i, :], ALU.mult).then_inc(f_out, 1)

    S.append(Fourier)

    rows_in, w3_in = sem("rows_in"), sem("w3_in")
    cv_out, tr, tok_a, tok_d = sem("cv_out"), sem("tr"), sem("tok_a"), sem("tok_d")
    g_h, g_dec, g_g, g_abs, g_sum, g_pm, g_inv = (sem("g_" + x) for x in ("h", "dec", "g", "abs", "sum", "pm", "inv"))
    k_t, k_c, k_d, z_t, z_c, z_d = (sem("fft_" + x) for x in ("kt", "kc", "kd", "zt", "zc", "zd"))
    i_t, i_skip, z_new = sem("inv_t"), sem("inv_skip"), sem("z_new")
    b_t, b_o, g_d = sem("back_t"), sem("back_o"), sem("gated")
    UC, SP_ = ar(B_TMP, T), ar(B_TMP + T, T + 2)
    TMP = [ar(B_TMP, T), ar(B_TMP + T, T)]
    G = [ar(B_K, H), ar(B_K + H, H)]
    GA = [ar(B_K + 2 * H, H), ar(B_K + 3 * H, H)]
    DEC = [ar(B_K + 4 * H, 256), ar(B_K + 4 * H + 256, 256)]
    DELTA, SKIP = SQ[:, 0:256], [SQ[:, 256:512], SQ[:, 512:768]]
    KF = ar(B_K, 4096, "p (i b c) -> p i b c", i=2, b=8)
    PM = ar(B_Y, 4096, "p (i b c) -> p i b c", i=2, b=8)
    YF = ar(B_Y, 4096, "p (b q) -> p b q", b=4)

    def tok_cols(t, tb):
        a = tb // 4 + 2 * P * (tb % 4)
        return t[:, a:a + 2 * P - 1:2]

    class Hyena(Stage):
        name = "od_in"
        st = PLAN["od_in"]
        done = pairs_done(PLAN["od_in"], 24) + [(g_d, 6)]

        def pool(g, link):
            wait_done(g, Fourier.done)
            for c in range(3):
                if c:
                    g.wait_ge(z_new, 8 * c)
                    g.wait_ge(i_skip, 2 * c)
                g.dma_start(SQ[:, 0:768], ins["hy_rows"][c]).then_inc(rows_in, 16)
                for o in range(2):
                    n = 2 * c + o
                    if n:
                        g.wait_ge(g_h, 8 * n)
                    g.dma_start(W3S[0:64, :], ins["hy_w3"][n]).then_inc(w3_in, 16)
                    g.wait_ge(z_t, 4 * (n + 1))
                    g.wait_ge(rows_in, 16 * (c + 1))
                    nc.gpsimd.tensor_tensor(Z1, Z1, SKIP[o].unsqueeze(1).broadcast_to([P, 8, 256]),
                                            ALU.mult).then_inc(i_skip, 1)

        def pe(p):
            st = Hyena.st
            wait_done(p, Fourier.done)
            for c in range(3):
                for i in range(7):
                    if i < 6:
                        matmul_tile(p, st, 8 * c + i, 8 * c + i, HT)
                    if i:
                        q = 6 * c + i - 1
                        p.wait_ge(cv_out, q + 1)
                        if q:
                            p.wait_ge(tok_a, q)
                            p.wait_ge(tok_d, q)
                        for tb in range(8):
                            mm = nc.tensor.transpose(PS[:, 4 + tb // 4, (tb % 4) * P:(tb % 4 + 1) * P],
                                                     tok_cols(UC, tb), IDENT[:, :])
                            if tb % 4 == 3:
                                mm.then_inc(tr, 1)
                for o in range(2):
                    n = 2 * c + o
                    p.wait_ge(w3_in, 16 * (n + 1))
                    if o == 0:
                        p.wait_ge(tok_a, 6 * c + 6)
                        p.wait_ge(tok_d, 6 * c + 6)
                    else:
                        p.wait_ge(z_new, 4 * n)
                    for tb in range(9):
                        g = 8 * n + tb
                        if tb < 8:
                            if tb >= 2:
                                p.wait_ge(g_g, g - 1)
                            nc.tensor.matmul(PS[:, 4 + tb % 2, :], tok_cols(HDN[0:64, :], tb), W3S[0:64, :],
                                             start=True, stop=True).then_inc(g_h, 1)
                        if tb:
                            p.wait_ge(g_abs, g)
                            nc.tensor.matmul(PS[:, 6, :], ONES[:, :], GA[(tb - 1) % 2], start=(tb == 1),
                                             stop=(tb == 8)).then_inc(g_sum, 1)
                    p.wait_ge(g_pm, 8 * (n + 1))
                    p.wait_ge(g_inv, n + 1)
                    for which, (cos_src, sin_src, done_s, copied) in enumerate(
                            ((PM[:, 0], PM[:, 1], k_t, k_c), (Z1, Z1, z_t, z_c))):
                        for mb in range(4):
                            q = 4 * n + mb
                            if mb >= 2:
                                p.wait_ge(copied, q - 1)
                            elif which:
                                p.wait_ge(k_c, 4 * n + 3 + mb)
                            for ty, src in ((0, cos_src), (1, sin_src)):
                                for par in range(2):
                                    tab = TAB[:, 2 * ty + par]
                                    for ub in range(4):
                                        mm = nc.tensor.matmul(
                                            PS[:, 4 + 2 * (mb % 2) + ty, par * 256:(par + 1) * 256],
                                            tab[:, ub, mb * P:(mb + 1) * P], src[:, 4 * par + ub, :],
                                            start=(ub == 0), stop=(ub == 3))
                            mm.then_inc(done_s, 1)
                    p.wait_ge(z_d, 4 * (n + 1))
                    for tb in range(8):
                        par, ub = tb // 4, tb % 4
                        for ty in range(2):
                            tab = (ICE, ISE)[ty] if par == 0 else (FCO, FSO)[ty]
                            for mb in range(4):
                                part = 2 * ty + par
                                mm = nc.tensor.matmul(PS[:, 4 + tb // 2, (tb % 2) * 256:(tb % 2 + 1) * 256],
                                                      tab[:, mb, ub * P:(ub + 1) * P],
                                                      YF[:, mb, part * 256:(part + 1) * 256],
                                                      start=(ty == 0 and mb == 0), stop=(ty == 1 and mb == 3))
                        if tb % 2:
                            mm.then_inc(i_t, 1)
                p.wait_ge(z_new, 8 * (c + 1))
                for i in range(2):
                    for tb in range(8):
                        mm = nc.tensor.transpose(PS[:, 4 + 2 * i + tb // 4, (tb % 4) * P:(tb % 4 + 1) * P],
                                                 Z1[:, tb, i * P:(i + 1) * P], IDENT[:, :])
                        if tb % 4 == 3:
                            mm.then_inc(b_t, 1)
                for i in range(2):
                    matmul_tile(p, st, 8 * c + 6 + i, 8 * c + 6 + i, HT)
                p.wait_ge(b_o, 4 * (c + 1))

        def act(a, link):
            st = Hyena.st
            wait_done(a, Fourier.done)
            for c in range(3):
                if c:
                    a.wait_ge(g_d, 2 * c)
                for i in range(7):
                    if i < 6:
                        j, q = 8 * c + i, 6 * c + i
                        blk = (i // 2) * 6 + 2 * c + i % 2
                        wait_sums(a, st, j)
                        if i:
                            a.wait_ge(tr, 2 * q)
                        pr = pair(st, j)
                        nc.scalar.activation(UC, bank2(pr), ACT.Identity, scale=vec("conv_w", 3 * blk + 1),
                                             bias=vec("conv_b", blk))
                        if q:
                            a.wait_ge(cv_out, q)
                        nc.scalar.activation(SP_[:, 1:1 + T], bank2(pr), ACT.Identity).then_inc(evicted[pr], 1)
                    if i:
                        q, ii = 6 * c + i - 1, i - 1
                        dst = (Z1, XO[0], XO[1])[ii // 2]
                        a.wait_ge(tr, 2 * q + 1)
                        nc.scalar.activation(dst[:, 0:4, (ii % 2) * P:(ii % 2 + 1) * P],
                                             PS[:, 4, :].rearrange("p (b n) -> p b n", b=4),
                                             ACT.Identity).then_inc(tok_a, 1)
                a.wait_ge(rows_in, 16 * (c + 1))
                for o in range(2):
                    n = 2 * c + o
                    if n:
                        a.wait_ge(z_d, 4 * n)
                    for tb in range(9):
                        g = 8 * n + tb
                        if tb < 8:
                            if tb >= 2:
                                a.wait_ge(g_g, g - 1)
                            nc.scalar.activation(DEC[tb % 2], DELTA, ACT.Exp,
                                                 scale=COLS[:, tb:tb + 1]).then_inc(g_dec, 1)
                        if tb:
                            a.wait_ge(g_g, g)
                            if tb >= 3:
                                a.wait_ge(g_sum, g - 2)
                            nc.scalar.activation(GA[(tb - 1) % 2], G[(tb - 1) % 2], ACT.Abs).then_inc(g_abs, 1)
                    for made, copied, used in ((k_t, k_c, k_d), (z_t, z_c, z_d)):
                        for mb in range(4):
                            q = 4 * n + mb
                            a.wait_ge(made, q + 1)
                            if mb >= 2:
                                a.wait_ge(used, q - 1)
                            elif made is z_t:
                                a.wait_ge(k_d, 4 * n + 3 + mb)
                            b = 4 + 2 * (mb % 2)
                            nc.scalar.activation(TMP[mb % 2], PS[:, b:b + 2, :].rearrange("p b t -> p (b t)"),
                                                 ACT.Identity).then_inc(copied, 1)
                for q in range(4):
                    i, par = q // 2, q % 2
                    a.wait_ge(b_t, 4 * c + q + 1)
                    nc.scalar.activation(M1[:, 2 * c + i, par:T:2], PS[:, 4 + q, :],
                                         ACT.Identity).then_inc(b_o, 1)
                for i in range(2):
                    j = 8 * c + 6 + i
                    wait_sums(a, st, j)
                    nc.scalar.activation(TMP[i], bank2(pair(st, j)), ACT.Silu).then_inc(evicted[pair(st, j)], 1)

        def dve(v, link):
            st = Hyena.st
            wait_done(v, Fourier.done)
            tt, ts, stt = nc.vector.tensor_tensor, nc.vector.tensor_scalar, nc.vector.scalar_tensor_tensor
            for c in range(3):
                link(nc.vector.memset(SP_[:, 0:1], 0.0))
                link(nc.vector.memset(SP_[:, T + 1:T + 2], 0.0))
                for i in range(7):
                    if i < 6:
                        j, q = 8 * c + i, 6 * c + i
                        blk = (i // 2) * 6 + 2 * c + i % 2
                        pr = pair(st, j)
                        v.wait_ge(evicted[pr], (st.n0 + j) // 2 + 1)
                        link(stt(UC, SP_[:, 0:T], vec("conv_w", 3 * blk), UC, ALU.mult, ALU.add))
                        stt(UC, SP_[:, 2:T + 2], vec("conv_w", 3 * blk + 2), UC, ALU.mult,
                            ALU.add).then_inc(cv_out, 1)
                    if i:
                        q, ii = 6 * c + i - 1, i - 1
                        dst = (Z1, XO[0], XO[1])[ii // 2]
                        v.wait_ge(tr, 2 * q + 2)
                        nc.vector.tensor_copy(dst[:, 4:8, (ii % 2) * P:(ii % 2 + 1) * P],
                                              PS[:, 5, :].rearrange("p (b n) -> p b n", b=4)).then_inc(tok_d, 1)
                for o in range(2):
                    n = 2 * c + o
                    for tb in range(8):
                        g = 8 * n + tb
                        v.wait_ge(g_h, g + 1)
                        v.wait_ge(g_dec, g + 1)
                        if tb >= 2:
                            v.wait_ge(g_abs, g - 1)
                        gg = G[tb % 2]
                        tt(gg.rearrange("p (s c) -> p s c", s=2), PS[:, 4 + tb % 2, :].rearrange("p (s c) -> p s c", s=2),
                           DEC[tb % 2].unsqueeze(1).broadcast_to([P, 2, 256]), ALU.mult).then_inc(g_g, 1)
                        v.wait_ge(g_g, g + 1)
                        h0, h1 = gg[:, 0:256], gg[:, 256:512]
                        if tb == 0:
                            stt(PM[:, 0, tb, :], h1, COLS[:, 8:9], h0, ALU.mult, ALU.add)
                            stt(PM[:, 1, tb, :], h1, COLS[:, 9:10], h0, ALU.mult, ALU.add).then_inc(g_pm, 1)
                        else:
                            tt(PM[:, 0, tb, :], h0, h1, ALU.add)
                            tt(PM[:, 1, tb, :], h0, h1, ALU.subtract).then_inc(g_pm, 1)
                    v.wait_ge(g_sum, 8 * (n + 1))
                    link(nc.vector.tensor_copy(INVN, PS[:, 6, 0:256]))
                    link(tt(INVN, INVN, PS[:, 6, 256:512], ALU.add))
                    link(ts(INVN, INVN, 1e-6, float(T), ALU.add, ALU.mult))
                    nc.vector.reciprocal(INVN, INVN).then_inc(g_inv, 1)
                    for mb in range(4):
                        q = 4 * n + mb
                        t = TMP[mb % 2]
                        e, od, se, so = (t[:, k * 256:(k + 1) * 256] for k in range(4))
                        v.wait_ge(k_c, q + 1)
                        tt(KF[:, 0, mb, :], e, od, ALU.add)
                        tt(KF[:, 0, 4 + mb, :], e, od, ALU.subtract)
                        tt(KF[:, 1, mb, :], se, so, ALU.add)
                        tt(KF[:, 1, 4 + mb, :], so, se, ALU.subtract).then_inc(k_d, 1)
                    v.wait_ge(k_d, 4 * (n + 1))
                    for mb in range(4):
                        q = 4 * n + mb
                        t = TMP[mb % 2]
                        e, od, se, so = (t[:, k * 256:(k + 1) * 256] for k in range(4))
                        y = YF[:, mb, :]
                        v.wait_ge(z_c, q + 1)
                        tt(y[:, 0:256], e, od, ALU.add)
                        tt(y[:, 256:512], e, od, ALU.subtract)
                        tt(y[:, 512:768], se, so, ALU.add)
                        link(tt(y[:, 768:1024], so, se, ALU.subtract))
                        two = "p (b c) -> p b c"
                        zc, zs = y[:, 0:512].rearrange(two, b=2), y[:, 512:1024].rearrange(two, b=2)
                        lo, hi = t[:, 0:512].rearrange(two, b=2), t[:, 512:1024].rearrange(two, b=2)
                        kc, ks = KF[:, 0, mb:mb + 5:4, :], KF[:, 1, mb:mb + 5:4, :]
                        tt(lo, zc, kc, ALU.mult)
                        link(tt(hi, zs, ks, ALU.mult))
                        link(tt(lo, lo, hi, ALU.subtract))
                        tt(hi, zc, ks, ALU.mult)
                        link(tt(zs, zs, kc, ALU.mult))
                        link(tt(hi, hi, zs, ALU.add))
                        yr, yrm, yi, yim = (t[:, k * 256:(k + 1) * 256] for k in range(4))
                        tt(y[:, 0:256], yr, yrm, ALU.add)
                        tt(y[:, 256:512], yr, yrm, ALU.subtract)
                        tt(y[:, 512:768], yi, yim, ALU.subtract)
                        tt(y[:, 768:1024], yi, yim, ALU.add).then_inc(z_d, 1)
                    v.wait_ge(i_skip, n + 1)
                    v.wait_ge(z_d, 4 * (n + 1))
                    for b in range(4):
                        v.wait_ge(i_t, 4 * n + b + 1)
                        two = "p (b c) -> p b c"
                        t = TMP[b % 2][:, 0:512].rearrange(two, b=2)
                        link(tt(t, PS[:, 4 + b, :].rearrange(two, b=2),
                                INVN.unsqueeze(1).broadcast_to([P, 2, 256]), ALU.mult))
                        link(tt(t, t, Z1[:, 2 * b:2 * b + 2, :], ALU.add))
                        tt(Z1[:, 2 * b:2 * b + 2, :], t, XO[o][:, 2 * b:2 * b + 2, :], ALU.mult).then_inc(z_new, 1)
                for i in range(2):
                    j = 8 * c + 6 + i
                    v.wait_ge(evicted[pair(st, j)], (st.n0 + j) // 2 + 1)
                    v.wait_ge(b_o, 4 * c + 2 * i + 2)
                    m = M1[:, 2 * c + i, :]
                    tt(m, m, TMP[i], ALU.mult).then_inc(g_d, 1)
                v.wait_ge(g_d, 2 * (c + 1))

    S.append(Hyena)

    class OdOut(Stage):
        name = "od_out"
        st = PLAN["od_out"]
        done = pairs_done(PLAN["od_out"], 8)

        def pool(g, link):
            wait_done(g, Hyena.done)
            g.dma_start(HT, spill).then_inc(unspilled, 16)

        def pe(p):
            wait_done(p, Hyena.done)
            for n in range(8):
                matmul_tile(p, OdOut.st, n, n, M1)

        def dve(v, link):
            st = OdOut.st
            wait_done(v, Hyena.done)
            v.wait_ge(unspilled, 16)
            for n in range(8):
                wait_sums(v, st, n)
                nc.vector.scalar_tensor_tensor(HT[:, n, :], bank2(pair(st, n)), mod(1, 2, n), HT[:, n, :],
                                               ALU.mult, ALU.add).then_inc(evicted[pair(st, n)], 1)

    S.append(OdOut)
    x2_done = norm_stage("n_first", "rms", HT, XT, T, RMS_EPS, lambda k: vec("final_g", k), None, OdOut.done)

    CK, NC = 8, T // 8
    NG, NP_, QP = 64, 32, 8
    u_dram = nc.dram_tensor("s5_in", (D, CK, NC), F32, kind="Internal").ap()
    y_dram = nc.dram_tensor("s5_out", (D, CK, NC), F32, kind="Internal").ap()
    at = [0]

    def take(words, pattern=None, **kw):
        at[0] += words
        assert at[0] <= 29184
        return ar(at[0] - words, words, pattern, **kw)

    PAR = take(96, "p (i j) -> p i j", i=3)
    SM = [take(32) for _ in range(24)]
    (DT, LRE, MAG, TH, TN, SH, S1, CO, LBR, LBI, NRE, DEN, CFR, CFI, TA, TB, M8, TC_) = SM[:18]
    BC = take(2048, "p (i j h) -> p i j h", i=4, j=NP_)
    BB = take(1024, "p (i j h) -> p i j h", i=2, j=NP_)
    PWR = take(2 * 9 * 32, "p (i n j) -> p i n j", i=2, n=9)
    WL = take(2 * 7 * 32, "p (i n j) -> p i n j", i=2, n=7)
    EPH = take(2048, "p (i j c) -> p i j c", i=2, j=QP)
    MAGC = take(1024, "p (j c) -> p j c", j=QP)
    CL = take(2 * QP * 9 * 16, "p (i j n h) -> p i j n h", i=2, j=QP, n=9)
    VB = take(2048, "p (i j s h) -> p i j s h", i=2, j=QP, s=CK)
    VBT = take(2048, "p (j i n) -> p j i n", j=QP, i=2)
    KM = take(16 * 240, "p (g n) -> p g n", g=16)
    TP = take(2048, "p (g n) -> p g n", g=16)
    RV = take(2048, "p (i j c) -> p i j c", i=2, j=QP)
    TV = take(2048, "p (i j c) -> p i j c", i=2, j=QP)
    STT_ = take(2 * QP * (NC + 1), "p (i j c) -> p i j c", i=2, j=QP)
    s5p_in, s5_exp, s5_ang, s5_sin, s5_ready = (sem("s5_" + x) for x in ("par", "exp", "ang", "sin", "ready"))
    s5_r, u_out, u_in, s5_zero = (sem("s5_" + x) for x in ("r", "u_out", "u_in", "zero"))
    s5_cl, s5_e, s5_vb, s5_k, s5_km, s5_tp = (sem("s5_" + x) for x in ("cl", "e", "vb", "k", "km", "tp"))
    s5_vt, s5_vbt, s5_v, s5_st, s5_y, s5_ye, y_out = (sem("s5_" + x) for x in
                                                     ("vt", "vbt", "v", "st", "y", "ye", "y_out"))
    y_in, s5_d, s5_h = sem("s5_y_in"), sem("s5_d"), sem("s5_h")
    YT = ar(0, 8192, "p (k t c) -> p k t c", k=KB, t=CK)
    YD = ar(8192, 8192, "p (k t) -> p k t", k=KB)

    class S5(Stage):
        name = "s5"
        done = [(s5_h, KB)]

        def pool(g, link):
            tt = nc.gpsimd.tensor_tensor
            wait_done(g, x2_done)
            g.dma_start(PAR, ins["s5_par"].rearrange("p (i j) -> p i j", i=3)).then_inc(s5p_in, 16)
            g.dma_start(BC, ins["s5_bc"].rearrange("p (i j h) -> p i j h", i=4, j=NP_)).then_inc(s5p_in, 16)
            nc.gpsimd.memset(KM[0:16], 0.0).then_inc(s5_zero, 1)
            nc.gpsimd.memset(STT_, 0.0).then_inc(s5_zero, 1)
            g.wait_ge(s5_r, KB)
            g.dma_start(u_dram.rearrange("(k p) s c -> p k (s c)", p=P), HT).then_inc(u_out, 16)
            g.wait_ge(u_out, 16)
            for s in range(CK):
                g.dma_start(HT_[16 * s:16 * s + 16, :].rearrange("p (g c) -> p g c", g=NG),
                            u_dram[:, s, :].rearrange("(g h) c -> h g c", h=16)).then_inc(u_in, 16)
            g.wait_ge(s5_ready, 1)
            for q in range(4):
                j0 = q * QP
                sh = [P, QP, 9, 16]
                pw = [PWR[:, i, :, j0:j0 + QP].rearrange("p n j -> p j n").unsqueeze(3).broadcast_to(sh)
                      for i in range(2)]
                cc = [BC[:, 2 + i, j0:j0 + QP, :].unsqueeze(2).broadcast_to(sh) for i in range(2)]
                if q:
                    g.wait_ge(s5_y, 4 * q)
                tmp = TCL.rearrange("p (j n h) -> p j n h", j=QP, n=9)
                link(tt(CL[:, 0], pw[0], cc[0], ALU.mult))
                link(tt(tmp, pw[1], cc[1], ALU.mult))
                link(tt(CL[:, 0], CL[:, 0], tmp, ALU.subtract))
                link(tt(CL[:, 1], pw[0], cc[1], ALU.mult))
                link(tt(tmp, pw[1], cc[0], ALU.mult))
                link(tt(CL[:, 1], CL[:, 1], tmp, ALU.add))
                nc.gpsimd.tensor_scalar(CL[:, 1], CL[:, 1], -1.0, None, ALU.mult).then_inc(s5_cl, 1)
                if q:
                    g.wait_ge(s5_st, q)
                link(nc.gpsimd.memset(EPH[:, 0, :, 0:1], 1.0))
                link(nc.gpsimd.memset(EPH[:, 1, :, 0:1], 0.0))
                for n in range(7):
                    k = 1 << n
                    w = [WL[:, i, n, j0:j0 + QP].unsqueeze(2).broadcast_to([P, QP, k]) for i in range(2)]
                    a, b = EPH[:, 0, :, 0:k], EPH[:, 1, :, 0:k]
                    x, y = EPH[:, 0, :, k:2 * k], EPH[:, 1, :, k:2 * k]
                    t = TCL[:, 0:QP * k].rearrange("p (j c) -> p j c", j=QP)
                    link(tt(x, a, w[0], ALU.mult))
                    link(tt(t, b, w[1], ALU.mult))
                    link(tt(x, x, t, ALU.subtract))
                    link(tt(y, a, w[1], ALU.mult))
                    link(tt(t, b, w[0], ALU.mult))
                    link(tt(y, y, t, ALU.add))
                link(nc.gpsimd.tensor_copy(MAGC, M8[:, j0:j0 + QP].unsqueeze(2).broadcast_to([P, QP, NC])))
                nc.gpsimd.memset(MAGC[:, :, 0:1], 0.0).then_inc(s5_e, 1)
            g.wait_ge(y_out, 16 * CK * 4)
            wait_done(g, [(s5_st, 4), (s5_y, 16)])
            g.dma_start(YT.rearrange("p k t c -> p k (t c)"),
                        y_dram.rearrange("(k p) t c -> p k (t c)", p=P)).then_inc(y_in, 16)

        def dve(v, link):
            tt, ts, stt = nc.vector.tensor_tensor, nc.vector.tensor_scalar, nc.vector.scalar_tensor_tensor
            wait_done(v, x2_done)
            for k in range(0, KB, 2):
                nc.vector.tensor_copy(HT[:, k, :].rearrange("p (s c) -> p s c", s=CK),
                                      XT[:, k, :].rearrange("p (c s) -> p s c", s=CK)).then_inc(s5_r, 1)
            v.wait_ge(s5p_in, 32)
            a_re, a_im = PAR[:, 0, :], PAR[:, 1, :]
            link(ts(LRE, a_re, -1e-4, None, ALU.min))
            v.wait_ge(s5_exp, 1)
            link(tt(TH, a_im, DT, ALU.mult))
            reduce_angle(v, link, TH, TN)
            tt(TA, LRE, DT, ALU.mult).then_inc(s5_ang, 1)
            v.wait_ge(s5_sin, 3)
            link(tt(CO, SH, SH, ALU.mult))
            link(ts(CO, CO, -2.0, 1.0, ALU.mult, ALU.add))
            link(tt(LBR, MAG, CO, ALU.mult))
            link(tt(LBI, MAG, S1, ALU.mult))
            link(ts(NRE, LBR, -1.0, None, ALU.add))
            link(tt(DEN, LRE, LRE, ALU.mult))
            link(tt(TB, a_im, a_im, ALU.mult))
            link(tt(DEN, DEN, TB, ALU.add))
            link(nc.vector.reciprocal(DEN, DEN))
            link(tt(CFR, NRE, LRE, ALU.mult))
            link(tt(TB, LBI, a_im, ALU.mult))
            link(tt(CFR, CFR, TB, ALU.add))
            link(tt(CFR, CFR, DEN, ALU.mult))
            link(tt(CFI, LBI, LRE, ALU.mult))
            link(tt(TB, NRE, a_im, ALU.mult))
            link(tt(CFI, CFI, TB, ALU.subtract))
            link(tt(CFI, CFI, DEN, ALU.mult))

            def cmul(xr, xi, ar_, ai, br, bi, t):
                link(tt(t, ai, bi, ALU.mult))
                link(tt(xr, ar_, br, ALU.mult))
                link(tt(xr, xr, t, ALU.subtract))
                link(tt(t, ai, br, ALU.mult))
                link(tt(xi, ar_, bi, ALU.mult))
                link(tt(xi, xi, t, ALU.add))

            sh = [P, NP_, 16]
            tb = TV.rearrange("p i j c -> p (i j c)")[:, 0:512].rearrange("p (j h) -> p j h", j=NP_)
            cmul(BB[:, 0], BB[:, 1], CFR.unsqueeze(2).broadcast_to(sh), CFI.unsqueeze(2).broadcast_to(sh),
                 BC[:, 0], BC[:, 1], tb)
            link(nc.vector.memset(PWR[:, 0, 0, :], 1.0))
            link(nc.vector.memset(PWR[:, 1, 0, :], 0.0))
            link(nc.vector.tensor_copy(PWR[:, 0, 1, :], LBR))
            link(nc.vector.tensor_copy(PWR[:, 1, 1, :], LBI))
            for n in range(2, 9):
                cmul(PWR[:, 0, n, :], PWR[:, 1, n, :], PWR[:, 0, n - 1, :], PWR[:, 1, n - 1, :], LBR, LBI, TB)
            link(tt(M8, MAG, MAG, ALU.mult))
            link(tt(M8, M8, M8, ALU.mult))
            link(tt(M8, M8, M8, ALU.mult))
            ph = [(CO, S1), (TN, TC_), (TA, SH)]
            cmul(TN, TC_, CO, S1, CO, S1, TB)
            cmul(TA, SH, TN, TC_, TN, TC_, TB)
            cmul(WL[:, 0, 0, :], WL[:, 1, 0, :], TA, SH, TA, SH, TB)
            for n in range(1, 7):
                r, i = WL[:, 0, n - 1, :], WL[:, 1, n - 1, :]
                cmul(WL[:, 0, n, :], WL[:, 1, n, :], r, i, r, i, TB)
            nc.vector.memset(FLAG[:, 0:1], 0.0).then_inc(s5_ready, 1)
            v.wait_ge(s5_zero, 2)
            for q in range(4):
                j0 = q * QP
                sh = [P, QP, CK, 16]
                pw = [PWR[:, i, 0:CK, j0:j0 + QP].rearrange("p n j -> p j n")[:, :, ::-1].unsqueeze(3)
                      .broadcast_to(sh) for i in range(2)]
                bb = [BB[:, i, j0:j0 + QP, :].unsqueeze(2).broadcast_to(sh) for i in range(2)]
                if q:
                    v.wait_ge(s5_vt, 4 * q)
                t4 = TV.rearrange("p i j c -> p (i j c)")[:, 0:1024].rearrange("p (j s h) -> p j s h", j=QP, s=CK)
                cmul(VB[:, 0], VB[:, 1], pw[0], pw[1], bb[0], bb[1], t4)
                nc.vector.memset(FLAG[:, 0:1], 0.0).then_inc(s5_vb, 1)
                v.wait_ge(s5_v, q + 1)
                v.wait_ge(s5_e, q + 1)
                ps = [PS[:, 4 + 2 * i:6 + 2 * i, :].rearrange("p b (j c) -> p (b j) c", c=NC) for i in range(2)]
                er, ei = EPH[:, 0], EPH[:, 1]
                link(tt(RV[:, 0], ps[0], er, ALU.mult))
                link(tt(RV[:, 1], ps[1], er, ALU.mult))
                link(tt(TV[:, 0], ps[1], ei, ALU.mult))
                link(tt(TV[:, 1], ps[0], ei, ALU.mult))
                link(tt(RV[:, 0], RV[:, 0], TV[:, 0], ALU.add))
                link(tt(RV[:, 1], RV[:, 1], TV[:, 1], ALU.subtract))
                mg = MAGC.rearrange("p j c -> p (j c)")
                for i in range(2):
                    link(nc.vector.tensor_tensor_scan(TV[:, i].rearrange("p j c -> p (j c)"), mg,
                                                      RV[:, i].rearrange("p j c -> p (j c)"), 0.0,
                                                      ALU.mult, ALU.add))
                if q:
                    v.wait_ge(s5_y, 4 * q)
                o = [STT_[:, i, :, 1:NC + 1] for i in range(2)]
                link(tt(RV[:, 0], TV[:, 1], ei, ALU.mult))
                link(tt(RV[:, 1], TV[:, 0], ei, ALU.mult))
                link(tt(o[0], TV[:, 0], er, ALU.mult))
                link(tt(o[1], TV[:, 1], er, ALU.mult))
                link(tt(o[0], o[0], RV[:, 0], ALU.subtract))
                tt(o[1], o[1], RV[:, 1], ALU.add).then_inc(s5_st, 1)
            v.wait_ge(y_in, 16)
            for k in range(KB):
                stt(YD[:, k, :].rearrange("p (c t) -> p c t", t=CK), XT[:, k, :].rearrange("p (c t) -> p c t", t=CK),
                    vec("ssm_d", k), YT[:, k].rearrange("p t c -> p c t"), ALU.mult, ALU.add).then_inc(s5_d, 1)

        def act(a, link):
            wait_done(a, x2_done)
            for k in range(1, KB, 2):
                nc.scalar.activation(HT[:, k, :].rearrange("p (s c) -> p s c", s=CK),
                                     XT[:, k, :].rearrange("p (c s) -> p s c", s=CK), ACT.Identity).then_inc(s5_r, 1)
            a.wait_ge(s5p_in, 32)
            nc.scalar.activation(DT, PAR[:, 2, :], ACT.Exp).then_inc(s5_exp, 1)
            a.wait_ge(s5_ang, 1)
            nc.scalar.activation(MAG, TA, ACT.Exp).then_inc(s5_sin, 1)
            nc.scalar.activation(SH, TH, ACT.Sin, scale=0.5).then_inc(s5_sin, 1)
            nc.scalar.activation(S1, TH, ACT.Sin).then_inc(s5_sin, 1)
            a.wait_ge(s5_zero, 2)
            for q in range(4):
                if q:
                    a.wait_ge(s5_tp, 16 * CK * q)
                for n, (b, g0) in enumerate(PARITY_BANKS):
                    a.wait_ge(s5_k, 4 * q + n + 1)
                    nc.scalar.activation(KM[0:16, g0:g0 + 7:2, 112:240],
                                         PS[0:16, 4 + b, :].rearrange("p (g n) -> p g n", g=4),
                                         ACT.Identity).then_inc(s5_km, 1)
                a.wait_ge(s5_km, 4 * (q + 1))
                if q:
                    a.wait_ge(s5_y, 4 * q)
                for s in range(CK):
                    a.dma_start(TP[16 * s:16 * s + 16], KM[0:16, :, (7 - s) * 16:(7 - s) * 16 + P]).then_inc(s5_tp, 16)
                if q:
                    a.wait_ge(s5_v, q)
                for b in range(4):
                    a.wait_ge(s5_vt, 4 * q + b + 1)
                    nc.scalar.activation(VBT[:, 2 * b:2 * b + 2], PS[:, 4 + b, :].rearrange("p (j i n) -> p j i n", j=2, i=2),
                                         ACT.Identity).then_inc(s5_vbt, 1)
                for n, (b, g0) in enumerate(PARITY_BANKS):
                    a.wait_ge(s5_y, 4 * q + n + 1)
                    nc.scalar.activation(HT_[:, :].rearrange("p (g c) -> p g c", c=NC)[:, 16 * q + g0:16 * q + g0 + 7:2, :],
                                         PS[:, b, :].rearrange("p (g c) -> p g c", c=NC),
                                         ACT.Identity).then_inc(s5_ye, 1)
                a.wait_ge(s5_ye, 4 * (q + 1))
                for t in range(CK):
                    a.dma_start(y_dram[256 * q:256 * (q + 1), t, :].rearrange("(g h) c -> h g c", h=16),
                                HT_[16 * t:16 * t + 16, 16 * q * NC:16 * (q + 1) * NC]
                                .rearrange("p (g c) -> p g c", g=16)).then_inc(y_out, 16)
            for k in range(KB):
                a.wait_ge(s5_d, k + 1)
                nc.scalar.activation(HT[:, k, :], YD[:, k, :], ACT.Gelu_apprx_tanh).then_inc(s5_h, 1)

        def pe(p):
            wait_done(p, x2_done)
            p.wait_ge(s5_ready, 1)
            for q in range(4):
                p.wait_ge(s5_cl, q + 1)
                if q:
                    p.wait_ge(s5_st, q)
                for g in range(16):
                    j, lo = g // 2, 64 * (g % 2)
                    for i in range(2):
                        mm = nc.tensor.matmul(PS[0:16, 4 + 2 * (g % 2) + j // 4, (j % 4) * P:(j % 4 + 1) * P],
                                              BB[lo:lo + 64, i, q * QP + j, :],
                                              CL[lo:lo + 64, i, j, 0:CK, :].rearrange("p n h -> p (n h)"),
                                              start=(i == 0), stop=(i == 1))
                    if j % 4 == 3:
                        mm.then_inc(s5_k, 1)
                p.wait_ge(s5_vb, q + 1)
                for n in range(16):
                    j, i = n // 2, n % 2
                    if n == 0:
                        p.wait_ge(s5_km, 4 * (q + 1))
                    mm = nc.tensor.transpose(PS[:, 4 + n // 4, (n % 4) * P:(n % 4 + 1) * P],
                                             VB[:, i, j].rearrange("p s h -> p (s h)"), IDENT[:, :])
                    if n % 4 == 3:
                        mm.then_inc(s5_vt, 1)
                p.wait_ge(s5_vbt, 4 * (q + 1))
                p.wait_ge(u_in, 16 * CK)
                for g in range(16):
                    j, lo = g // 2, 64 * (g % 2)
                    for i in range(2):
                        mm = nc.tensor.matmul(PS[lo:lo + 64, 4 + 2 * i + j // 4, (j % 4) * NC:(j % 4 + 1) * NC],
                                              VBT[:, j, i, lo:lo + 64],
                                              HT_[:, (16 * q + g) * NC:(16 * q + g + 1) * NC], start=True, stop=True)
                mm.then_inc(s5_v, 1)
                p.wait_ge(s5_st, q + 1)
                p.wait_ge(s5_tp, 16 * CK * (q + 1))
                if q:
                    p.wait_ge(s5_ye, 4 * q)
                for g in range(16):
                    j, lo = g // 2, 64 * (g % 2)
                    o = PS[:, 2 * (g % 2) + j // 4, (j % 4) * NC:(j % 4 + 1) * NC]
                    nc.tensor.matmul(o, TP[:, g, :], HT_[:, (16 * q + g) * NC:(16 * q + g + 1) * NC],
                                     start=True, stop=False)
                    for i in range(2):
                        mm = nc.tensor.matmul(o, CL[lo:lo + 64, i, j, 1:CK + 1, :].rearrange("p n h -> p (n h)"),
                                              STT_[lo:lo + 64, i, j, 0:NC], start=False, stop=(i == 1))
                    if j % 4 == 3:
                        mm.then_inc(s5_y, 1)

    TCL = take(QP * 9 * 16)
    PARITY_BANKS = ((0, 0), (2, 1), (1, 8), (3, 9))
    S.append(S5)

    SG = [ar(24576, T), ar(25600, T)]

    def gated_linear(name, src, dst_at, func, first_gated, after):
        class St(Stage):
            pass
        st = PLAN[name]
        trips = st.tiles // 4
        St.name, St.st = name, st
        St.done = pairs_done(st, st.tiles)
        f, o = (0, 1) if first_gated else (1, 0)

        def pe(p):
            wait_done(p, after)
            with p.Fori(0, trips) as it:
                for j in range(4):
                    matmul_tile(p, st, j, j, src, it, 4, 4)

        def act(a, link):
            wait_done(a, after)
            with a.Fori(0, trips) as it:
                for i in range(2):
                    j = 2 * i + f
                    wait_sums(a, st, j, it, 4)
                    nc.scalar.activation(SG[i], bank2(pair(st, j)), func).then_inc(evicted[pair(st, j)], 1)

        def dve(v, link):
            wait_done(v, after)
            with v.Fori(0, trips) as it:
                for i in range(2):
                    j, g = 2 * i + o, 2 * i + f
                    wait_sums(v, st, j, it, 4)
                    v.wait_ge(evicted[pair(st, g)], span((st.n0 + g) // 2 + 1, it, 2))
                    dst = AR[:, bass.ds(span(dst_at + i * T, it, 2 * T), T)]
                    nc.vector.tensor_tensor(dst, bank2(pair(st, j)), SG[i],
                                            ALU.mult).then_inc(evicted[pair(st, j)], 1)

        St.pe, St.act, St.dve = pe, act, dve
        S.append(St)
        return St.done

    done = gated_linear("glu", HT, 8192, ACT.Sigmoid, False, S5.done)
    ZG = ar(8192, 8192, "p (k t) -> p k t", k=KB)
    done = residual_linear("s5_out", ZG, done, keep=ALPHA)
    done = norm_stage("ln0", "layer", XT, XT, T, LN_EPS, lambda k: vec("ln_mix_g", k), lambda k: vec("ln_mix_b", k),
                      done)

    w_hi, w_lo = sem("w_hi"), sem("w_lo")
    x_hi, x_lo = sem("x_hi"), sem("x_lo")
    hid = sem("hid")
    split = dict.fromkeys(("w", "x", "hid"), 0)
    SGH = [FTMP[:, i * H:(i + 1) * H] for i in range(2)]
    HIDF = [FTMP[:, (2 + i) * H:(3 + i) * H] for i in range(2)]

    def ffn_half(i, half, after):
        gu, down = PLAN["gu%d%s" % (i, "ab"[half])], PLAN["down%d%s" % (i, "ab"[half])]
        w0, x0, hid0 = split["w"], split["x"], split["hid"]
        split["w"] += gu.tiles + down.tiles
        split["x"] += KB
        split["hid"] += FB + 2
        pieces = [range(a, min(a + KB, FB)) for a in range(0, FB, KB)]

        class St(Stage):
            name, also, done = down.name, gu.name, pairs_done(down, 8)

            def tile(p, n, st, j, it):
                p.wait_ge(w_lo, span(w0 + n + 1, it, 4 if st is gu else 12))
                return [WPART[:, (st.t0 + j) % 2, x, :].rearrange("p (k n) -> p k n", k=KB) for x in range(2)]

            def pe(p):
                wait_done(p, after)
                with p.Fori(0, gu.tiles // 4) as it:
                    for j in range(4):
                        hi, lo = St.tile(p, j, gu, j, it)
                        wait_pair(p, gu, j, it, 4)
                        for k in range(KB):
                            if j == 0:
                                p.wait_ge(x_lo, x0 + k + 1)
                            for q, (w, x) in enumerate(((hi, 0), (hi, 1), (lo, 0))):
                                mm = nc.tensor.matmul(PS[:, 2 * pair(gu, j), :], w[:, k, :], XPART[:, x, k, :],
                                                      start=(k + q == 0), stop=(k == KB - 1 and q == 2))
                        mm.then_inc(w_done[slot(gu, j)], 1)
                with p.Fori(0, 2) as it:
                    for n in range(4):
                        for c, ks in enumerate(pieces):
                            j = 3 * n + c
                            hi, lo = St.tile(p, gu.tiles + j, down, j, it)
                            if c == 0:
                                wait_pair(p, down, n, it, 4)
                            if n == 0:
                                p.wait_ge(hid, hid0 + 2 + ks[-1] + 1)
                            for k in ks:
                                for q, (w, x) in enumerate(((hi, 0), (hi, 1), (lo, 0))):
                                    mm = nc.tensor.matmul(PS[:, 2 * pair(down, n), :], w[:, k % KB, :],
                                                          HPART[:, x, k, :], start=(k + q == 0),
                                                          stop=(k == FB - 1 and q == 2))
                            mm.then_inc(w_done[slot(down, j)], 1)

            def act(a, link):
                wait_done(a, after)

                def round_tile(j, it, tiles):
                    g = gu.t0 + j
                    a.wait_ge(w_full[g % RING], span(16 * (g // RING + 1), it, 16 * tiles // RING))
                    a.wait_ge(w_done[(g - 2) % RING], span((g - 2) // RING + 1, it, tiles // RING))
                    nc.scalar.activation(WPART[:, g % 2, 0, :], WR[:, (g % RING) * TILE:(g % RING + 1) * TILE],
                                         ACT.Identity).then_inc(w_hi, 1)

                def silu(j, it):
                    nc.scalar.activation(SGH[(j // 2) % 2], PS[:, 2 * pair(gu, j), :],
                                         ACT.Silu).then_inc(evicted[pair(gu, j)], 1)

                for j in range(4):
                    round_tile(j, 0, 0)
                    if j == 2:
                        silu(0, 0)
                with a.Fori(0, gu.tiles // 4 - 1) as it:
                    for j in range(4, 8):
                        round_tile(j, it, 4)
                        if j % 2 == 0:
                            silu(j - 2, it)
                round_tile(gu.tiles, 0, 0)
                silu(gu.tiles - 2, 0)
                for j in range(gu.tiles + 1, gu.tiles + 4):
                    round_tile(j, 0, 0)
                with a.Fori(0, down.tiles // 4 - 1) as it:
                    for j in range(gu.tiles + 4, gu.tiles + 8):
                        round_tile(j, it, 4)

            def pool(g, link):
                wait_done(g, after)
                with g.Fori(0, (gu.tiles + down.tiles) // 4) as it:
                    for j in range(4):
                        g.wait_ge(w_hi, span(w0 + j + 1, it, 4))
                        q, s = (gu.t0 + j) % 2, slot(gu, j)
                        nc.gpsimd.tensor_tensor(WPART[:, q, 1, :], WR[:, s * TILE:(s + 1) * TILE],
                                                WPART[:, q, 0, :].bitcast(F32),
                                                ALU.subtract).then_inc(w_lo, 1)

            def dve(v, link):
                wait_done(v, after)
                def split_input(half, x0):
                    for k in range(KB + 1):
                        if k < KB:
                            nc.vector.tensor_copy(XPART[:, 0, k, :], XT[:, k, half * H:(half + 1) * H]).then_inc(x_hi, 1)
                        if k:
                            v.wait_ge(x_hi, x0 + k)
                            nc.vector.tensor_tensor(XPART[:, 1, k - 1, :], XT[:, k - 1, half * H:(half + 1) * H],
                                                    XPART[:, 0, k - 1, :].bitcast(F32), ALU.subtract).then_inc(x_lo, 1)

                def gate(b, it):
                    j = 2 * b + 1
                    wait_sums(v, gu, j, it, 4)
                    v.wait_ge(evicted[pair(gu, j - 1)], span((gu.n0 + j - 1) // 2 + 1, it, 2))
                    u = PS[:, 2 * pair(gu, j), :]
                    blk = bass.ds(span(b, it, 2), 1)
                    nc.vector.tensor_tensor(HPART[:, 0, blk, :].rearrange("p a t -> p (a t)"), u, SGH[b], ALU.mult)
                    v.wait_ge(hid, span(hid0 + 2 + b - 1, it, 2))
                    nc.vector.tensor_tensor(HIDF[b], u, SGH[b], ALU.mult).then_inc(evicted[pair(gu, j)], 1)
                    v.wait_ge(evicted[pair(gu, j)], span((gu.n0 + j) // 2 + 1, it, 2))
                    nc.vector.tensor_tensor(HPART[:, 1, blk, :].rearrange("p a t -> p (a t)"), HIDF[b],
                                            HPART[:, 0, blk, :].rearrange("p a t -> p (a t)").bitcast(F32),
                                            ALU.subtract).then_inc(hid, 1)

                if half == 0:
                    split_input(0, x0)
                for b in range(2):
                    nc.vector.memset(HIDF[b], 0.0).then_inc(hid, 1)
                with v.Fori(0, FB // 2) as it:
                    for b in range(2):
                        gate(b, it)
                if half == 0:
                    split_input(1, x0 + KB)
                with v.Fori(0, 2) as it:
                    for n in range(4):
                        wait_sums(v, down, 3 * n + 2, it, 12)
                        x = XT_[:, bass.ds(span(n * T + half * H, it, 4 * T), H)]
                        nc.vector.scalar_tensor_tensor(x, x, ALPHA, PS[:, 2 * pair(down, n), :], ALU.mult,
                                                       ALU.add).then_inc(evicted[pair(down, n)], 1)

        S.append(St)
        return St.done

    def ffn(i, after):
        for half in range(2):
            after = ffn_half(i, half, [] if half else after)
        return norm_stage("ln_f%d" % i, "layer", XT, XT, T, LN_EPS, lambda k: vec("ln_ffn_g", 8 * i + k),
                          lambda k: vec("ln_ffn_b", 8 * i + k), after)

    ffn0_done = ffn(0, done)

    SBD = 64
    n_pairs, PPT = D // P, 4
    QS = [ar(i * T, T) for i in range(2)]
    KS = [ar(2 * T + i * T, T) for i in range(2)]
    VS = [ar(4 * T + i * T, T, "p (b n) -> p b n", b=8) for i in range(2)]
    RZ, RE, RP = 6, 3, 4
    ZS = [ar(6144 + i * H, H) for i in range(RZ)]
    EL = [ar(9216 + i * H, H) for i in range(RE)]
    PP = [ar(10752 + i * H, H) for i in range(RP)]
    TRI = ar(12800, 3 * P, "p (i n) -> p i n", i=3)
    INCL, STRICT, CAP = TRI[:, 0], TRI[:, 1], TRI[:, 2]
    UN = [(half, j, hd) for half in (1, 0) for j in range(4 * half + 3, -1, -1) for hd in range(2)]
    NU = len(UN)
    BU = NU * PPT
    tri_in = sem("tri_in")
    sb_lin, sb_linv = sem("sb_lin"), sem("sb_linv")
    sb_z, sb_zs, sb_ab, sb_l, sb_p = (sem("sb_" + x) for x in ("z", "zs", "ab", "l", "p"))
    sb_t1, sb_tt, sb_t2, sb_w, sb_pv, sb_o = (sem("sb_" + x) for x in ("t1", "tt", "t2", "w", "pv", "o"))

    def unit(u):
        half, j, hd = UN[u % NU]
        lo = max(P * j - H * half, 0)
        return half, j, hd, H - lo, lo

    def diagonal(u):
        half, j = UN[u % NU][:2]
        return j >= 4 * half

    class Stick(Stage):
        name = "qkv"
        st = PLAN["qkv"]
        after = ffn0_done
        done = [(sb_o, 2 * n_pairs), (sb_linv, 3 * n_pairs), (sb_w, BU * 2)]

        def portion(p, it, pp, i, part):
            st, j = Stick.st, 3 * pp + i
            s = slot(st, j)
            if part == 0:
                wait_tile(p, st, j, it, 3 * PPT)
                if j:
                    p.wait_ge(sb_linv, span(j, it, 3 * PPT))
            if i < 2:
                for h in range(2):
                    mm = nc.tensor.matmul(PS[:, h, :], W[:, s, part, :], XT[:, part, h * H:(h + 1) * H],
                                          start=(part == 0), stop=(part == 7), skip_group_check=True)
            else:
                for k in range(KB):
                    mm = nc.tensor.matmul(PS[:, part // 4, (part % 4) * P:(part % 4 + 1) * P],
                                          XT[:, k, part * P:(part + 1) * P], W[:, s, k, :],
                                          start=(k == 0), stop=(k == KB - 1), skip_group_check=True)
            if part == 7:
                mm.then_inc(w_done[s], 1)

        def pe(p):
            wait_done(p, Stick.after)
            p.wait_ge(tri_in, 16)
            with p.Fori(0, 2) as it:
                v_ = lambda n: span(n, it, BU)
                p.wait_ge(sb_trip, span(1, it, 1))
                for i in range(3):
                    for part in range(8):
                        Stick.portion(p, it, 0, i, part)
                for s in range(BU + 4):
                    pp = s // NU
                    if s < BU:
                        half, j, hd, w, lo = unit(s)
                        if s % NU == 0:
                            p.wait_ge(sb_linv, span(3 * (pp + 1), it, 3 * PPT))
                        if s >= 3:
                            p.wait_ge(sb_zs, v_(s - 2))
                        a = half * H + lo
                        nc.tensor.matmul(PS[:, 2 + s % 3, 0:w], KS[pp % 2][SBD * hd:SBD * hd + SBD, j * P:(j + 1) * P],
                                         QS[pp % 2][SBD * hd:SBD * hd + SBD, a:a + w],
                                         start=True, stop=True).then_inc(sb_z, 1)
                    if 2 <= s < BU + 2:
                        u = s - 2
                        half, j, hd, w, lo = unit(u)
                        first = j == 4 * half + 3
                        p.wait_ge(sb_p, v_(u + 1))
                        nc.tensor.matmul(PS[:, 5 + hd, lo:H], INCL, PP[u % RP][:, 0:w], start=first, stop=True,
                                         skip_group_check=True).then_inc(sb_t1, 1)
                    if 3 <= s < BU + 3:
                        u = s - 3
                        half, j, hd, w, lo = unit(u)
                        p.wait_ge(sb_tt, v_(u + 1))
                        nc.tensor.matmul(PS[:, 5 + hd, lo:H], STRICT, PP[u % RP][:, 0:w], start=False, stop=True,
                                         skip_group_check=True).then_inc(sb_t2, 1)
                    if s >= 4:
                        u = s - 4
                        half, j, hd, w, lo = unit(u)
                        first = j == 4 * half + 3
                        p.wait_ge(sb_w, v_(u + 1))
                        if first and hd == 0:
                            n = 2 * (u // NU) + (1 - half)
                            if n:
                                p.wait_ge(sb_o, span(n, it, 2 * PPT))
                        nc.tensor.matmul(PS[SBD * hd:SBD * hd + SBD, 7, lo:H],
                                         VS[(u // NU) % 2][:, j, SBD * hd:SBD * hd + SBD], ZS[u % RZ][:, 0:w],
                                         start=first, stop=True, skip_group_check=True).then_inc(sb_pv, 1)
                    if s < BU and pp + 1 < PPT:
                        Stick.portion(p, it, pp + 1, (s % NU) // 8, s % 8)

        def act(a, link):
            wait_done(a, Stick.after)
            with a.Fori(0, 2) as it:
                v_ = lambda n: span(n, it, BU)
                link.enter(it, BU)
                a.wait_ge(sb_trip, span(1, it, 1))

                def linear(pp, i):
                    if i == 2:
                        return
                    j = 3 * pp + i
                    wait_sums(a, Stick.st, j, it, 3 * PPT)
                    if pp >= 2:
                        a.wait_ge(sb_z, v_((pp - 1) * NU))
                    nc.scalar.activation((QS, KS)[i][pp % 2], bank2(0), ACT.Identity,
                                         scale=SBD ** -0.5 if i == 0 else 1.0).then_inc(sb_linv, 1)

                linear(0, 0)
                linear(0, 1)
                for s in range(BU + 3):
                    if s < BU:
                        w = unit(s)[3]
                        a.wait_ge(sb_z, v_(s + 1))
                        if s >= RZ:
                            a.wait_ge(sb_pv, v_(s - RZ + 1))
                        nc.scalar.activation(ZS[s % RZ][:, 0:w], PS[:, 2 + s % 3, 0:w], ACT.Identity).then_inc(sb_zs, 1)
                    if 1 <= s < BU + 1:
                        u = s - 1
                        w = unit(u)[3]
                        a.wait_ge(sb_ab, v_(u + 1))
                        e = EL[u % RE][:, 0:w]
                        link(nc.scalar.activation(e, e, ACT.Exp))
                        nc.scalar.activation(e, e, ACT.Ln, bias=1.0).then_inc(sb_l, 1)
                    if s >= 3:
                        u = s - 3
                        w = unit(u)[3]
                        a.wait_ge(sb_tt, v_(u + 1))
                        z = ZS[u % RZ][:, 0:w]
                        nc.scalar.activation(z, z, ACT.Exp).then_inc(sb_w, 1)
                    if s < BU and s // NU + 1 < PPT and s % 8 == 7:
                        linear(s // NU + 1, (s % NU) // 8)
                link.leave(2)

        def dve(v, link):
            wait_done(v, Stick.after)
            nc.vector.memset(FLAG[:, 0:1], 0.0).then_inc(sb_trip, 1)
            with v.Fori(0, 2) as it:
                v_ = lambda n: span(n, it, BU)

                def linear_v(pp):
                    wait_sums(v, Stick.st, 3 * pp + 2, it, 3 * PPT)
                    if pp >= 2:
                        v.wait_ge(sb_pv, v_((pp - 1) * NU))
                    nc.vector.tensor_copy(VS[pp % 2].rearrange("p b n -> p (b n)"), bank2(0)).then_inc(sb_linv, 1)

                def output(u):
                    v.wait_ge(sb_pv, v_(u + 1))
                    half, pp = unit(u)[0], u // NU
                    at_ = span(pp * T + half * H, it, PPT * T)
                    nc.vector.tensor_copy(HT_[:, bass.ds(at_, H)], PS[:, 7, :]).then_inc(sb_o, 1)

                v.wait_ge(sb_trip, span(1, it, 1))
                linear_v(0)
                for s in range(BU + 6):
                    if s < BU:
                        w = unit(s)[3]
                        v.wait_ge(sb_zs, v_(s + 1))
                        if s >= RE:
                            v.wait_ge(sb_p, v_(s - RE + 1))
                        z = ZS[s % RZ][:, 0:w]
                        nc.vector.scalar_tensor_tensor(EL[s % RE][:, 0:w], z, -1.0, z, ALU.mult,
                                                       ALU.min).then_inc(sb_ab, 1)
                    if 1 <= s < BU + 1:
                        u = s - 1
                        w = unit(u)[3]
                        pb = PP[u % RP]
                        v.wait_ge(sb_l, v_(u + 1))
                        if u >= RP:
                            v.wait_ge(sb_t2, v_(u - RP + 1))
                        i_ = nc.vector.scalar_tensor_tensor(pb[:, 0:w], ZS[u % RZ][:, 0:w], 0.0, EL[u % RE][:, 0:w],
                                                            ALU.max, ALU.add)
                        if diagonal(u):
                            i_.then_inc(sb_pd, 1)
                            n_diag = sum(diagonal(x) for x in range(u + 1))
                            v.wait_ge(sb_pd, span(n_diag, it, N_DIAG))
                            i_ = nc.vector.tensor_tensor(pb[:, 0:P], pb[:, 0:P], STRICT, ALU.mult)
                        i_.then_inc(sb_p, 1)
                    if 2 <= s < BU + 2:
                        u = s - 2
                        half, j, hd, w, lo = unit(u)
                        z = ZS[u % RZ]
                        v.wait_ge(sb_t1, v_(u + 1))
                        i_ = nc.vector.tensor_tensor(z[:, 0:w], z[:, 0:w], PS[:, 5 + hd, lo:H], ALU.subtract)
                        if diagonal(u):
                            i_.then_inc(sb_td, 1)
                            n_diag = sum(diagonal(x) for x in range(u + 1))
                            v.wait_ge(sb_td, span(n_diag, it, N_DIAG))
                            i_ = nc.vector.tensor_tensor(z[:, 0:P], z[:, 0:P], CAP, ALU.min)
                        i_.then_inc(sb_tt, 1)
                    if s < BU and s // NU + 1 < PPT and s % NU == NU - 1:
                        linear_v(s // NU + 1)
                    if s >= 5 and s - 5 < BU and (unit(s - 5)[1], unit(s - 5)[2]) == (0, 1):
                        output(s - 5)
                v.wait_ge(sb_o, span(2 * PPT, it, 2 * PPT))
                nc.vector.memset(FLAG[:, 0:1], 0.0).then_inc(sb_trip, 1)

        def pool(g, link):
            wait_done(g, Stick.after)
            g.dma_start(TRI, ins["tri"].rearrange("i p n -> p i n")).then_inc(tri_in, 16)

    sb_trip = sem("sb_trip")
    sb_pd, sb_td = sem("sb_p_diag"), sem("sb_t_diag")
    N_DIAG = sum(diagonal(u) for u in range(BU))
    S.append(Stick)

    done = residual_linear("sb_out", HT, Stick.done, keep=ALPHA)
    done = norm_stage("ln1", "layer", XT, XT, T, LN_EPS, lambda k: vec("ln_mix_g", 8 + k),
                      lambda k: vec("ln_mix_b", 8 + k), done)
    done = ffn(1, done)

    out_done = sem("out_done")

    stages = S if stop is None else S[:[s.name for s in S].index(stop) + 1]
    runs = []
    for st in (PLAN[n] for n in PLAN if n in [s.name for s in stages] or n in [s.also for s in stages]):
        if runs and runs[-1][1] == st.t0 and runs[-1][2] + st.t0 - runs[-1][0] == st.dram:
            runs[-1][1] = st.t0 + st.tiles
        else:
            runs.append([st.t0, st.t0 + st.tiles, st.dram])

    block = ctx.enter_context(nc.Block())

    @block.sync
    def _(sp):
        Setup.sp(sp)
        EvIn.sp(sp)
        for s in range(RING):
            sp.dma_start(W[:, s], ins["weights"][s].rearrange("p (k n) -> p k n", k=KB)).then_inc(w_full[s], 16)
        for t0, t1, dram in runs:
            with sp.Fori(1 if t0 == 0 else 0, (t1 - t0) // RING) as it:
                for s in range(RING):
                    sp.wait_ge(w_done[s], it if t0 == 0 else span(t0 // RING, it, 1))
                    sp.dma_start(W[:, s], ins["weights"][bass.ds(span(dram + s, it, RING), 1)]
                                 .rearrange("a p (k n) -> p (a k) n", k=KB)).then_inc(w_full[s], 16)
        wait_done(sp, stages[-1].done)
        sp.dma_start(out.rearrange("(k p) t -> p k t", p=P), XT).then_inc(out_done, 16)
        sp.wait_ge(out_done, 16)

    @block.tensor
    def _(pe):
        for s in stages:
            if s.pe is not None:
                s.pe(pe)

    @block.scalar
    def _(act):
        link = Link(act, "act")
        for s in stages:
            if s.act is not None:
                s.act(act, link)

    @block.vector
    def _(dve):
        link = Link(dve, "dve")
        for s in stages:
            if s.dve is not None:
                s.dve(dve, link)

    @block.gpsimd
    def _(pool):
        link = Link(pool, "pool")
        for s in stages:
            if s.pool is not None:
                s.pool(pool, link)


def tiles_of(w):
    k, n = w.shape
    kb = k // P
    t = w.reshape(kb, P, n // P, P).transpose(2, 1, 0, 3)
    pieces = []
    for a in range(0, kb, KB):
        piece = np.zeros((n // P, P, KB, P), np.float32)
        piece[:, :, :min(KB, kb - a)] = t[:, :, a:a + KB]
        pieces.append(piece.reshape(n // P, P, TILE))
    return np.stack(pieces, 1)


def pack_weights(x):
    out = [tiles_of(x["w_mod"][i])[:, 0] for i in range(2)]
    ev = tiles_of(x["ev_w_in"][0])[:, 0]
    out.append(ev[[0, 1, 2, 3, 10, 11, 10, 11, 12, 13, 12, 13, 4, 5, 6, 7, 8, 9, 14, 15, 16, 17, 18, 19]])
    out.append(tiles_of(x["ev_w_out"][0])[:, 0])
    od = tiles_of(x["od_w_in"][0])[:, 0]
    out.append(od[24:28])
    for c in range(3):
        out.append(od[[g + 2 * c + i for g in (0, 6, 12, 18) for i in range(2)]])
    out.append(tiles_of(x["od_w_out"][0])[:, 0])
    glu = tiles_of(x["ssm_w_glu_2"][0])[:, 0]
    out.append(glu[[i // 2 + 8 * (i % 2) for i in range(16)]])
    out.append(tiles_of(x["ssm_w_out_2"][0])[:, 0])

    def ffn(i):
        gu = tiles_of(x["ffn_w_gu_2"][i])[:, 0]
        return [gu[[n // 2 + FB * (n % 2) for n in range(2 * FB)]],
                tiles_of(x["ffn_w_down_2"][i]).reshape(-1, P, TILE)]

    out += ffn(0)
    qkv = tiles_of(x["sb_w_qkv_2"][0])[:, 0]
    out.append(qkv[[n for pr in range(8) for n in (pr, 8 + pr, 16 + pr)]])
    out.append(tiles_of(x["sb_w_o_2"][0])[:, 0])
    out += ffn(1)
    return np.concatenate([o.reshape(-1, P, TILE) for o in out])


def pack_vectors(x):
    cols = {
        "cond": np.stack([x["c"][0], x["c_ctx"]], 1).reshape(KB, P, 2).transpose(1, 0, 2).reshape(P, 16),
        "conv_w": x["hy_conv_w"][0].reshape(3, 18, P).transpose(2, 1, 0).reshape(P, 54),
    }
    plain = {"b_mod": x["b_mod"], "norm_g": x["norm_g"], "pool_scale": x["pool_scale"], "q_g": x["q_norm_g"],
             "k_g": x["k_norm_g"], "conv_b": x["hy_conv_b"], "final_g": x["final_g"], "ssm_d": x["ssm_d_2"],
             "ln_mix_g": x["ln_mix_g_2"], "ln_mix_b": x["ln_mix_b_2"], "ln_ffn_g": x["ln_ffn_g_2"],
             "ln_ffn_b": x["ln_ffn_b_2"]}
    for name, a in plain.items():
        cols[name] = a.reshape(-1, P).T
    for name in ("hy_b1", "hy_b2", "hy_freq"):
        col = np.zeros((P, 1), np.float32)
        col[0:64, 0] = x[name][0]
        cols[name] = col
    return np.concatenate([cols[name] for name in VECS], 1)


def shape_tables():
    t = np.arange(T)
    inv_freq = 10000.0 ** (-np.arange(32) / 32)
    p = np.arange(P)
    pos = np.where((p // 64)[:, None] == 0, (t // 64)[None], (t % 64)[None])
    ang = pos * inv_freq[p % 32][:, None]
    swap = np.zeros((P, P))
    for m in range(P):
        if (m // 32) % 2 == 0:
            swap[m + 32, m] = -1.0
        else:
            swap[m - 32, m] = 1.0
    inv = np.zeros((2, P, T))
    for g, w in enumerate((2, 4, 8, 16)):
        cnt = np.clip(t + w // 2, 0, T) - np.clip(t - w // 2, 0, T)
        inv[g // 2, (g % 2) * 64:(g % 2) * 64 + 64] = 1.0 / cnt
    return {"rope": np.stack([np.cos(ang), np.sin(ang)]), "rope_swap": swap, "invcnt": inv, "ident": np.eye(P)}


def pack(inputs):
    x = {k: np.asarray(v) for k, v in inputs.items()}
    arrays = {k: np.ascontiguousarray(v, np.float32) for k, v in shape_tables().items()}
    arrays["xT"] = np.ascontiguousarray(x["x"][0].T)
    arrays["ctxT"] = np.ascontiguousarray(x["ctx"][0].T)
    arrays["weights"] = pack_weights(x)
    arrays["vecs"] = np.ascontiguousarray(pack_vectors(x))
    pool_w = np.zeros((2, P, P), np.float32)
    for g in range(4):
        lo = (g % 2) * 64
        pool_w[g // 2, lo:lo + 64, lo:lo + 64] = x["pool_w"][0, g]
    arrays["pool_w"] = pool_w
    more_arrays(x, arrays)
    return arrays


def more_arrays(x, arrays):
    f32 = np.float32
    arrays["hy_w1"] = np.ascontiguousarray(x["hy_w1"][0])
    arrays["hy_w2"] = np.ascontiguousarray(x["hy_w2"][0])
    arrays["hy_w3"] = np.ascontiguousarray(
        x["hy_w3"][0].reshape(64, 2, 2, 3, 256).transpose(3, 1, 0, 2, 4).reshape(6, 64, 512))
    arrays["fn_w"] = np.ascontiguousarray(x["fn_w"][0])
    deltas = np.abs(np.linspace(np.log(1e-2) / 1.5, np.log(1e-2) / 0.3, HYW))
    rows = np.concatenate([deltas.astype(f32).reshape(1, 3, 256), x["hy_skip"][0].reshape(2, 3, 256)])
    arrays["hy_rows"] = np.ascontiguousarray(
        np.broadcast_to(rows.transpose(1, 0, 2).reshape(3, 1, 768), (3, P, 768)))
    lin = np.linspace(0.0, 1.0, T)
    w = 2 * np.pi * np.arange(T) / T
    f = np.linspace(1e-4, 15, 16)
    ang = f[:, None] * w[None]
    arrays["hy_emb"] = np.concatenate([lin[None], np.cos(ang), -np.sin(ang)]).astype(f32)
    tok = np.arange(8)[None] // 4 + 2 * ((np.arange(8)[None] % 4) * P + np.arange(P)[:, None])
    first = np.ones((P, 1))
    first[0] = 0.0
    alt = 1.0 - 2.0 * (np.arange(P)[:, None] % 2)
    arrays["hy_cols"] = np.concatenate([-lin[tok], first, -first, alt], 1).astype(f32)
    u, m = np.arange(H)[:, None], np.arange(H)[None]
    even, odd = 2 * np.pi * (m + 0.5) * (2 * u) / 2048, 2 * np.pi * (m + 0.5) * (2 * u + 1) / 2048
    arrays["hy_dft"] = np.stack([np.cos(even), np.cos(odd), np.sin(even), np.sin(odd),
                                 np.cos(even).T, np.sin(even).T]).astype(f32)
    st = np.outer(np.arange(T), np.arange(H)) % T
    arrays["fn_seq"] = np.stack([np.cos(2 * np.pi * st / T), np.sin(2 * np.pi * st / T)]).astype(f32)
    cc = np.outer(np.arange(256), np.arange(256)) % 256
    arrays["fn_ch"] = (np.stack([np.cos(2 * np.pi * cc / 256), np.sin(2 * np.pi * cc / 256)]) / 512).astype(f32)
    yet_more(x, arrays)


def yet_more(x, arrays):
    def by_state(a):
        a = a.reshape((32, 2, 64) + a.shape[2:])
        return np.moveaxis(a, 0, 2).reshape((P, 32) + a.shape[3:])

    a_re, a_im = by_state(x["ssm_a_re_2"][0]), by_state(x["ssm_a_im_2"][0])
    ldt = by_state(np.repeat(x["ssm_log_dt_2"][0][:, None], 64, 1))
    arrays["s5_par"] = np.ascontiguousarray(np.stack([a_re, a_im, ldt], 1).reshape(P, 96))
    b = [by_state(x[n][0]) for n in ("ssm_b_re_2", "ssm_b_im_2")]
    c = [by_state(x[n][0].transpose(0, 2, 1)) for n in ("ssm_c_re_2", "ssm_c_im_2")]
    arrays["s5_bc"] = np.ascontiguousarray(np.stack(b + c, 1).reshape(P, 2048))
    r, s = np.arange(P)[:, None], np.arange(P)[None]
    arrays["tri"] = np.stack([r >= s, r < s, np.where(r < s, 3e38, -1e30)]).astype(np.float32)


def kernel(**inputs):
    import concourse.bacc as _bacc
    from concourse.bass_utils import run_bass_kernel_spmd as _run

    arrays = pack(inputs)
    nc = _bacc.Bacc("TRN2", target_bir_lowering=False, num_devices=1)
    ins = {n: nc.dram_tensor("in_" + n, a.shape, F32, kind="ExternalInput").ap() for n, a in arrays.items()}
    out = nc.dram_tensor("out", (D, T), F32, kind="ExternalOutput").ap()
    build(nc, ins, out)
    r = _run(nc, [{"in_" + n: a for n, a in arrays.items()}], core_ids=[0])
    return np.ascontiguousarray(r.results[0]["out"].T).reshape(1, T, D)
```

```python
from contextlib import ExitStack

import numpy as np

import concourse.bass as bass
from concourse import mybir

F32 = mybir.dt.float32
F32R = mybir.dt.float32r
ALU = mybir.AluOpType
ACT = mybir.ActivationFunctionType
AX_X = mybir.AxisListType.X

P = 128
D = 1024
T = 1024
H = 512
KB = D // P
CTX = 256
N_HEADS, N_KV, HD = 6, 2, 128
POOLW = 256
KEYS = CTX + T
HYW = 768
FFN = 2816
FB = FFN // P
RING = 4
TILE = KB * P
RMS_EPS, LN_EPS = 1e-6, 1e-5
ALPHA = (2 * 2) ** 0.25
SCALE0 = HD ** -0.5
TWO_PI = 2 * np.pi


class Linear:

    def __init__(self, name, t0, tiles, n0, dram):
        self.name, self.t0, self.tiles, self.n0, self.dram = name, t0, tiles, n0, dram


def plan():
    stages, t, n, dram = {}, 0, 0, 0
    for name, tiles, outs in (
        ("mod", 24, 0),
        ("ev_in", 24, 24),
        ("ev_out", 32, 8),
        ("fn_in", 4, 4),
        ("od_in", 24, 24),
        ("od_out", 8, 8),
        ("glu", 16, 16),
        ("s5_out", 8, 8),
        ("gu0a", 44, 44),
        ("down0a", 24, 8),
        ("gu0b", 44, 44),
        ("down0b", 24, 8),
        ("qkv", 24, 0),
        ("sb_out", 8, 8),
        ("gu1a", 44, 44),
        ("down1a", 24, 8),
        ("gu1b", 44, 44),
        ("down1b", 24, 8),
    ):
        if name.endswith("b"):
            stages[name] = Linear(name, t, tiles, n, stages[name[:-1] + "a"].dram)
        else:
            stages[name] = Linear(name, t, tiles, n, dram)
            dram += tiles
        t += tiles
        n += outs
    return stages


PLAN = plan()

VECS = {}
for _name, _n in (("cond", 16), ("b_mod", 48), ("norm_g", 16), ("pool_scale", 2), ("q_g", 1), ("k_g", 1),
                  ("conv_w", 54), ("conv_b", 18), ("hy_b1", 1), ("hy_b2", 1), ("hy_freq", 1), ("final_g", 8),
                  ("ssm_d", 8), ("ln_mix_g", 16), ("ln_mix_b", 16), ("ln_ffn_g", 16), ("ln_ffn_b", 16)):
    VECS[_name] = (sum(n for _, n in VECS.values()), _n)
N_VECS = sum(n for _, n in VECS.values())


class Stage:
    pe = act = dve = pool = also = None


def span(base, it, step):
    return it * step + base if step else base


def build(nc, ins, out, stop=None):
    ctx = ExitStack()
    with ctx:
        _build(nc, ctx, ins, out, stop)


def _build(nc, ctx, ins, out, stop):
    def sb(name, words):
        return ctx.enter_context(nc.sbuf_tensor(name, [P, words], F32))

    def sem(name):
        return ctx.enter_context(nc.semaphore(name))

    XT_ = sb("resid", KB * T)
    WR = sb("w_ring", RING * TILE)
    with ExitStack() as first_use:
        HT_ = first_use.enter_context(nc.sbuf_tensor("hidden", [P, KB * T], F32))
        AR = first_use.enter_context(nc.sbuf_tensor("arena", [P, 29184], F32))
    with ExitStack() as second_use:
        def parts(name, shape):
            return second_use.enter_context(nc.sbuf_tensor(name, [P] + shape, F32R))
        PTB = parts("parts_b", [2, KB, T])
        WP = parts("w_parts", [2, 2, TILE])
        parts("not_used", [H])
        PTA = parts("parts_a", [2, KB, T])
    HHI = ctx.enter_context(nc.sbuf_tensor("hidden_high", [P, FB, H], F32R))
    XHI = ctx.enter_context(nc.sbuf_tensor("x_high", [P, KB, H], F32R))
    GATE = sb("gate_temps", 2 * H)
    sb("w_parts_place", 4 * TILE)
    HLO = ctx.enter_context(nc.sbuf_tensor("hidden_low", [P, FB, H], F32R))
    XLO = ctx.enter_context(nc.sbuf_tensor("x_low", [P, KB, H], F32R))
    HIDF = sb("hidden_temps", 3 * H)
    RINV = sb("rinv", T)
    SQ = sb("squares", 2 * H)
    IDENT = sb("ident", P)
    ONES = sb("ones", P)
    VEC = sb("vectors", N_VECS)
    MOD = sb("mods", 96)
    PS = ctx.enter_context(nc.psum_tensor("banks", [P, 8, H], F32))

    def ar(at, words, pattern=None, **kw):
        v = AR[:, at:at + words]
        return v.rearrange(pattern, **kw) if pattern else v

    def three(t, blocks, width):
        return t[:, 0:blocks * width].rearrange("p (k t) -> p k t", k=blocks)

    XT, HT = three(XT_, KB, T), three(HT_, KB, T)
    W = WR[:, :].rearrange("p (s k n) -> p s k n", s=RING, k=KB)

    def vec(name, i=0, n=1):
        c = VECS[name][0] + i
        return VEC[:, c:c + n]

    def bank2(pair):
        return PS[:, 2 * pair:2 * pair + 2, :].rearrange("p b t -> p (b t)")

    w_full = [sem(f"w_full{s}") for s in range(RING)]
    w_done = [sem(f"w_done{s}") for s in range(RING)]
    evicted = [sem(f"evicted{p}") for p in range(2)]
    link_s = {k: sem(f"link_{k}") for k in ("act", "dve", "pool")}

    class Link:

        def __init__(self, eng, key):
            self.eng, self.sem, self.n, self.it, self.per = eng, link_s[key], 0, None, 0

        def __call__(self, ins):
            ins.then_inc(self.sem, 1)
            self.n += 1
            self.eng.wait_ge(self.sem, self.n if self.it is None else span(self.n, self.it, self.per))

        def enter(self, it, per):
            self.it, self.per, self.at = it, per, self.n

        def leave(self, trips):
            assert self.n - self.at == self.per, (self.n - self.at, self.per)
            self.n = self.at + trips * self.per
            self.it = None

    def slot(st, j):
        return (st.t0 + j) % RING

    def loads(st, j):
        return (st.t0 + j) // RING + 1

    def wait_tile(eng, st, j, it=None, tiles=0):
        eng.wait_ge(w_full[slot(st, j)], span(16 * loads(st, j), it, 16 * tiles // RING) if it is not None
                    else 16 * loads(st, j))

    def wait_sums(eng, st, j, it=None, tiles=0):
        eng.wait_ge(w_done[slot(st, j)], span(loads(st, j), it, tiles // RING) if it is not None
                    else loads(st, j))

    def wait_pair(eng, st, n, it=None, outs=0):
        used = (st.n0 + n) // 2
        if it is not None:
            eng.wait_ge(evicted[(st.n0 + n) % 2], span(used, it, outs // 2))
        elif used:
            eng.wait_ge(evicted[(st.n0 + n) % 2], used)

    def pair(st, n):
        return (st.n0 + n) % 2

    def wait_done(eng, done):
        for s, v in done:
            eng.wait_ge(s, v)

    def pairs_done(st, outs):
        return [(evicted[p], (st.n0 + outs + 1 - p) // 2) for p in range(2)]

    G0 = PLAN["glu"].t0
    w_hi, w_lo = sem("w_hi"), sem("w_lo")

    def round_ahead(a, st, j, it=None, tiles=0):
        g = st.t0 + j + 2
        if g - 2 >= G0:
            wait_sums(a, st, j, it, tiles)
        a.wait_ge(w_full[g % RING], span(16 * (g // RING + 1), it, 16 * tiles // RING))
        nc.scalar.activation(WP[:, g % 2, 0, :], WR[:, (g % RING) * TILE:(g % RING + 1) * TILE],
                             ACT.Identity).then_inc(w_hi, 1)

    def split_tile(p, st, j, bank, srcs, at, width, it=None, tiles=0, ks=range(KB), first=True, last=True,
                   block=None):
        p.wait_ge(w_lo, span(st.t0 + j - G0 + 1, it, tiles))
        w = [WP[:, (st.t0 + j) % 2, x, :].rearrange("p (k n) -> p k n", k=KB) for x in range(2)]
        for i, k in enumerate(ks):
            if block is not None:
                block(k)
            for h in range(0, width, H):
                for q, (a, b) in enumerate(((0, 0), (0, 1), (1, 0))):
                    mm = nc.tensor.matmul(PS[:, bank + h // H, :], w[a][:, k % KB, :],
                                          srcs[b][:, k, at + h:at + h + H],
                                          start=(first and i + q == 0), stop=(last and k == ks[-1] and q == 2))
        mm.then_inc(w_done[slot(st, j)], 1)

    def matmul_tile(pe, st, j, n, src, it=None, tiles=0, outs=0, width=T, between=None):
        wait_tile(pe, st, j, it, tiles)
        wait_pair(pe, st, n, it, outs)
        s, b = slot(st, j), 2 * pair(st, n)
        for k in range(KB):
            for h in range(0, width, H):
                w = min(H, width - h)
                mm = nc.tensor.matmul(PS[:, b + h // H, 0:w], W[:, s, k, :], src[:, k, h:h + w],
                                      start=(k == 0), stop=(k == KB - 1))
            if between is not None:
                between(k)
        mm.then_inc(w_done[s], 1)

    S = []


    n_sem = {key: sem("n_" + key) for key in ("sq_ready", "sq_free", "stat", "mean_in", "centred", "root",
                                              "scaled", "shifted")}
    n_count = dict.fromkeys(n_sem, 0)

    NORMS = {}

    def norm_stage(name, kind, src, dst, tokens, eps, gain, shift, after, scratch=0, rinv=None,
                   early=None, summed=0):
        rinv = RINV if rinv is None else rinv
        first = after if early is None else early[0]
        base = dict(n_count)
        segs = [(i, min(H, tokens - i)) for i in range(0, tokens, H)]
        layer = kind == "layer"
        uses = {"sq_ready": KB, "sq_free": KB, "stat": layer, "mean_in": layer, "centred": KB * layer,
                "root": 1, "scaled": KB, "shifted": KB * (shift is not None)}
        for key, per_seg in uses.items():
            n_count[key] += len(segs) * per_seg

        def wait(eng, key, n):
            eng.wait_ge(n_sem[key], base[key] + n)

        class St(Stage):
            between = None

        NORMS[name] = St
        St.done = [(n_sem[key], n_count[key]) for key in ("shifted", "root", "scaled") if uses[key]]

        def mean_block(k):
            for i, (a, w) in enumerate(segs):
                mm = nc.tensor.matmul(PS[:, 4 + i, 0:w], ONES[:, :], src[:, k, a:a + w],
                                      start=(k == 0), stop=(k == KB - 1))
                if k == KB - 1:
                    mm.then_inc(n_sem["mean_in"], 1)

        St.mean_block = mean_block

        def pe(pe_):
            wait_done(pe_, first)
            if layer:
                for k in range(summed, KB):
                    mean_block(k)
            for i, (a, w) in enumerate(segs):
                for k in range(KB):
                    j = i * KB + k
                    wait(pe_, "sq_ready", j + 1)
                    mm = nc.tensor.matmul(PS[:, 6 + i, 0:w], ONES[:, :], SQ[:, (j % 2) * H:(j % 2) * H + w],
                                          start=(k == 0), stop=(k == KB - 1))
                    mm.then_inc(n_sem["sq_free"], 1)

        def root(a_, i):
            a, w = segs[i]
            wait(a_, "sq_free", (i + 1) * KB)
            nc.scalar.activation(rinv[:, a:a + w], PS[:, 6 + i, 0:w], ACT.Sqrt, scale=1.0 / D,
                                 bias=EPS(eps)).then_inc(n_sem["root"], 1)

        def act_stats(a_, link):
            wait_done(a_, first)
            if layer:
                for i, (a, w) in enumerate(segs):
                    wait(a_, "mean_in", i + 1)
                    nc.scalar.activation(AR[:, scratch + a:scratch + a + w], PS[:, 4 + i, 0:w], ACT.Identity,
                                         scale=1.0 / D).then_inc(n_sem["stat"], 1)
            for i, (a, w) in enumerate(segs):
                for k in range(KB):
                    j = i * KB + k
                    if layer:
                        wait(a_, "centred", j + 1)
                    if j >= 2:
                        wait(a_, "sq_free", j - 1)
                    nc.scalar.activation(SQ[:, (j % 2) * H:(j % 2) * H + w], src[:, k, a:a + w],
                                         ACT.Square).then_inc(n_sem["sq_ready"], 1)
                    if j == KB + 1:
                        root(a_, 0)
            if len(segs) == 1:
                root(a_, 0)

        def act_shift(a_, link):
            if early is not None:
                wait_done(a_, after)
            for i, (a, w) in enumerate(segs):
                if shift is not None:
                    for k in range(KB):
                        wait(a_, "scaled", i * KB + k + 1)
                        nc.scalar.activation(dst[:, k, a:a + w], dst[:, k, a:a + w], ACT.Identity,
                                             bias=shift(k)).then_inc(n_sem["shifted"], 1)

        def dve(v_, link):
            wait_done(v_, after)
            if layer:
                for i, (a, w) in enumerate(segs):
                    wait(v_, "stat", i + 1)
                    for k in range(KB):
                        nc.vector.tensor_tensor(src[:, k, a:a + w], src[:, k, a:a + w],
                                                AR[:, scratch + a:scratch + a + w],
                                                ALU.subtract).then_inc(n_sem["centred"], 1)
            for i, (a, w) in enumerate(segs):
                if early is None:
                    reciprocal(v_, link, i)
                for k in range(KB):
                    nc.vector.scalar_tensor_tensor(dst[:, k, a:a + w], src[:, k, a:a + w], gain(k),
                                                   rinv[:, a:a + w], ALU.mult, ALU.mult).then_inc(n_sem["scaled"], 1)
                if i == 0 and St.between is not None:
                    St.between(v_, wait)

        def reciprocal(v_, link, i):
            a, w = segs[i]
            wait(v_, "root", i + 1)
            link(nc.vector.reciprocal(rinv[:, a:a + w], rinv[:, a:a + w]))

        def dve_stats(v_, link):
            for i in range(len(segs)):
                reciprocal(v_, link, i)

        def act_all_stats(a_, link):
            act_stats(a_, link)
            if len(segs) == 2:
                root(a_, 1)

        def act(a_, link):
            act_stats(a_, link)
            if len(segs) == 2:
                root(a_, 1)
            act_shift(a_, link)

        if early is not None:
            early.append((pe, act_all_stats, dve_stats))
            St.act, St.dve = act_shift, dve
        else:
            St.pe, St.act, St.dve = pe, act, dve
        St.name = name
        S.append(St)
        return St.done

    EPSV = sb("eps", 2)

    def EPS(e):
        return EPSV[:, 0:1] if e == RMS_EPS else EPSV[:, 1:2]

    vec_in, x_in, ctx_in, tab_in = sem("vec_in"), sem("x_in"), sem("ctx_in"), sem("tab_in")
    consts = sem("consts")
    cond_ready, mod_ready, mod_done = sem("cond_ready"), sem("mod_ready"), sem("mod_done")
    A_AV, A_AG, A_Q, A_K, A_BG, A_V = 0, 2080, 4128, 10272, 12832, 18976
    A_S0 = 21536
    CT = ar(A_Q, KB * CTX, "p (k t) -> p k t", k=KB)
    COS, SIN = ar(A_S0, T), ar(A_S0 + T, T)
    QN, RT = A_S0 + 2 * T, A_S0 + 2 * T + 2 * H
    CTN = ar(A_S0 + 2 * T + 4 * H, KB * CTX, "p (k t) -> p k t", k=KB)
    INVCNT = ar(A_BG, 2 * T, "p (b t) -> p b t", b=2)
    PA, PB = A_BG + 2 * T, A_BG + 2 * T + 1040
    AV = ar(A_AV, 2080, "p (b t) -> p b t", b=2)
    AG = ar(A_AG, 2 * T, "p (b t) -> p b t", b=2)

    class Setup(Stage):
        name = "mod"
        st = PLAN["mod"]
        done = [(mod_done, 2)]

        def sp(s):
            s.dma_start(VEC[:, :], ins["vecs"]).then_inc(vec_in, 16)

        def loads(s):
            s.dma_start(CT, ins["ctxT"].rearrange("(k p) t -> p k t", p=P)).then_inc(ctx_in, 16)
            s.dma_start(XT, ins["xT"].rearrange("(k p) t -> p k t", p=P)).then_inc(x_in, 16)
            s.dma_start(COS, ins["rope"][0]).then_inc(tab_in, 16)
            s.dma_start(SIN, ins["rope"][1]).then_inc(tab_in, 16)
            s.dma_start(INVCNT, ins["invcnt"].rearrange("b p t -> p b t")).then_inc(tab_in, 16)
            s.dma_start(IDENT[:, :], ins["ident"]).then_inc(tab_in, 16)

        def act(a, link):
            Setup.loads(a)
            a.wait_ge(vec_in, 16)
            nc.scalar.activation(vec("cond", 0, 16), vec("cond", 0, 16), ACT.Silu).then_inc(cond_ready, 1)
            for early in (CTX_EARLY, X_EARLY):
                early[1][1](a, link)

        def pe(p):
            st = PLAN["mod"]
            p.wait_ge(cond_ready, 1)
            for a, b in ((0, 3), (3, 6)):
                with p.Fori(a, b) as it:
                    for j in range(4):
                        wait_tile(p, st, j, it, 4)
                        s = slot(st, j)
                        for k in range(KB):
                            mm = nc.tensor.matmul(PS[:, 4, bass.ds(it * 8 + 2 * j, 2)], W[:, s, k, :],
                                                  vec("cond", 2 * k, 2), start=(k == 0), stop=(k == KB - 1))
                        mm.then_inc(w_done[s], 1)
                if a == 0:
                    for early in (CTX_EARLY, X_EARLY):
                        early[1][0](p)

        def dve(v, link):
            nc.vector.memset(ONES[:, :], 1.0).then_inc(consts, 1)
            nc.vector.memset(EPSV[:, 0:1], RMS_EPS).then_inc(consts, 1)
            nc.vector.memset(EPSV[:, 1:2], LN_EPS).then_inc(consts, 1)
            for early in (CTX_EARLY, X_EARLY):
                early[1][2](v, link)
            for s in range(RING):
                v.wait_ge(w_done[s], 6)
            modulation(link, 0)
            v.wait_ge(tab_in, 64)
            v.wait_ge(x_in, 16)
            v.wait_ge(ctx_in, 16)
            nc.vector.memset(AR[:, A_AV:A_AV + 2080], 0.0).then_inc(mod_done, 1)

    S.append(Setup)

    def modulation(link, layer):
        m = MOD[:, 48 * layer:48 * layer + 48].rearrange("p (n c) -> p n c", c=2)
        link(nc.vector.tensor_tensor(m, PS[:, 4, 48 * layer:48 * layer + 48].rearrange("p (n c) -> p n c", c=2),
                                     vec("b_mod", 24 * layer, 24).unsqueeze(2).broadcast_to([P, 24, 2]), ALU.add))
        nc.vector.scalar_tensor_tensor(m[:, 8:16, :], m[:, 8:16, :], 1.0,
                                       vec("norm_g", 8 * layer, 8).unsqueeze(2).broadcast_to([P, 8, 2]),
                                       ALU.add, ALU.mult).then_inc(mod_done, 1)

    def mod(layer, what, k, c=0):
        i = 2 * (24 * layer + 8 * what + k) + c
        return MOD[:, i:i + 1]

    CTX_EARLY, X_EARLY = [[(ctx_in, 16), (consts, 3)]], [[(x_in, 16), (consts, 3)]]
    done = norm_stage("n_ctx", "rms", CT, CTN, CTX, RMS_EPS, lambda k: mod(0, 1, k, 1), lambda k: mod(0, 0, k, 1),
                      Setup.done, rinv=ar(A_AG, CTX), early=CTX_EARLY)
    h0_done = norm_stage("n_x0", "rms", XT, HT, T, RMS_EPS, lambda k: mod(0, 1, k), lambda k: mod(0, 0, k), done,
                         early=X_EARLY)

    ROT = sb("rope_swap", P)
    Q0, BG = ar(A_Q, 6 * T), ar(A_BG, 6 * T)
    K0 = ar(A_K, N_KV * KEYS, "p (h t) -> p h t", h=N_KV)
    V0 = ar(A_V, (KEYS // P) * N_KV * HD, "p (b n) -> p b n", b=KEYS // P)
    POOLW_T = ar(A_S0 + 6144, 2 * P, "p (b n) -> p b n", b=2)
    rot_in, pw_in = sem("rot_in"), sem("pw_in")
    e_sq, e_ss, e_root, e_qn = sem("e_sq"), sem("e_ss"), sem("e_root"), sem("e_qn")
    e_rot, e_rt, e_cos, e_head = sem("e_rot"), sem("e_rt"), sem("e_cos"), sem("e_head")
    pool_mix = sem("pool_mix")

    EV = ([("val", 0), ("val", 1), ("gate", 0), ("gate", 1), ("k", 0), ("k", 1), ("kctx", 0), ("kctx", 1),
           ("v", 0), ("v", 1), ("vctx", 0), ("vctx", 1)] + [("q", i) for i in range(6)]
          + [("bgate", i) for i in range(6)])
    SEGS = []
    for _j, (_kind, _i) in enumerate(EV):
        if _kind in ("k", "q"):
            SEGS += [(_j, 0, H, True), (_j, 1, H, True)]
        if _kind == "kctx":
            SEGS += [(_j, 0, CTX, False)]
    N_ROT = sum(s[3] for s in SEGS)

    def segs_of(j):
        out_ = []
        for g, (jj, h, w, r) in enumerate(SEGS):
            if jj == j:
                out_.append((g, sum(s[3] for s in SEGS[:g]), h, w, r))
        return out_

    def head_dst(kind, i, h, w):
        if kind == "q":
            return Q0[:, i * T + h * H:i * T + h * H + w]
        if kind == "k":
            return K0[:, i, CTX + h * H:CTX + h * H + w]
        return K0[:, i, 0:CTX]

    class EvIn(Stage):
        name = "ev_in"
        st = PLAN["ev_in"]
        after = h0_done
        done = pairs_done(PLAN["ev_in"], 24) + [(e_head, N_ROT), (pool_mix, 2), (e_qn, len(SEGS))]

        def sp(s):
            s.dma_start(ROT[:, :], ins["rope_swap"]).then_inc(rot_in, 16)
            s.dma_start(POOLW_T, ins["pool_w"].rearrange("b p n -> p b n")).then_inc(pw_in, 16)

        def pe(p):
            st = EvIn.st
            wait_done(p, EvIn.after)
            p.wait_ge(rot_in, 16)

            def heads(j):
                for g, _, h, w, _r in segs_of(j - 1):
                    p.wait_ge(e_sq, g + 1)
                    if g >= 2:
                        p.wait_ge(e_root, g - 1)
                    nc.tensor.matmul(PS[:, 4 + g % 2, 0:w], ONES[:, :], SQ[:, (g % 2) * H:(g % 2) * H + w],
                                     start=True, stop=True).then_inc(e_ss, 1)
                for g, r, h, w, rotated in segs_of(j - 2):
                    if rotated:
                        p.wait_ge(e_qn, g + 1)
                        if r >= 2:
                            p.wait_ge(e_rt, r - 1)
                        nc.tensor.matmul(PS[:, 6 + r % 2, 0:w], ROT[:, :],
                                         AR[:, QN + (r % 2) * H:QN + (r % 2) * H + w],
                                         start=True, stop=True).then_inc(e_rot, 1)

            for j, (kind, i) in enumerate(EV):
                src = CTN if kind in ("kctx", "vctx") else HT
                width = CTX if kind in ("kctx", "vctx") else T
                if kind in ("v", "vctx"):
                    wait_tile(p, st, j)
                    wait_pair(p, st, j)
                    s, b = slot(st, j), 2 * pair(st, j)
                    for tb in range(width // P):
                        for k in range(KB):
                            mm = nc.tensor.matmul(PS[:, b + tb // 4, (tb % 4) * P:(tb % 4 + 1) * P],
                                                  src[:, k, tb * P:(tb + 1) * P], W[:, s, k, :],
                                                  start=(k == 0), stop=(k == KB - 1))
                        if tb == 0:
                            heads(j)
                    mm.then_inc(w_done[s], 1)
                else:
                    matmul_tile(p, st, j, j, src, width=width, 
                                between=lambda k: heads(j) if k == 1 else None)
            assert all(not segs_of(j) for j in range(len(EV) - 2, len(EV)))

        def act(a, link):
            st = EvIn.st
            wait_done(a, EvIn.after)
            for j in range(len(EV)):
                kind, i = EV[j]
                wait_sums(a, st, j)
                pr = pair(st, j)
                ev = None
                if kind == "val":
                    ev = nc.scalar.activation(AV[:, i, 8:8 + T], bank2(pr), ACT.Identity)
                elif kind == "gate":
                    ev = nc.scalar.activation(AG[:, i, :], bank2(pr), ACT.Silu)
                elif kind == "v":
                    ev = nc.scalar.activation(V0[:, 2:10, i * HD:(i + 1) * HD],
                                              bank2(pr).rearrange("p (b n) -> p b n", n=HD), ACT.Identity)
                elif kind == "vctx":
                    ev = nc.scalar.activation(V0[:, 0:2, i * HD:(i + 1) * HD],
                                              bank2(pr)[:, 0:CTX].rearrange("p (b n) -> p b n", n=HD),
                                              ACT.Identity)
                elif kind == "bgate":
                    if i == 0:
                        a.wait_ge(pool_mix, 2)
                    ev = nc.scalar.activation(BG[:, i * T:(i + 1) * T], bank2(pr), ACT.Silu)
                if ev is not None:
                    ev.then_inc(evicted[pr], 1)
                for g, _, h, w, _r in segs_of(j):
                    if g >= 2:
                        a.wait_ge(e_ss, g - 1)
                    nc.scalar.activation(SQ[:, (g % 2) * H:(g % 2) * H + w], PS[:, 2 * pr + h, 0:w],
                                         ACT.Square).then_inc(e_sq, 1)
                for g, _, h, w, _r in segs_of(j):
                    a.wait_ge(e_ss, g + 1)
                    if g >= 2:
                        a.wait_ge(e_qn, g - 1)
                    nc.scalar.activation(RINV[:, (g % 2) * H:(g % 2) * H + w], PS[:, 4 + g % 2, 0:w], ACT.Sqrt,
                                         scale=1.0 / HD, bias=EPS(RMS_EPS)).then_inc(e_root, 1)

        def dve(v, link):
            st = EvIn.st
            wait_done(v, EvIn.after)
            for j in range(len(EV) + 2):
                ss = segs_of(j - 1)
                for n, (g, r, h, w, rotated) in enumerate(ss):
                    kind, i = EV[j - 1]
                    pr = pair(st, j - 1)
                    rv = RINV[:, (g % 2) * H:(g % 2) * H + w]
                    v.wait_ge(e_root, g + 1)
                    link(nc.vector.reciprocal(rv, rv))
                    gain = vec("q_g" if kind == "q" else "k_g")
                    if rotated and r >= 2:
                        v.wait_ge(e_rot, r - 1)
                        v.wait_ge(e_cos, r - 1)
                    dst = AR[:, QN + (r % 2) * H:QN + (r % 2) * H + w] if rotated else head_dst(kind, i, h, w)
                    nc.vector.scalar_tensor_tensor(dst, PS[:, 2 * pr + h, 0:w], gain, rv,
                                                   ALU.mult, ALU.mult).then_inc(e_qn, 1)
                    if n == len(ss) - 1:
                        v.wait_ge(e_qn, g + 1)
                        nc.vector.memset(FLAG[:, 0:1], 0.0).then_inc(evicted[pr], 1)
                for g, r, h, w, rotated in segs_of(j - 2):
                    if rotated:
                        kind, i = EV[j - 2]
                        v.wait_ge(e_rot, r + 1)
                        rt = AR[:, RT + (r % 2) * H:RT + (r % 2) * H + w]
                        if r >= 2:
                            v.wait_ge(e_head, r - 1)
                        nc.vector.tensor_tensor(rt, PS[:, 6 + r % 2, 0:w], SIN[:, h * H:h * H + w],
                                                ALU.mult).then_inc(e_rt, 1)
                        v.wait_ge(e_rt, r + 1)
                        v.wait_ge(e_cos, r + 1)
                        dst = head_dst(kind, i, h, w)
                        nc.vector.tensor_tensor(dst, dst, rt, ALU.add).then_inc(e_head, 1)

        def pool(g_, link):
            st = EvIn.st
            wait_done(g_, EvIn.after)
            g_.wait_ge(tab_in, 64)
            pa, pb = ar(PA, 1040), ar(PB, 1040)
            tt = nc.gpsimd.tensor_tensor
            for b in range(2):
                g_.wait_ge(evicted[pair(st, b)], (st.n0 + b) // 2 + 1)
                x = AV[:, b, :]
                link(tt(pa[:, 1:1040], x[:, 0:1039], x[:, 1:1040], ALU.add))
                link(tt(pb[:, 2:1039], pa[:, 1:1038], pa[:, 3:1040], ALU.add))
                if b == 1:
                    link(tt(pa[:, 4:1037], pb[:, 2:1035], pb[:, 6:1039], ALU.add))
                    link(tt(pb[:, 8:1032], pa[:, 4:1028], pa[:, 12:1036], ALU.add))
                for lo, s in ((0, pa), (64, pb)):
                    m = s[lo:lo + 64, 8:8 + T]
                    link(tt(m, m, INVCNT[lo:lo + 64, b, :], ALU.mult))
                    y = x[lo:lo + 64, 8:8 + T]
                    i_ = tt(y, m, y, ALU.subtract)
                    link(i_)
                nc.gpsimd.memset(FLAG[:, 1:2], 0.0).then_inc(pool_mix, 1)
            for g, (j, h, w, rotated) in enumerate(SEGS):
                if not rotated:
                    continue
                r = sum(s[3] for s in SEGS[:g])
                kind, i = EV[j]
                g_.wait_ge(e_qn, g + 1)
                nc.gpsimd.tensor_tensor(head_dst(kind, i, h, w), AR[:, QN + (r % 2) * H:QN + (r % 2) * H + w],
                                        COS[:, h * H:h * H + w], ALU.mult).then_inc(e_cos, 1)

    FLAG = sb("flags", 4)
    S.append(EvIn)

    MT = HT
    A_P, A_PT, A_QC = A_S0, A_S0 + 2 * KEYS, A_S0 + 4 * KEYS
    NEG, RS = sb("neg_max", 2), sb("row_sum", 2)
    a_qc, a_s, a_mx, a_neg, a_p, a_rs = (sem("a_" + x) for x in ("qc", "s", "mx", "neg", "p", "rs"))
    a_pn, a_t, a_pta, a_ptb, a_pv, a_o = (sem("a_" + x) for x in ("pn", "t", "pta", "ptb", "pv", "o"))
    pm, pme = sem("pool_mm"), sem("pool_out")
    UNITS = N_HEADS * (T // P)
    HALF_U = UNITS // N_KV

    def kv_of(u):
        return min(u, UNITS - 1) // HALF_U

    class Attention(Stage):
        name = "attention"
        after = EvIn.done
        done = [(a_o, UNITS), (pme, 4)]

        def cycles(eng, fn, link=None, per=0):
            def run(lo, hi, loop):
                if not loop:
                    for i in range(lo, hi):
                        fn(None, i)
                    return
                with eng.Fori(0, (hi - lo) // 2) as it:
                    if link:
                        link.enter(it, per)
                    fn(it, lo)
                    fn(it, lo + 1)
                if link:
                    link.leave((hi - lo) // 2)

            run(0, 4, False)
            run(4, 20, True)
            run(20, 28, False)
            run(28, 44, True)
            run(44, UNITS + 1, False)

        def pe(p):
            wait_done(p, Attention.after)
            p.wait_ge(pw_in, 16)
            p.wait_ge(tab_in, 64)
            for b in range(2):
                for h in range(2):
                    if b:
                        p.wait_ge(pme, h + 1)
                    nc.tensor.matmul(PS[:, 6 + h, :], POOLW_T[:, b, :], AV[:, b, 8 + h * H:8 + h * H + H],
                                     start=True, stop=True).then_inc(pm, 1)
            p.wait_ge(pme, 4)

            def scores(it, u):
                par, kv = u % 2, kv_of(u)
                p.wait_ge(a_qc, span(u + 1, it, 2) if it is not None else u + 1)
                if u >= 2:
                    p.wait_ge(a_pta, span(u - 1, it, 2) if it is not None else u - 1)
                    p.wait_ge(a_ptb, span(u - 1, it, 2) if it is not None else u - 1)
                q = AR[:, A_QC + par * P:A_QC + par * P + P]
                for c in range(0, KEYS, H):
                    w = min(H, KEYS - c)
                    mm = nc.tensor.matmul(PS[:, 3 * par + c // H, 0:w], q, K0[:, kv, c:c + w],
                                          start=True, stop=True)
                mm.then_inc(a_s, 1)

            def cycle(it, i):
                v_ = lambda n: span(n, it, 2) if it is not None else n
                par = i % 2
                if i < UNITS:
                    p.wait_ge(a_pn, v_(i + 1))
                    pw = A_P + par * KEYS
                    for b in range(KEYS // P):
                        mm = nc.tensor.transpose(PS[:, 3 * par + b // 4, (b % 4) * P:(b % 4 + 1) * P],
                                                 AR[:, pw + b * P:pw + (b + 1) * P], IDENT[:, :])
                    mm.then_inc(a_t, 1)
                if i >= 1:
                    q = (i - 1) % 2
                    p.wait_ge(a_pta, v_(i))
                    p.wait_ge(a_ptb, v_(i))
                    if i >= 3:
                        p.wait_ge(a_o, v_(i - 2))
                    for b in range(KEYS // P):
                        mm = nc.tensor.matmul(PS[:, 6 + q, 0:P],
                                              V0[:, b, kv_of(i - 1) * HD:(kv_of(i - 1) + 1) * HD],
                                              AR[:, A_PT + q * KEYS + b * P:A_PT + q * KEYS + (b + 1) * P],
                                              start=(b == 0), stop=(b == KEYS // P - 1))
                    mm.then_inc(a_pv, 1)
                if i + 2 < UNITS:
                    scores(it, i + 2)

            scores(None, 0)
            scores(None, 1)
            Attention.cycles(p, cycle)

        def act(a, link):
            wait_done(a, Attention.after)

            def softexp(it, u):
                par = u % 2
                v_ = lambda n: span(n, it, 2) if it is not None else n
                a.wait_ge(a_neg, v_(u + 1))
                if u >= 2:
                    a.wait_ge(a_t, v_(u - 1))
                nc.scalar.activation(AR[:, A_P + par * KEYS:A_P + (par + 1) * KEYS],
                                     PS[:, 3 * par:3 * par + 3, :].rearrange("p b t -> p (b t)")[:, 0:KEYS],
                                     ACT.Exp, bias=NEG[:, par:par + 1], scale=SCALE0,
                                     accum_out=RS[:, par:par + 1]).then_inc(a_p, 1)

            def cycle(it, i):
                par = i % 2
                v_ = lambda n: span(n, it, 2) if it is not None else n
                if i < UNITS:
                    a.wait_ge(a_t, v_(i + 1))
                    if i >= 2:
                        a.wait_ge(a_pv, v_(i - 1))
                    nc.scalar.activation(AR[:, A_PT + par * KEYS + H:A_PT + par * KEYS + 2 * H],
                                         PS[:, 3 * par + 1, :], ACT.Identity).then_inc(a_ptb, 1)
                if i + 2 < UNITS:
                    softexp(it, i + 2)

            softexp(None, 0)
            softexp(None, 1)
            Attention.cycles(a, cycle)

        def dve(v, link):
            wait_done(v, Attention.after)
            for b in range(2):
                for h in range(2):
                    v.wait_ge(pm, 2 * b + h + 1)
                    nc.vector.scalar_tensor_tensor(MT[:, b, h * H:(h + 1) * H], PS[:, 6 + h, :],
                                                   vec("pool_scale", b), AG[:, b, h * H:(h + 1) * H],
                                                   ALU.mult, ALU.mult).then_inc(pme, 1)

            def top(it, u):
                par = u % 2
                v_ = lambda n: span(n, it, 2) if it is not None else n
                v.wait_ge(a_s, v_(u + 1))
                if u >= 2:
                    v.wait_ge(a_p, v_(u - 1))
                sc = PS[:, 3 * par:3 * par + 3, :].rearrange("p b t -> p (b t)")[:, 0:KEYS]
                nc.vector.reduce_max(NEG[:, par:par + 1], sc, AX_X).then_inc(a_mx, 1)
                v.wait_ge(a_mx, v_(u + 1))
                nc.vector.tensor_scalar(NEG[:, par:par + 1], NEG[:, par:par + 1], -SCALE0, None,
                                        ALU.mult).then_inc(a_neg, 1)

            def normalise(it, u):
                par = u % 2
                v_ = lambda n: span(n, it, 2) if it is not None else n
                v.wait_ge(a_p, v_(u + 1))
                rs = RS[:, par:par + 1]
                nc.vector.reciprocal(rs, rs).then_inc(a_rs, 1)
                v.wait_ge(a_rs, v_(u + 1))
                pw = AR[:, A_P + par * KEYS:A_P + (par + 1) * KEYS]
                nc.vector.tensor_scalar(pw, pw, rs, None, ALU.mult).then_inc(a_pn, 1)

            def cycle(it, i):
                par = i % 2
                v_ = lambda n: span(n, it, 2) if it is not None else n
                if i < UNITS:
                    v.wait_ge(a_t, v_(i + 1))
                    if i >= 2:
                        v.wait_ge(a_pv, v_(i - 1))
                    pt = A_PT + par * KEYS
                    nc.vector.tensor_copy(AR[:, pt:pt + H], PS[:, 3 * par, :])
                    nc.vector.tensor_copy(AR[:, pt + 2 * H:pt + KEYS],
                                          PS[:, 3 * par + 2, 0:KEYS - 2 * H]).then_inc(a_pta, 1)
                if i >= 1:
                    q = (i - 1) % 2
                    v.wait_ge(a_pv, v_(i))
                    at = span((i - 1) * P, it, 2 * P) if it is not None else (i - 1) * P
                    nc.vector.tensor_tensor(HT_[:, bass.ds(at + 2 * T, P)], PS[:, 6 + q, 0:P],
                                            BG[:, bass.ds(at, P)], ALU.mult).then_inc(a_o, 1)
                if i + 1 < UNITS:
                    normalise(it, i + 1)
                if i + 2 < UNITS:
                    top(it, i + 2)

            top(None, 0)
            top(None, 1)
            normalise(None, 0)
            Attention.cycles(v, cycle)

        def pool(g, link):
            wait_done(g, Attention.after)

            def copy(it, u):
                v_ = lambda n: span(n, it, 2) if it is not None else n
                if u >= 2:
                    g.wait_ge(a_s, v_(u - 1))
                at = span(u * P, it, 2 * P) if it is not None else u * P
                nc.gpsimd.tensor_copy(AR[:, A_QC + (u % 2) * P:A_QC + (u % 2 + 1) * P],
                                      Q0[:, bass.ds(at, P)]).then_inc(a_qc, 1)

            copy(None, 0)
            copy(None, 1)
            with g.Fori(0, UNITS // 2 - 1) as it:
                copy(it, 2)
                copy(it, 3)

    S.append(Attention)

    class EvOut(Stage):
        name = "ev_out"
        st = PLAN["ev_out"]
        done = pairs_done(PLAN["ev_out"], 8) + [(mod_done, 3)]

        def pe(p):
            st = EvOut.st
            wait_done(p, Attention.done)

            def modulation_tile(n, i):
                j, c = 4 * n + i, 48 + 2 * (3 * n + i)
                wait_tile(p, st, j)
                for k in range(KB):
                    mm = nc.tensor.matmul(PS[:, 4, c:c + 2], W[:, slot(st, j), k, :], vec("cond", 2 * k, 2),
                                          start=(k == 0), stop=(k == KB - 1))
                mm.then_inc(w_done[slot(st, j)], 1)

            for n in range(8):
                for i in range(3):
                    modulation_tile(n, i)
                matmul_tile(p, st, 4 * n + 3, n, MT)
                if n in (4, 6):
                    HyPrep.products(p, n // 2 - 2)

        def act(a, link):
            wait_done(a, Attention.done)
            HyPrep.sines(a)

        def dve(v, link):
            st = EvOut.st
            wait_done(v, Attention.done)
            for n in range(8):
                wait_sums(v, st, 4 * n + 3)
                nc.vector.scalar_tensor_tensor(XT[:, n, :], bank2(pair(st, n)), mod(0, 2, n), XT[:, n, :],
                                               ALU.mult, ALU.add).then_inc(evicted[pair(st, n)], 1)
                if n in (4, 6):
                    HyPrep.angles(v, link, n // 2 - 2)
            modulation(link, 1)

    S.append(EvOut)
    done = EvOut.done

    spill = nc.dram_tensor("resid_spill", (D, T), F32, kind="Internal").ap().rearrange("(k p) t -> p k t", p=P)
    spilled, unspilled = sem("spilled"), sem("unspilled")
    ev_out_done = done
    h1_done = norm_stage("n_x1", "rms", XT, HT, T, RMS_EPS, lambda k: mod(1, 1, k), lambda k: mod(1, 0, k),
                         ev_out_done, rinv=ar(12800, T))

    B_Z, B_X1, B_X2, B_K, B_Y, B_TMP = 0, 2048, 4096, 6144, 10240, 14336
    B_COLS, B_INVN, B_TAB = 16386, 16397, 16896
    COLS = ar(B_COLS, 11)
    INVN = ar(B_INVN, 256)
    TAB = ar(B_TAB, 6 * 4 * H, "p (i b n) -> p i b n", i=6, b=4)
    FCE, FCO, FSE, FSO, ICE, ISE = (TAB[:, i] for i in range(6))
    W3S = sb("w3_slice", H)
    HDN = RINV
    CWSW = SQ[:, :].rearrange("p (m n) -> p m n", m=2)
    Z1 = ar(B_Z, 2048, "p (b c) -> p b c", b=8)
    XO = [ar(B_X1, 2048, "p (b c) -> p b c", b=8), ar(B_X2, 2048, "p (b c) -> p b c", b=8)]
    M1 = XT

    C1 = float(np.float32(6.28125))
    C2 = float(np.float32(TWO_PI - 6.28125))
    C3 = float(TWO_PI - 6.28125 - C2)
    ROUND = 1.5 * 2.0 ** 23
    PI_DOWN = float(np.nextafter(np.float32(np.pi), np.float32(0)))

    def reduce_angle(v, link, x, n):
        link(nc.vector.tensor_scalar(n, x, 1.0 / TWO_PI, ROUND, ALU.mult, ALU.add))
        link(nc.vector.tensor_scalar(n, n, -ROUND, None, ALU.add))
        for c in (C1, C2, C3):
            link(nc.vector.scalar_tensor_tensor(x, n, -c, x, ALU.mult, ALU.add))
        link(nc.vector.tensor_scalar(x, x, PI_DOWN, -PI_DOWN, ALU.min, ALU.max))

    mlp_in, hp_mm, hp_arg, hp_sin = sem("mlp_in"), sem("hp_mm"), sem("hp_arg"), sem("hp_sin")
    dft_in, seq_in, ch_in = sem("dft_in"), sem("seq_in"), sem("ch_in")
    E0 = 8192
    EMB, W1, W2 = AR[0:33, E0:E0 + T], AR[0:33, E0 + T:E0 + T + 64], AR[0:64, E0 + T + 64:E0 + T + 128]
    ANG, ROT_N = AR[0:64, E0 + T + 128:E0 + 2 * T + 128], AR[0:64, E0 + 2 * T + 128:E0 + 3 * T + 128]
    HDN1 = AR[0:64, E0 + 3 * T + 128:E0 + 4 * T + 128]

    class HyPrep(Stage):
        name = "hy_prep"
        done = [(hp_sin, 2)] + h1_done

        def pool(g, link):
            wait_done(g, Attention.done)
            g.dma_start(EMB, ins["hy_emb"]).then_inc(mlp_in, 16)
            g.dma_start(W1, ins["hy_w1"]).then_inc(mlp_in, 16)
            g.dma_start(W2, ins["hy_w2"]).then_inc(mlp_in, 16)
            g.dma_start(COLS, ins["hy_cols"]).then_inc(dft_in, 16)
            g.dma_start(ar(0, 8192, "p (i b t) -> p i b t", i=2, b=8),
                        ins["fn_seq"].rearrange("i (b p) t -> p i b t", p=P)).then_inc(seq_in, 16)
            for i in range(6):
                g.dma_start(TAB[:, i], ins["hy_dft"][i].rearrange("(b p) n -> p b n", p=P)).then_inc(dft_in, 16)
            wait_done(g, ev_out_done)
            g.dma_start(spill, XT).then_inc(spilled, 16)

        def products(p, i):
            p.wait_ge(mlp_in, 48)
            if i:
                p.wait_ge(hp_sin, 1)
            for h in range(2):
                nc.tensor.matmul(PS[0:64, 5 + h, :], (W1, W2)[i], (EMB, HDN1)[i][:, h * H:(h + 1) * H],
                                 start=True, stop=True).then_inc(hp_mm, 1)

        def angles(v, link, i):
            v.wait_ge(hp_mm, 2 * (i + 1))
            if i:
                v.wait_ge(hp_sin, 1)
            link(nc.vector.tensor_scalar(ANG, PS[0:64, 5:7, :].rearrange("p b t -> p (b t)"),
                                         vec("hy_b%d" % (i + 1))[0:64], vec("hy_freq")[0:64], ALU.add, ALU.mult))
            reduce_angle(v, link, ANG, ROT_N)
            nc.vector.memset(FLAG[:, 0:1], 0.0).then_inc(hp_arg, 1)

        def sines(a):
            for i, dst in enumerate((HDN1, HDN[0:64, :])):
                a.wait_ge(hp_arg, i + 1)
                nc.scalar.activation(dst, ANG, ACT.Sin).then_inc(hp_sin, 1)

    S.append(HyPrep)

    SEQ = ar(0, 8192, "p (i b t) -> p i b t", i=2, b=8)
    FAB = ar(8192, 4096, "p (b n) -> p b n", b=8)
    FIN, FGT = ar(12288, 2048, "p (k t) -> p k t", k=2), ar(14336, 2048, "p (k t) -> p k t", k=2)
    CH = ar(8192, 1024, "p (i k n) -> p i k n", i=2, k=2)
    FNW = ar(9216, 512, "p (k n) -> p k n", k=2)
    YS = ar(12288, 2048, "p (i t) -> p i t", i=4)
    f_cw, f_cwv, f_ab, f_aba, f_abd = (sem("f_" + x) for x in ("cw", "cwv", "ab", "aba", "abd"))
    f_y, f_ys, f_out = sem("f_y"), sem("f_ys"), sem("f_out")

    class Fourier(Stage):
        name = "fn_in"
        st = PLAN["fn_in"]
        done = pairs_done(PLAN["fn_in"], 4) + [(f_out, 2)]

        def pool(g, link):
            wait_done(g, HyPrep.done)
            g.dma_start(CH, ins["fn_ch"].rearrange("i (k p) n -> p i k n", p=P)).then_inc(ch_in, 16)
            g.dma_start(FNW, ins["fn_w"].rearrange("(k p) n -> p k n", p=P)).then_inc(ch_in, 16)

        def pe(p):
            st = Fourier.st
            wait_done(p, HyPrep.done)
            for n in range(4):
                matmul_tile(p, st, n, n, HT)
            p.wait_ge(ch_in, 32)
            for m in range(2):
                for i in range(2):
                    for k in range(2):
                        mm = nc.tensor.matmul(PS[:, 4 + m, i * 256:(i + 1) * 256], CH[:, i, k, m * P:(m + 1) * P],
                                              FNW[:, k, :], start=(k == 0), stop=(k == 1))
                mm.then_inc(f_cw, 1)
            p.wait_ge(f_cwv, 2)
            wait_done(p, pairs_done(st, 4))
            for b in range(8):
                if b >= 4:
                    p.wait_ge(f_aba if b % 2 else f_abd, (b - 4) // 2 + 1)
                for k in range(2):
                    mm = nc.tensor.matmul(PS[:, 4 + b % 4, :], FIN[:, k, b * P:(b + 1) * P], CWSW[:, k, :],
                                          start=(k == 0), stop=(k == 1))
                mm.then_inc(f_ab, 1)
            p.wait_ge(f_aba, 4)
            p.wait_ge(f_abd, 4)
            p.wait_ge(seq_in, 16)
            p.wait_ge(dft_in, 16 * 7)
            for i in range(2):
                for ty in range(2):
                    for b in range(8):
                        mm = nc.tensor.matmul(PS[:, 4 + 2 * i + ty, :], FAB[:, b, ty * 256 + i * P:ty * 256 + (i + 1) * P],
                                              SEQ[:, ty, b, :], start=(b == 0), stop=(b == 7))
                for b in range(8):
                    mm = nc.tensor.matmul(PS[:, i, 0:1], FAB[:, b, i * P:(i + 1) * P], COLS[:, 10:11],
                                          start=(b == 0), stop=(b == 7))
                mm.then_inc(f_y, 1)

        def act(a, link):
            st = Fourier.st
            wait_done(a, HyPrep.done)
            for n in range(4):
                wait_sums(a, st, n)
                dst = FIN[:, n, :] if n < 2 else FGT[:, n - 2, :]
                nc.scalar.activation(dst, bank2(pair(st, n)),
                                     ACT.Identity if n < 2 else ACT.Silu).then_inc(evicted[pair(st, n)], 1)
            for b in range(1, 8, 2):
                a.wait_ge(f_ab, b + 1)
                nc.scalar.activation(FAB[:, b, :], PS[:, 4 + b % 4, :], ACT.Identity).then_inc(f_aba, 1)
            for i in range(2):
                a.wait_ge(f_y, i + 1)
                nc.scalar.activation(YS[:, i, :], PS[:, 5 + 2 * i, :], ACT.Identity).then_inc(f_ys, 1)

        def dve(v, link):
            wait_done(v, HyPrep.done)
            for m in range(2):
                v.wait_ge(f_cw, m + 1)
                nc.vector.tensor_copy(CWSW[:, m, :], PS[:, 4 + m, :]).then_inc(f_cwv, 1)
            for b in range(0, 8, 2):
                v.wait_ge(f_ab, b + 1)
                nc.vector.tensor_copy(FAB[:, b, :], PS[:, 4 + b % 4, :]).then_inc(f_abd, 1)
            v.wait_ge(spilled, 16)
            for i in range(2):
                y, yc = M1[:, 6 + i, :], PS[:, 4 + 2 * i, :]
                v.wait_ge(f_ys, i + 1)
                link(nc.vector.tensor_tensor(y[:, 0:H], yc, YS[:, i, :], ALU.subtract))
                link(nc.vector.tensor_tensor(y[:, T - 1:H:-1], yc[:, 1:H], YS[:, i, 1:H], ALU.add))
                link(nc.vector.tensor_copy(y[:, H:H + 1], PS[:, i, 0:1]))
                nc.vector.tensor_tensor(y, y, FGT[:, i, :], ALU.mult).then_inc(f_out, 1)

    S.append(Fourier)

    rows_in, w3_in = sem("rows_in"), sem("w3_in")
    cv_out, tr, tok_a, tok_d = sem("cv_out"), sem("tr"), sem("tok_a"), sem("tok_d")
    g_h, g_dec, g_g, g_abs, g_sum, g_pm, g_inv = (sem("g_" + x) for x in ("h", "dec", "g", "abs", "sum", "pm", "inv"))
    k_t, k_c, k_d, z_t, z_c, z_d = (sem("fft_" + x) for x in ("kt", "kc", "kd", "zt", "zc", "zd"))
    i_t, i_skip, z_new = sem("inv_t"), sem("inv_skip"), sem("z_new")
    b_t, b_o, g_d = sem("back_t"), sem("back_o"), sem("gated")
    UC, SP_ = ar(B_TMP, T), ar(B_TMP + T, T + 2)
    TMP = [ar(B_TMP, T), ar(B_TMP + T, T)]
    G = [ar(B_K, H), ar(B_K + H, H)]
    GA = [ar(B_K + 2 * H, H), ar(B_K + 3 * H, H)]
    DEC = [ar(B_K + 4 * H, 256), ar(B_K + 4 * H + 256, 256)]
    DELTA, SKIP = SQ[:, 0:256], [SQ[:, 256:512], SQ[:, 512:768]]
    KF = ar(B_K, 4096, "p (i b c) -> p i b c", i=2, b=8)
    PM = ar(B_Y, 4096, "p (i b c) -> p i b c", i=2, b=8)
    YF = ar(B_Y, 4096, "p (b q) -> p b q", b=4)

    def tok_cols(t, tb):
        a = tb // 4 + 2 * P * (tb % 4)
        return t[:, a:a + 2 * P - 1:2]

    class Hyena(Stage):
        name = "od_in"
        st = PLAN["od_in"]
        done = pairs_done(PLAN["od_in"], 24) + [(g_d, 6)]

        def pool(g, link):
            wait_done(g, Fourier.done)
            for c in range(3):
                if c:
                    g.wait_ge(z_new, 8 * c)
                    g.wait_ge(i_skip, 2 * c)
                g.dma_start(SQ[:, 0:768], ins["hy_rows"][c]).then_inc(rows_in, 16)
                for o in range(2):
                    n = 2 * c + o
                    if n:
                        g.wait_ge(g_h, 8 * n)
                    g.dma_start(W3S[0:64, :], ins["hy_w3"][n]).then_inc(w3_in, 16)
                    g.wait_ge(z_t, 4 * (n + 1))
                    g.wait_ge(rows_in, 16 * (c + 1))
                    nc.gpsimd.tensor_tensor(Z1, Z1, SKIP[o].unsqueeze(1).broadcast_to([P, 8, 256]),
                                            ALU.mult).then_inc(i_skip, 1)

        def pe(p):
            st = Hyena.st
            wait_done(p, Fourier.done)
            for c in range(3):
                for i in range(7):
                    if i < 6:
                        matmul_tile(p, st, 8 * c + i, 8 * c + i, HT)
                    if i:
                        q = 6 * c + i - 1
                        p.wait_ge(cv_out, q + 1)
                        if q:
                            p.wait_ge(tok_a, q)
                            p.wait_ge(tok_d, q)
                        for tb in range(8):
                            mm = nc.tensor.transpose(PS[:, 4 + tb // 4, (tb % 4) * P:(tb % 4 + 1) * P],
                                                     tok_cols(UC, tb), IDENT[:, :])
                            if tb % 4 == 3:
                                mm.then_inc(tr, 1)
                for o in range(2):
                    n = 2 * c + o
                    p.wait_ge(w3_in, 16 * (n + 1))
                    if o == 0:
                        p.wait_ge(tok_a, 6 * c + 6)
                        p.wait_ge(tok_d, 6 * c + 6)
                    else:
                        p.wait_ge(z_new, 4 * n)
                    for tb in range(9):
                        g = 8 * n + tb
                        if tb < 8:
                            if tb >= 2:
                                p.wait_ge(g_g, g - 1)
                            nc.tensor.matmul(PS[:, 4 + tb % 2, :], tok_cols(HDN[0:64, :], tb), W3S[0:64, :],
                                             start=True, stop=True).then_inc(g_h, 1)
                        if tb:
                            p.wait_ge(g_abs, g)
                            nc.tensor.matmul(PS[:, 6, :], ONES[:, :], GA[(tb - 1) % 2], start=(tb == 1),
                                             stop=(tb == 8)).then_inc(g_sum, 1)
                    p.wait_ge(g_pm, 8 * (n + 1))
                    p.wait_ge(g_inv, n + 1)
                    for which, (cos_src, sin_src, done_s, copied) in enumerate(
                            ((PM[:, 0], PM[:, 1], k_t, k_c), (Z1, Z1, z_t, z_c))):
                        for mb in range(4):
                            q = 4 * n + mb
                            if mb >= 2:
                                p.wait_ge(copied, q - 1)
                            elif which:
                                p.wait_ge(k_c, 4 * n + 3 + mb)
                            for ty, src in ((0, cos_src), (1, sin_src)):
                                for par in range(2):
                                    tab = TAB[:, 2 * ty + par]
                                    for ub in range(4):
                                        mm = nc.tensor.matmul(
                                            PS[:, 4 + 2 * (mb % 2) + ty, par * 256:(par + 1) * 256],
                                            tab[:, ub, mb * P:(mb + 1) * P], src[:, 4 * par + ub, :],
                                            start=(ub == 0), stop=(ub == 3))
                            mm.then_inc(done_s, 1)
                    matmul_tile(p, st, 8 * c + 6 + o, 8 * c + 6 + o, HT)
                    p.wait_ge(z_d, 4 * (n + 1))
                    for tb in range(8):
                        par, ub = tb // 4, tb % 4
                        for ty in range(2):
                            tab = (ICE, ISE)[ty] if par == 0 else (FCO, FSO)[ty]
                            for mb in range(4):
                                part = 2 * ty + par
                                mm = nc.tensor.matmul(PS[:, 4 + tb // 2, (tb % 2) * 256:(tb % 2 + 1) * 256],
                                                      tab[:, mb, ub * P:(ub + 1) * P],
                                                      YF[:, mb, part * 256:(part + 1) * 256],
                                                      start=(ty == 0 and mb == 0), stop=(ty == 1 and mb == 3))
                        if tb % 2:
                            mm.then_inc(i_t, 1)
                p.wait_ge(z_new, 8 * (c + 1))
                for i in range(2):
                    for tb in range(8):
                        mm = nc.tensor.transpose(PS[:, 4 + 2 * i + tb // 4, (tb % 4) * P:(tb % 4 + 1) * P],
                                                 Z1[:, tb, i * P:(i + 1) * P], IDENT[:, :])
                        if tb % 4 == 3:
                            mm.then_inc(b_t, 1)
                p.wait_ge(b_o, 4 * (c + 1))

        def act(a, link):
            st = Hyena.st
            wait_done(a, Fourier.done)
            for c in range(3):
                if c:
                    a.wait_ge(g_d, 2 * c)
                for i in range(7):
                    if i < 6:
                        j, q = 8 * c + i, 6 * c + i
                        blk = (i // 2) * 6 + 2 * c + i % 2
                        wait_sums(a, st, j)
                        if i:
                            a.wait_ge(tr, 2 * q)
                        pr = pair(st, j)
                        nc.scalar.activation(UC, bank2(pr), ACT.Identity, scale=vec("conv_w", 3 * blk + 1),
                                             bias=vec("conv_b", blk))
                        if q:
                            a.wait_ge(cv_out, q)
                        nc.scalar.activation(SP_[:, 1:1 + T], bank2(pr), ACT.Identity).then_inc(evicted[pr], 1)
                    if i:
                        q, ii = 6 * c + i - 1, i - 1
                        dst = (Z1, XO[0], XO[1])[ii // 2]
                        a.wait_ge(tr, 2 * q + 1)
                        nc.scalar.activation(dst[:, 0:4, (ii % 2) * P:(ii % 2 + 1) * P],
                                             PS[:, 4, :].rearrange("p (b n) -> p b n", b=4),
                                             ACT.Identity).then_inc(tok_a, 1)
                a.wait_ge(rows_in, 16 * (c + 1))
                for o in range(2):
                    n = 2 * c + o
                    if n:
                        a.wait_ge(z_d, 4 * n)
                    for tb in range(9):
                        g = 8 * n + tb
                        if tb < 8:
                            if tb >= 2:
                                a.wait_ge(g_g, g - 1)
                            nc.scalar.activation(DEC[tb % 2], DELTA, ACT.Exp,
                                                 scale=COLS[:, tb:tb + 1]).then_inc(g_dec, 1)
                        if tb:
                            a.wait_ge(g_g, g)
                            if tb >= 3:
                                a.wait_ge(g_sum, g - 2)
                            nc.scalar.activation(GA[(tb - 1) % 2], G[(tb - 1) % 2], ACT.Abs).then_inc(g_abs, 1)
                    for made, copied, used in ((k_t, k_c, k_d), (z_t, z_c, z_d)):
                        for mb in range(4):
                            q = 4 * n + mb
                            a.wait_ge(made, q + 1)
                            if mb >= 2:
                                a.wait_ge(used, q - 1)
                            elif made is z_t:
                                a.wait_ge(k_d, 4 * n + 3 + mb)
                            b = 4 + 2 * (mb % 2)
                            nc.scalar.activation(TMP[mb % 2], PS[:, b:b + 2, :].rearrange("p b t -> p (b t)"),
                                                 ACT.Identity).then_inc(copied, 1)
                for q in range(4):
                    i, par = q // 2, q % 2
                    a.wait_ge(b_t, 4 * c + q + 1)
                    nc.scalar.activation(M1[:, 2 * c + i, par:T:2], PS[:, 4 + q, :],
                                         ACT.Identity).then_inc(b_o, 1)
                for i in range(2):
                    j = 8 * c + 6 + i
                    wait_sums(a, st, j)
                    nc.scalar.activation(TMP[i], bank2(pair(st, j)), ACT.Silu).then_inc(evicted[pair(st, j)], 1)

        def dve(v, link):
            st = Hyena.st
            wait_done(v, Fourier.done)
            tt, ts, stt = nc.vector.tensor_tensor, nc.vector.tensor_scalar, nc.vector.scalar_tensor_tensor
            for c in range(3):
                link(nc.vector.memset(SP_[:, 0:1], 0.0))
                link(nc.vector.memset(SP_[:, T + 1:T + 2], 0.0))
                for i in range(7):
                    if i < 6:
                        j, q = 8 * c + i, 6 * c + i
                        blk = (i // 2) * 6 + 2 * c + i % 2
                        pr = pair(st, j)
                        v.wait_ge(evicted[pr], (st.n0 + j) // 2 + 1)
                        link(stt(UC, SP_[:, 0:T], vec("conv_w", 3 * blk), UC, ALU.mult, ALU.add))
                        stt(UC, SP_[:, 2:T + 2], vec("conv_w", 3 * blk + 2), UC, ALU.mult,
                            ALU.add).then_inc(cv_out, 1)
                    if i:
                        q, ii = 6 * c + i - 1, i - 1
                        dst = (Z1, XO[0], XO[1])[ii // 2]
                        v.wait_ge(tr, 2 * q + 2)
                        nc.vector.tensor_copy(dst[:, 4:8, (ii % 2) * P:(ii % 2 + 1) * P],
                                              PS[:, 5, :].rearrange("p (b n) -> p b n", b=4)).then_inc(tok_d, 1)
                for o in range(2):
                    n = 2 * c + o
                    for tb in range(8):
                        g = 8 * n + tb
                        v.wait_ge(g_h, g + 1)
                        v.wait_ge(g_dec, g + 1)
                        if tb >= 2:
                            v.wait_ge(g_abs, g - 1)
                        gg = G[tb % 2]
                        tt(gg.rearrange("p (s c) -> p s c", s=2), PS[:, 4 + tb % 2, :].rearrange("p (s c) -> p s c", s=2),
                           DEC[tb % 2].unsqueeze(1).broadcast_to([P, 2, 256]), ALU.mult).then_inc(g_g, 1)
                        v.wait_ge(g_g, g + 1)
                        h0, h1 = gg[:, 0:256], gg[:, 256:512]
                        if tb == 0:
                            stt(PM[:, 0, tb, :], h1, COLS[:, 8:9], h0, ALU.mult, ALU.add)
                            stt(PM[:, 1, tb, :], h1, COLS[:, 9:10], h0, ALU.mult, ALU.add).then_inc(g_pm, 1)
                        else:
                            tt(PM[:, 0, tb, :], h0, h1, ALU.add)
                            tt(PM[:, 1, tb, :], h0, h1, ALU.subtract).then_inc(g_pm, 1)
                    v.wait_ge(g_sum, 8 * (n + 1))
                    link(nc.vector.tensor_copy(INVN, PS[:, 6, 0:256]))
                    link(tt(INVN, INVN, PS[:, 6, 256:512], ALU.add))
                    link(ts(INVN, INVN, 1e-6, float(T), ALU.add, ALU.mult))
                    nc.vector.reciprocal(INVN, INVN).then_inc(g_inv, 1)
                    for mb in range(4):
                        q = 4 * n + mb
                        t = TMP[mb % 2]
                        e, od, se, so = (t[:, k * 256:(k + 1) * 256] for k in range(4))
                        v.wait_ge(k_c, q + 1)
                        tt(KF[:, 0, mb, :], e, od, ALU.add)
                        tt(KF[:, 0, 4 + mb, :], e, od, ALU.subtract)
                        tt(KF[:, 1, mb, :], se, so, ALU.add)
                        tt(KF[:, 1, 4 + mb, :], so, se, ALU.subtract).then_inc(k_d, 1)
                    v.wait_ge(k_d, 4 * (n + 1))
                    for mb in range(4):
                        q = 4 * n + mb
                        t = TMP[mb % 2]
                        e, od, se, so = (t[:, k * 256:(k + 1) * 256] for k in range(4))
                        y = YF[:, mb, :]
                        v.wait_ge(z_c, q + 1)
                        tt(y[:, 0:256], e, od, ALU.add)
                        tt(y[:, 256:512], e, od, ALU.subtract)
                        tt(y[:, 512:768], se, so, ALU.add)
                        link(tt(y[:, 768:1024], so, se, ALU.subtract))
                        two = "p (b c) -> p b c"
                        zc, zs = y[:, 0:512].rearrange(two, b=2), y[:, 512:1024].rearrange(two, b=2)
                        lo, hi = t[:, 0:512].rearrange(two, b=2), t[:, 512:1024].rearrange(two, b=2)
                        kc, ks = KF[:, 0, mb:mb + 5:4, :], KF[:, 1, mb:mb + 5:4, :]
                        tt(lo, zc, kc, ALU.mult)
                        link(tt(hi, zs, ks, ALU.mult))
                        link(tt(lo, lo, hi, ALU.subtract))
                        tt(hi, zc, ks, ALU.mult)
                        link(tt(zs, zs, kc, ALU.mult))
                        link(tt(hi, hi, zs, ALU.add))
                        yr, yrm, yi, yim = (t[:, k * 256:(k + 1) * 256] for k in range(4))
                        tt(y[:, 0:256], yr, yrm, ALU.add)
                        tt(y[:, 256:512], yr, yrm, ALU.subtract)
                        tt(y[:, 512:768], yi, yim, ALU.subtract)
                        tt(y[:, 768:1024], yi, yim, ALU.add).then_inc(z_d, 1)
                    v.wait_ge(i_skip, n + 1)
                    v.wait_ge(z_d, 4 * (n + 1))
                    for b in range(4):
                        v.wait_ge(i_t, 4 * n + b + 1)
                        two = "p (b c) -> p b c"
                        t = TMP[b % 2][:, 0:512].rearrange(two, b=2)
                        link(tt(t, PS[:, 4 + b, :].rearrange(two, b=2),
                                INVN.unsqueeze(1).broadcast_to([P, 2, 256]), ALU.mult))
                        link(tt(t, t, Z1[:, 2 * b:2 * b + 2, :], ALU.add))
                        tt(Z1[:, 2 * b:2 * b + 2, :], t, XO[o][:, 2 * b:2 * b + 2, :], ALU.mult).then_inc(z_new, 1)
                for i in range(2):
                    j = 8 * c + 6 + i
                    v.wait_ge(evicted[pair(st, j)], (st.n0 + j) // 2 + 1)
                    v.wait_ge(b_o, 4 * c + 2 * i + 2)
                    m = M1[:, 2 * c + i, :]
                    tt(m, m, TMP[i], ALU.mult).then_inc(g_d, 1)
                v.wait_ge(g_d, 2 * (c + 1))

    S.append(Hyena)

    class OdOut(Stage):
        name = "od_out"
        st = PLAN["od_out"]
        done = pairs_done(PLAN["od_out"], 8)

        def pool(g, link):
            wait_done(g, Hyena.done)
            g.dma_start(HT, spill).then_inc(unspilled, 16)

        def pe(p):
            wait_done(p, Hyena.done)
            for n in range(8):
                matmul_tile(p, OdOut.st, n, n, M1)

        def dve(v, link):
            st = OdOut.st
            wait_done(v, Hyena.done)
            v.wait_ge(unspilled, 16)
            for n in range(8):
                wait_sums(v, st, n)
                nc.vector.scalar_tensor_tensor(HT[:, n, :], bank2(pair(st, n)), mod(1, 2, n), HT[:, n, :],
                                               ALU.mult, ALU.add).then_inc(evicted[pair(st, n)], 1)
                if n == 0:
                    S5Prep.reciprocal(v)

    S.append(OdOut)
    x2_done = norm_stage("n_first", "rms", HT, XT, T, RMS_EPS, lambda k: vec("final_g", k), None, OdOut.done)

    CK, NC = 8, T // 8
    NG, NP_, QP = 64, 32, 8
    u_dram = nc.dram_tensor("s5_in", (D, CK, NC), F32, kind="Internal").ap()
    y_dram = nc.dram_tensor("s5_out", (D, CK, NC), F32, kind="Internal").ap()
    at = [0]

    def take(words, pattern=None, **kw):
        at[0] += words
        assert at[0] <= 29184
        return ar(at[0] - words, words, pattern, **kw)

    PAR = take(96, "p (i j) -> p i j", i=3)
    SM = [take(32) for _ in range(24)]
    (DT, LRE, MAG, TH, TN, SH, S1, CO, LBR, LBI, NRE, DEN, CFR, CFI, TA, TB, M8, TC_) = SM[:18]
    BC = take(2048, "p (i j h) -> p i j h", i=4, j=NP_)
    BB = take(1024, "p (i j h) -> p i j h", i=2, j=NP_)
    PWR = take(2 * 9 * 32, "p (i n j) -> p i n j", i=2, n=9)
    WL = take(2 * 7 * 32, "p (i n j) -> p i n j", i=2, n=7)
    EPH = take(2048, "p (i j c) -> p i j c", i=2, j=QP)
    MAGC = RINV[:, :].rearrange("p (j c) -> p j c", j=QP)
    CLS = [take(2 * QP * 9 * 16, "p (i j n h) -> p i j n h", i=2, j=QP, n=9) for _ in range(2)]
    VB = take(2048, "p (i j s h) -> p i j s h", i=2, j=QP, s=CK)
    VBT = take(2048, "p (j i n) -> p j i n", j=QP, i=2)
    KM = take(16 * 240, "p (g n) -> p g n", g=16)
    TP = take(2048, "p (g n) -> p g n", g=16)
    RV = take(2048, "p (i j c) -> p i j c", i=2, j=QP)
    TV = take(2048, "p (i j c) -> p i j c", i=2, j=QP)
    STT_ = take(2 * QP * (NC + 1), "p (i j c) -> p i j c", i=2, j=QP)
    s5p_in, s5_exp, s5_ang, s5_sin, s5_ready = (sem("s5_" + x) for x in ("par", "exp", "ang", "sin", "ready"))
    s5_r, u_out, u_in, s5_zero = (sem("s5_" + x) for x in ("r", "u_out", "u_in", "zero"))
    s5_cl, s5_e, s5_vb, s5_k, s5_km, s5_tp = (sem("s5_" + x) for x in ("cl", "e", "vb", "k", "km", "tp"))
    s5_vt, s5_vbt, s5_v, s5_st, s5_y, s5_ye, y_out = (sem("s5_" + x) for x in
                                                     ("vt", "vbt", "v", "st", "y", "ye", "y_out"))
    y_out3 = sem("s5_y_out3")
    y_in3 = sem("s5_y_in3")
    s5_den = sem("s5_den")
    s5_vr = sem("s5_vr")
    s5_hi, s5_part = sem("s5_hi"), sem("s5_part")
    y_in, s5_d, s5_h = sem("s5_y_in"), sem("s5_d"), sem("s5_h")
    YT = ar(0, 8192, "p (k t c) -> p k t c", k=KB, t=CK)

    class S5Prep(Stage):
        name = "s5_prep"
        done = [(s5_ready, 1)]

        def reciprocal(v):
            v.wait_ge(s5_den, 1)
            nc.vector.reciprocal(DEN, DEN).then_inc(s5_den, 1)

        def powers_c(g, link, q):
            tt = nc.gpsimd.tensor_tensor
            j0 = q * QP
            sh = [P, QP, 9, 16]
            pw = [PWR[:, i, :, j0:j0 + QP].rearrange("p n j -> p j n").unsqueeze(3).broadcast_to(sh)
                  for i in range(2)]
            cc = [BC[:, 2 + i, j0:j0 + QP, :].unsqueeze(2).broadcast_to(sh) for i in range(2)]
            CL = CLS[q % 2]
            if q >= 2:
                g.wait_ge(s5_y, 4 * (q - 1))
            tmp = TCL.rearrange("p (j n h) -> p j n h", j=QP, n=9)
            link(tt(CL[:, 0], pw[0], cc[0], ALU.mult))
            link(tt(tmp, pw[1], cc[1], ALU.mult))
            link(tt(CL[:, 0], CL[:, 0], tmp, ALU.subtract))
            link(tt(CL[:, 1], pw[0], cc[1], ALU.mult))
            link(tt(tmp, pw[1], cc[0], ALU.mult))
            link(tt(CL[:, 1], CL[:, 1], tmp, ALU.add))
            nc.gpsimd.tensor_scalar(CL[:, 1], CL[:, 1], -1.0, None, ALU.mult).then_inc(s5_cl, 1)

        def phases(g, link, q):
            tt, j0 = nc.gpsimd.tensor_tensor, q * QP
            link(nc.gpsimd.memset(EPH[:, 0, :, 0:1], 1.0))
            link(nc.gpsimd.memset(EPH[:, 1, :, 0:1], 0.0))
            for n in range(7):
                k = 1 << n
                w = [WL[:, i, n, j0:j0 + QP].unsqueeze(2).broadcast_to([P, QP, k]) for i in range(2)]
                a, b = EPH[:, 0, :, 0:k], EPH[:, 1, :, 0:k]
                x, y = EPH[:, 0, :, k:2 * k], EPH[:, 1, :, k:2 * k]
                t = TCL[:, 0:QP * k].rearrange("p (j c) -> p j c", j=QP)
                link(tt(x, a, w[0], ALU.mult))
                link(tt(t, b, w[1], ALU.mult))
                link(tt(x, x, t, ALU.subtract))
                link(tt(y, a, w[1], ALU.mult))
                link(tt(t, b, w[0], ALU.mult))
                link(tt(y, y, t, ALU.add))

        def pool(g, link):
            tt, ts = nc.gpsimd.tensor_tensor, nc.gpsimd.tensor_scalar
            wait_done(g, Hyena.done)
            g.dma_start(PAR, ins["s5_par"].rearrange("p (i j) -> p i j", i=3)).then_inc(s5p_in, 16)
            g.dma_start(BC, ins["s5_bc"].rearrange("p (i j h) -> p i j h", i=4, j=NP_)).then_inc(s5p_in, 16)
            nc.gpsimd.memset(KM[0:16], 0.0).then_inc(s5_zero, 1)
            nc.gpsimd.memset(STT_, 0.0).then_inc(s5_zero, 1)
            g.wait_ge(s5p_in, 32)
            a_re, a_im = PAR[:, 0, :], PAR[:, 1, :]
            link(ts(LRE, a_re, -1e-4, None, ALU.min))
            link(tt(DEN, LRE, LRE, ALU.mult))
            link(tt(TB, a_im, a_im, ALU.mult))
            tt(DEN, DEN, TB, ALU.add).then_inc(s5_den, 1)
            g.wait_ge(s5_exp, 1)
            link(tt(TH, a_im, DT, ALU.mult))
            link(ts(TN, TH, 1.0 / TWO_PI, ROUND, ALU.mult, ALU.add))
            link(ts(TN, TN, -ROUND, None, ALU.add))
            for c in (C1, C2, C3):
                link(ts(TB, TN, -c, None, ALU.mult))
                link(tt(TH, TH, TB, ALU.add))
            link(ts(TH, TH, PI_DOWN, -PI_DOWN, ALU.min, ALU.max))
            tt(TA, LRE, DT, ALU.mult).then_inc(s5_ang, 1)
            g.wait_ge(s5_sin, 3)
            link(tt(CO, SH, SH, ALU.mult))
            link(ts(CO, CO, -2.0, 1.0, ALU.mult, ALU.add))
            link(tt(LBR, MAG, CO, ALU.mult))
            link(tt(LBI, MAG, S1, ALU.mult))
            link(ts(NRE, LBR, -1.0, None, ALU.add))
            link(tt(CFR, NRE, LRE, ALU.mult))
            link(tt(TB, LBI, a_im, ALU.mult))
            link(tt(CFR, CFR, TB, ALU.add))
            g.wait_ge(s5_den, 2)
            link(tt(CFR, CFR, DEN, ALU.mult))
            link(tt(CFI, LBI, LRE, ALU.mult))
            link(tt(TB, NRE, a_im, ALU.mult))
            link(tt(CFI, CFI, TB, ALU.subtract))
            link(tt(CFI, CFI, DEN, ALU.mult))

            def cmul(xr, xi, ar_, ai, br, bi, t):
                link(tt(t, ai, bi, ALU.mult))
                link(tt(xr, ar_, br, ALU.mult))
                link(tt(xr, xr, t, ALU.subtract))
                link(tt(t, ai, br, ALU.mult))
                link(tt(xi, ar_, bi, ALU.mult))
                link(tt(xi, xi, t, ALU.add))

            sh = [P, NP_, 16]
            tb = TV.rearrange("p i j c -> p (i j c)")[:, 0:512].rearrange("p (j h) -> p j h", j=NP_)
            cmul(BB[:, 0], BB[:, 1], CFR.unsqueeze(2).broadcast_to(sh), CFI.unsqueeze(2).broadcast_to(sh),
                 BC[:, 0], BC[:, 1], tb)
            link(nc.gpsimd.memset(PWR[:, 0, 0, :], 1.0))
            link(nc.gpsimd.memset(PWR[:, 1, 0, :], 0.0))
            link(nc.gpsimd.tensor_copy(PWR[:, 0, 1, :], LBR))
            link(nc.gpsimd.tensor_copy(PWR[:, 1, 1, :], LBI))
            for n in range(2, 9):
                cmul(PWR[:, 0, n, :], PWR[:, 1, n, :], PWR[:, 0, n - 1, :], PWR[:, 1, n - 1, :], LBR, LBI, TB)
            link(tt(M8, MAG, MAG, ALU.mult))
            link(tt(M8, M8, M8, ALU.mult))
            link(tt(M8, M8, M8, ALU.mult))
            cmul(TN, TC_, CO, S1, CO, S1, TB)
            cmul(TA, SH, TN, TC_, TN, TC_, TB)
            cmul(WL[:, 0, 0, :], WL[:, 1, 0, :], TA, SH, TA, SH, TB)
            for n in range(1, 7):
                r, i = WL[:, 0, n - 1, :], WL[:, 1, n - 1, :]
                cmul(WL[:, 0, n, :], WL[:, 1, n, :], r, i, r, i, TB)
            nc.gpsimd.memset(FLAG[:, 1:2], 0.0).then_inc(s5_ready, 1)
            S5Prep.powers_c(g, link, 0)
            S5Prep.phases(g, link, 0)

        def act(a, link):
            wait_done(a, Hyena.done)
            a.wait_ge(s5p_in, 32)
            nc.scalar.activation(DT, PAR[:, 2, :], ACT.Exp).then_inc(s5_exp, 1)
            a.wait_ge(s5_ang, 1)
            nc.scalar.activation(MAG, TA, ACT.Exp).then_inc(s5_sin, 1)
            nc.scalar.activation(SH, TH, ACT.Sin, scale=0.5).then_inc(s5_sin, 1)
            nc.scalar.activation(S1, TH, ACT.Sin).then_inc(s5_sin, 1)

    TCL = take(QP * 9 * 16)
    S.insert(S.index(OdOut) + 1, S5Prep)

    class S5(Stage):
        name = "s5"
        done = [(s5_part, KB)]

        def pool(g, link):
            tt = nc.gpsimd.tensor_tensor
            wait_done(g, x2_done)
            for q in range(4):
                if q:
                    S5Prep.powers_c(g, link, q)
                    g.wait_ge(s5_st, q)
                    S5Prep.phases(g, link, q)
                j0 = q * QP
                link(nc.gpsimd.tensor_copy(MAGC, M8[:, j0:j0 + QP].unsqueeze(2).broadcast_to([P, QP, NC])))
                nc.gpsimd.memset(MAGC[:, :, 0:1], 0.0).then_inc(s5_e, 1)
            wait_done(g, [(s5_st, 4), (s5_v, 4), (s5_k, 16)])
            for a, b, s_, v_, back in ((0, 6, y_out, 16 * CK * 3, y_in), (6, 8, y_out3, 16 * CK, y_in3)):
                g.wait_ge(s_, v_)
                g.dma_start(YT[:, a:b].rearrange("p k t c -> p k (t c)"),
                            y_dram.rearrange("(k p) t c -> p k (t c)", p=P)[:, a:b]).then_inc(back, 16)

        def dve(v, link):
            tt, ts, stt = nc.vector.tensor_tensor, nc.vector.tensor_scalar, nc.vector.scalar_tensor_tensor
            wait_done(v, x2_done)
            for k in range(0, KB, 2):
                nc.vector.tensor_copy(HT[:, k, :].rearrange("p (s c) -> p s c", s=CK),
                                      XT[:, k, :].rearrange("p (c s) -> p s c", s=CK)).then_inc(s5_r, 1)

            def cmul(xr, xi, ar_, ai, br, bi, t):
                link(tt(t, ai, bi, ALU.mult))
                link(tt(xr, ar_, br, ALU.mult))
                link(tt(xr, xr, t, ALU.subtract))
                link(tt(t, ai, br, ALU.mult))
                link(tt(xi, ar_, bi, ALU.mult))
                link(tt(xi, xi, t, ALU.add))

            v.wait_ge(s5_ready, 1)
            v.wait_ge(s5_zero, 2)
            for q in range(4):
                j0 = q * QP
                sh = [P, QP, CK, 16]
                pw = [PWR[:, i, 0:CK, j0:j0 + QP].rearrange("p n j -> p j n")[:, :, ::-1].unsqueeze(3)
                      .broadcast_to(sh) for i in range(2)]
                bb = [BB[:, i, j0:j0 + QP, :].unsqueeze(2).broadcast_to(sh) for i in range(2)]
                if q:
                    v.wait_ge(s5_vt, 4 * q)
                t4 = TV.rearrange("p i j c -> p (i j c)")[:, 0:1024].rearrange("p (j s h) -> p j s h", j=QP, s=CK)
                cmul(VB[:, 0], VB[:, 1], pw[0], pw[1], bb[0], bb[1], t4)
                nc.vector.memset(FLAG[:, 0:1], 0.0).then_inc(s5_vb, 1)
                v.wait_ge(s5_v, q + 1)
                v.wait_ge(s5_e, q + 1)
                ps = [PS[:, 4 + 2 * i:6 + 2 * i, :].rearrange("p b (j c) -> p (b j) c", c=NC) for i in range(2)]
                er, ei = EPH[:, 0], EPH[:, 1]
                link(tt(RV[:, 0], ps[0], er, ALU.mult))
                link(tt(RV[:, 1], ps[1], er, ALU.mult))
                link(tt(TV[:, 0], ps[1], ei, ALU.mult))
                link(tt(TV[:, 1], ps[0], ei, ALU.mult))
                nc.vector.memset(FLAG[:, 0:1], 0.0).then_inc(s5_vr, 1)
                link(tt(RV[:, 0], RV[:, 0], TV[:, 0], ALU.add))
                link(tt(RV[:, 1], RV[:, 1], TV[:, 1], ALU.subtract))
                mg = MAGC.rearrange("p j c -> p (j c)")
                for i in range(2):
                    link(nc.vector.tensor_tensor_scan(TV[:, i].rearrange("p j c -> p (j c)"), mg,
                                                      RV[:, i].rearrange("p j c -> p (j c)"), 0.0,
                                                      ALU.mult, ALU.add))
                if q:
                    v.wait_ge(s5_y, 4 * q)
                o = [STT_[:, i, :, 1:NC + 1] for i in range(2)]
                link(tt(RV[:, 0], TV[:, 1], ei, ALU.mult))
                link(tt(RV[:, 1], TV[:, 0], ei, ALU.mult))
                link(tt(o[0], TV[:, 0], er, ALU.mult))
                link(tt(o[1], TV[:, 1], er, ALU.mult))
                link(tt(o[0], o[0], RV[:, 0], ALU.subtract))
                tt(o[1], o[1], RV[:, 1], ALU.add).then_inc(s5_st, 1)
            for k in range(KB):
                v.wait_ge(y_in if k < 6 else y_in3, 16)
                stt(HT[:, k, :].rearrange("p (c t) -> p c t", t=CK), XT[:, k, :].rearrange("p (c t) -> p c t", t=CK),
                    vec("ssm_d", k), YT[:, k].rearrange("p t c -> p c t"), ALU.mult, ALU.add).then_inc(s5_d, 1)
            v.wait_ge(s5_y, 16)
            for k in range(KB):
                v.wait_ge(s5_h, k + 1)
                tt(PTA[:, 1, k, :], HT[:, k, :], PTA[:, 0, k, :].bitcast(F32), ALU.subtract).then_inc(s5_part, 1)

        def act(a, link):
            wait_done(a, x2_done)
            for k in range(1, KB, 2):
                nc.scalar.activation(HT[:, k, :].rearrange("p (s c) -> p s c", s=CK),
                                     XT[:, k, :].rearrange("p (c s) -> p s c", s=CK), ACT.Identity).then_inc(s5_r, 1)
            a.wait_ge(s5_zero, 2)

            def kernels(q):
                if q:
                    a.wait_ge(s5_tp, 16 * CK * q)
                for n, (b, g0) in enumerate(PARITY_BANKS):
                    a.wait_ge(s5_k, 4 * q + n + 1)
                    nc.scalar.activation(KM[0:16, g0:g0 + 7:2, 112:240],
                                         PS[0:16, 4 + b, :].rearrange("p (g n) -> p g n", g=4),
                                         ACT.Identity).then_inc(s5_km, 1)

            def toeplitz(q):
                a.wait_ge(s5_km, 4 * (q + 1))
                for s in range(CK):
                    a.dma_start(TP[16 * s:16 * s + 16], KM[0:16, :, (7 - s) * 16:(7 - s) * 16 + P]).then_inc(s5_tp, 16)

            a.wait_ge(s5_r, KB)
            a.dma_start(u_dram.rearrange("(k p) s c -> p k (s c)", p=P), HT).then_inc(u_out, 16)
            kernels(0)
            toeplitz(0)
            a.wait_ge(u_out, 16)
            for s in range(CK):
                a.dma_start(HT_[16 * s:16 * s + 16, :].rearrange("p (g c) -> p g c", g=NG),
                            u_dram[:, s, :].rearrange("(g h) c -> h g c", h=16)).then_inc(u_in, 16)
            for q in range(4):
                if q:
                    a.wait_ge(s5_v, q)
                for b in range(4):
                    a.wait_ge(s5_vt, 4 * q + b + 1)
                    nc.scalar.activation(VBT[:, 2 * b:2 * b + 2], PS[:, 4 + b, :].rearrange("p (j i n) -> p j i n", j=2, i=2),
                                         ACT.Identity).then_inc(s5_vbt, 1)
                if q < 3:
                    kernels(q + 1)
                for n, (b, g0) in enumerate(PARITY_BANKS):
                    a.wait_ge(s5_y, 4 * q + n + 1)
                    nc.scalar.activation(HT_[:, :].rearrange("p (g c) -> p g c", c=NC)[:, 16 * q + g0:16 * q + g0 + 7:2, :],
                                         PS[:, b, :].rearrange("p (g c) -> p g c", c=NC),
                                         ACT.Identity).then_inc(s5_ye, 1)
                if q < 3:
                    toeplitz(q + 1)
                a.wait_ge(s5_ye, 4 * (q + 1))
                for t in range(CK):
                    a.dma_start(y_dram[256 * q:256 * (q + 1), t, :].rearrange("(g h) c -> h g c", h=16),
                                HT_[16 * t:16 * t + 16, 16 * q * NC:16 * (q + 1) * NC]
                                .rearrange("p (g c) -> p g c", g=16)).then_inc(y_out if q < 3 else y_out3, 16)
            for k in range(KB):
                if k == 0:
                    a.wait_ge(s5_y, 16)
                a.wait_ge(s5_d, k + 1)
                nc.scalar.activation(PTA[:, 0, k, :], HT[:, k, :], ACT.Gelu_apprx_tanh).then_inc(s5_hi, 1)
                a.wait_ge(s5_hi, k + 1)
                nc.scalar.activation(HT[:, k, :], HT[:, k, :], ACT.Gelu_apprx_tanh).then_inc(s5_h, 1)

        def pe(p):
            wait_done(p, x2_done)
            p.wait_ge(s5_ready, 1)

            def kernels(q):
                CL = CLS[q % 2]
                p.wait_ge(s5_cl, q + 1)
                if q:
                    p.wait_ge(s5_vr, q)
                for g in range(16):
                    j, lo = g // 2, 64 * (g % 2)
                    for i in range(2):
                        mm = nc.tensor.matmul(PS[0:16, 4 + 2 * (g % 2) + j // 4, (j % 4) * P:(j % 4 + 1) * P],
                                              BB[lo:lo + 64, i, q * QP + j, :],
                                              CL[lo:lo + 64, i, j, 0:CK, :].rearrange("p n h -> p (n h)"),
                                              start=(i == 0), stop=(i == 1))
                    if j % 4 == 3:
                        mm.then_inc(s5_k, 1)

            kernels(0)
            for q in range(4):
                CL = CLS[q % 2]
                p.wait_ge(s5_vb, q + 1)
                p.wait_ge(s5_km, 4 * (q + 1))
                for n in range(16):
                    j, i = n // 2, n % 2
                    mm = nc.tensor.transpose(PS[:, 4 + n // 4, (n % 4) * P:(n % 4 + 1) * P],
                                             VB[:, i, j].rearrange("p s h -> p (s h)"), IDENT[:, :])
                    if n % 4 == 3:
                        mm.then_inc(s5_vt, 1)
                p.wait_ge(s5_vbt, 4 * (q + 1))
                p.wait_ge(u_in, 16 * CK)
                for g in range(16):
                    j, lo = g // 2, 64 * (g % 2)
                    for i in range(2):
                        mm = nc.tensor.matmul(PS[lo:lo + 64, 4 + 2 * i + j // 4, (j % 4) * NC:(j % 4 + 1) * NC],
                                              VBT[:, j, i, lo:lo + 64],
                                              HT_[:, (16 * q + g) * NC:(16 * q + g + 1) * NC], start=True, stop=True)
                mm.then_inc(s5_v, 1)
                if q < 3:
                    kernels(q + 1)
                p.wait_ge(s5_st, q + 1)
                p.wait_ge(s5_tp, 16 * CK * (q + 1))
                if q:
                    p.wait_ge(s5_ye, 4 * q)
                for g in range(16):
                    j, lo = g // 2, 64 * (g % 2)
                    o = PS[:, 2 * (g % 2) + j // 4, (j % 4) * NC:(j % 4 + 1) * NC]
                    nc.tensor.matmul(o, TP[:, g, :], HT_[:, (16 * q + g) * NC:(16 * q + g + 1) * NC],
                                     start=True, stop=False)
                    for i in range(2):
                        mm = nc.tensor.matmul(o, CL[lo:lo + 64, i, j, 1:CK + 1, :].rearrange("p n h -> p (n h)"),
                                              STT_[lo:lo + 64, i, j, 0:NC], start=False, stop=(i == 1))
                    if j % 4 == 3:
                        mm.then_inc(s5_y, 1)

    PARITY_BANKS = ((0, 0), (2, 1), (1, 8), (3, 9))
    S.append(S5)

    z_part = sem("z_part")
    SG = [SQ[:, :], RINV[:, :]]

    class Glu(Stage):
        name = "glu"
        st = PLAN["glu"]
        done = [(z_part, KB)]

        def banks(j):
            return pair(PLAN["glu"], j) + 2 * (j // 2 % 2)

        def pe(p):
            st = Glu.st
            with p.Fori(0, st.tiles // 4) as it:
                for j in range(4):
                    p.wait_ge(evicted[pair(st, j)], span((st.n0 + j) // 2 - 1, it, 2))
                    split_tile(p, st, j, 2 * Glu.banks(j), [PTA[:, 0], PTA[:, 1]], 0, T, it, 4,
                               block=(lambda k: p.wait_ge(s5_part, k + 1)) if j == 0 else None)

        def act(a, link):
            st = Glu.st
            wait_done(a, [(s5_part, 1)])
            for j in range(-2, st.tiles):
                round_ahead(a, st, j)
                if j > 0 and j % 2:
                    b = j // 2
                    if b >= 2:
                        a.wait_ge(z_part, b - 1)
                    nc.scalar.activation(SG[b % 2], bank2(Glu.banks(j)),
                                         ACT.Sigmoid).then_inc(evicted[pair(st, j)], 1)

        def dve(v, link):
            st = Glu.st
            for b in range(KB):
                pv, pg = pair(st, 2 * b), pair(st, 2 * b + 1)
                wait_sums(v, st, 2 * b)
                v.wait_ge(evicted[pg], (st.n0 + 2 * b + 1) // 2 + 1)
                u, g = bank2(Glu.banks(2 * b)), SG[b % 2]
                nc.vector.tensor_tensor(PTB[:, 0, b, :], u, g, ALU.mult)
                nc.vector.tensor_tensor(g, u, g, ALU.mult).then_inc(evicted[pv], 1)
                v.wait_ge(evicted[pv], (st.n0 + 2 * b) // 2 + 1)
                nc.vector.tensor_tensor(PTB[:, 1, b, :], g, PTB[:, 0, b, :].bitcast(F32),
                                        ALU.subtract).then_inc(z_part, 1)

    S.append(Glu)

    def split_residual(name, norm, src, src_ready, old, old_ready):
        class St(Stage):
            st = PLAN[name]
            done = pairs_done(PLAN[name], 8)

            def pe(p):
                for n in range(8):
                    wait_pair(p, St.st, n)
                    split_tile(p, St.st, n, 2 * pair(St.st, n), [src[:, 0], src[:, 1]], 0, T,
                               block=(lambda k: p.wait_ge(src_ready[0], src_ready[1] + k + 1)) if n == 0 else None)
                    if n:
                        p.wait_ge(evicted[pair(St.st, n - 1)], (St.st.n0 + n - 1) // 2 + 1)
                        NORMS[norm].mean_block(n - 1)

            def act(a, link):
                for n in range(8):
                    round_ahead(a, St.st, n)

            def dve(v, link):
                wait_done(v, old_ready)
                for n in range(8):
                    wait_sums(v, St.st, n)
                    nc.vector.scalar_tensor_tensor(XT[:, n, :], old[:, n, :], ALPHA, bank2(pair(St.st, n)), ALU.mult,
                                                   ALU.add).then_inc(evicted[pair(St.st, n)], 1)

        St.name = name
        S.append(St)
        return St.done

    done = split_residual("s5_out", "ln0", PTB, (z_part, 0), XT, [])
    done = norm_stage("ln0", "layer", XT, XT, T, LN_EPS, lambda k: vec("ln_mix_g", k), lambda k: vec("ln_mix_b", k),
                      done, summed=KB - 1)

    x_hi, x_lo = sem("x_hi"), sem("x_lo")
    hid = sem("hid")
    count = dict.fromkeys(("x", "hid"), 0)
    PIECES = [range(a, min(a + KB, FB)) for a in range(0, FB, KB)]

    def ffn_half(i, half, norm, after):
        gu, down = PLAN["gu%d%s" % (i, "ab"[half])], PLAN["down%d%s" % (i, "ab"[half])]
        x0, hid0 = count["x"], count["hid"]
        count["x"] += KB
        count["hid"] += FB + 2
        final = (i, half) == (1, 1)

        def split_input(v, half, x0, shifted=None):
            for k in range(KB + 1):
                if k < KB:
                    if half == 0:
                        shifted(v, "shifted", k + 1)
                    nc.vector.tensor_copy(XHI[:, k, :], XT[:, k, half * H:(half + 1) * H]).then_inc(x_hi, 1)
                if k:
                    v.wait_ge(x_hi, x0 + k)
                    nc.vector.tensor_tensor(XLO[:, k - 1, :], XT[:, k - 1, half * H:(half + 1) * H],
                                            XHI[:, k - 1, :].bitcast(F32), ALU.subtract).then_inc(x_lo, 1)

        if half == 0:
            NORMS[norm].between = lambda v, wait: split_input(v, 0, x0, wait)

        class St(Stage):
            name, also, done = down.name, gu.name, pairs_done(down, 8)

            def pe(p):
                with p.Fori(0, gu.tiles // 4) as it:
                    for j in range(4):
                        wait_pair(p, gu, j, it, 4)
                        split_tile(p, gu, j, 2 * pair(gu, j), [XHI, XLO], 0, H, it, 4,
                                   block=(lambda k: p.wait_ge(x_lo, x0 + k + 1)) if j == 0 else None)
                with p.Fori(0, 2) as it:
                    for n in range(4):
                        wait_pair(p, down, n, it, 4)
                        for c, ks in enumerate(PIECES):
                            if n == 0:
                                p.wait_ge(hid, hid0 + 2 + ks[-1] + 1)
                            split_tile(p, down, 3 * n + c, 2 * pair(down, n), [HHI, HLO], 0, H, it, 12, ks,
                                       first=(c == 0), last=(c == len(PIECES) - 1))

            def act(a, link):
                wait_done(a, after)
                with a.Fori(0, gu.tiles // 4) as it:
                    for j in range(4):
                        round_ahead(a, gu, j, it, 4)
                        if j % 2 == 0:
                            nc.scalar.activation(GATE[:, (j // 2) * H:(j // 2 + 1) * H],
                                                 PS[:, 2 * pair(gu, j), :],
                                                 ACT.Silu).then_inc(evicted[pair(gu, j)], 1)
                with a.Fori(0, down.tiles // 4 - final) as it:
                    for j in range(4):
                        round_ahead(a, down, j, it, 4)
                if final:
                    for j in range(down.tiles - 4, down.tiles - 2):
                        round_ahead(a, down, j)

            def dve(v, link):
                wait_done(v, after)

                def gate(b, it):
                    j = 2 * b + 1
                    g, f = GATE[:, b * H:(b + 1) * H], HIDF[:, b * H:(b + 1) * H]
                    wait_sums(v, gu, j, it, 4)
                    v.wait_ge(evicted[pair(gu, j - 1)], span((gu.n0 + j - 1) // 2 + 1, it, 2))
                    u = PS[:, 2 * pair(gu, j), :]
                    blk = bass.ds(span(b, it, 2), 1)
                    hi, lo = (t[:, blk, :].rearrange("p a t -> p (a t)") for t in (HHI, HLO))
                    nc.vector.tensor_tensor(hi, u, g, ALU.mult)
                    v.wait_ge(hid, span(hid0 + 2 + b - 1, it, 2))
                    nc.vector.tensor_tensor(f, u, g, ALU.mult).then_inc(evicted[pair(gu, j)], 1)
                    v.wait_ge(evicted[pair(gu, j)], span((gu.n0 + j) // 2 + 1, it, 2))
                    nc.vector.tensor_tensor(lo, f, hi.bitcast(F32), ALU.subtract).then_inc(hid, 1)

                for b in range(2):
                    nc.vector.memset(HIDF[:, b * H:(b + 1) * H], 0.0).then_inc(hid, 1)
                with v.Fori(0, FB // 2) as it:
                    for b in range(2):
                        gate(b, it)
                if half == 0:
                    split_input(v, 1, x0 + KB)
                with v.Fori(0, 2) as it:
                    for n in range(4):
                        wait_sums(v, down, 3 * n + 2, it, 12)
                        x = XT_[:, bass.ds(span(n * T + half * H, it, 4 * T), H)]
                        nc.vector.scalar_tensor_tensor(x, x, ALPHA, PS[:, 2 * pair(down, n), :], ALU.mult,
                                                       ALU.add).then_inc(evicted[pair(down, n)], 1)

        S.append(St)
        return St.done

    def ffn(i, after):
        for half in range(2):
            after = ffn_half(i, half, "ln%d" % i, [] if half else after)
        return norm_stage("ln_f%d" % i, "layer", XT, XT, T, LN_EPS, lambda k: vec("ln_ffn_g", 8 * i + k),
                          lambda k: vec("ln_ffn_b", 8 * i + k), after)

    ffn0_done = ffn(0, done)

    SBD = 64
    n_pairs, PPT = D // P, 4
    C0 = 12288
    QS = [ar(C0 + i * T, T) for i in range(2)]
    KS = [ar(C0 + 2 * T + i * T, T) for i in range(2)]
    VS = [ar(C0 + 4 * T + i * T, T, "p (b n) -> p b n", b=8) for i in range(2)]
    RZ, RE, RP = 6, 3, 4
    ZS = [ar(C0 + 6144 + i * H, H) for i in range(RZ)]
    EL = [ar(C0 + 9216 + i * H, H) for i in range(RE)]
    PP = [ar(C0 + 10752 + i * H, H) for i in range(RP)]
    TRI = ar(C0 + 12800, 3 * P, "p (i n) -> p i n", i=3)
    INCL, STRICT, CAP = TRI[:, 0], TRI[:, 1], TRI[:, 2]
    UN = [(half, j, hd) for half in (1, 0) for j in range(4 * half + 3, -1, -1) for hd in range(2)]
    NU = len(UN)
    BU = NU * PPT
    tri_in = sem("tri_in")
    sb_lin, sb_linv = sem("sb_lin"), sem("sb_linv")
    sb_z, sb_zs, sb_ab, sb_l, sb_p = (sem("sb_" + x) for x in ("z", "zs", "ab", "l", "p"))
    sb_t1, sb_tt, sb_t2, sb_w, sb_pv, sb_o = (sem("sb_" + x) for x in ("t1", "tt", "t2", "w", "pv", "o"))

    def unit(u):
        half, j, hd = UN[u % NU]
        lo = max(P * j - H * half, 0)
        return half, j, hd, H - lo, lo

    def diagonal(u):
        half, j = UN[u % NU][:2]
        return j >= 4 * half

    class Stick(Stage):
        name = "qkv"
        st = PLAN["qkv"]
        after = ffn0_done
        done = [(sb_o, 2 * n_pairs), (sb_linv, 3 * n_pairs), (sb_w, BU * 2)]

        def portion(p, it, pp, i, part):
            st, j = Stick.st, 3 * pp + i
            s = slot(st, j)
            if part == 0:
                p.wait_ge(w_lo, span(st.t0 + j - G0 + 1, it, 3 * PPT))
                if j:
                    p.wait_ge(sb_linv, span(j, it, 3 * PPT))
            w = [WP[:, (st.t0 + j) % 2, x, :].rearrange("p (k n) -> p k n", k=KB) for x in range(2)]
            passes = ((0, 0), (0, 1), (1, 0))
            if i < 2:
                if pp == i == 0:
                    p.wait_ge(xp_lo, part + 1)
                for h in range(2):
                    for q, (a, b) in enumerate(passes):
                        mm = nc.tensor.matmul(PS[:, h, :], w[a][:, part, :], PTB[:, b, part, h * H:(h + 1) * H],
                                              start=(part + q == 0), stop=(part == 7 and q == 2),
                                              skip_group_check=True)
            else:
                for k in range(KB):
                    for q, (a, b) in enumerate(passes):
                        mm = nc.tensor.matmul(PS[:, part // 4, (part % 4) * P:(part % 4 + 1) * P],
                                              PTB[:, b, k, part * P:(part + 1) * P], w[a][:, k, :],
                                              start=(k + q == 0), stop=(k == KB - 1 and q == 2),
                                              skip_group_check=True)
            if part == 7:
                mm.then_inc(w_done[s], 1)

        def pe(p):
            wait_done(p, Stick.after)
            p.wait_ge(tri_in, 16)
            with p.Fori(0, 2) as it:
                v_ = lambda n: span(n, it, BU)
                p.wait_ge(sb_trip, span(1, it, 1))
                for i in range(3):
                    for part in range(8):
                        Stick.portion(p, it, 0, i, part)
                for s in range(BU + 4):
                    pp = s // NU
                    if s < BU:
                        half, j, hd, w, lo = unit(s)
                        if s % NU == 0:
                            p.wait_ge(sb_linv, span(3 * pp + 2, it, 3 * PPT))
                        if s >= 3:
                            p.wait_ge(sb_zs, v_(s - 2))
                        a = half * H + lo
                        nc.tensor.matmul(PS[:, 2 + s % 3, 0:w], KS[pp % 2][SBD * hd:SBD * hd + SBD, j * P:(j + 1) * P],
                                         QS[pp % 2][SBD * hd:SBD * hd + SBD, a:a + w],
                                         start=True, stop=True).then_inc(sb_z, 1)
                    if 2 <= s < BU + 2:
                        u = s - 2
                        half, j, hd, w, lo = unit(u)
                        first = j == 4 * half + 3
                        p.wait_ge(sb_p, v_(u + 1))
                        nc.tensor.matmul(PS[:, 5 + hd, lo:H], INCL, PP[u % RP][:, 0:w], start=first, stop=True,
                                         skip_group_check=True).then_inc(sb_t1, 1)
                    if 3 <= s < BU + 3:
                        u = s - 3
                        half, j, hd, w, lo = unit(u)
                        p.wait_ge(sb_tt, v_(u + 1))
                        nc.tensor.matmul(PS[:, 5 + hd, lo:H], STRICT, PP[u % RP][:, 0:w], start=False, stop=True,
                                         skip_group_check=True).then_inc(sb_t2, 1)
                    if s >= 4:
                        u = s - 4
                        half, j, hd, w, lo = unit(u)
                        first = j == 4 * half + 3
                        p.wait_ge(sb_w, v_(u + 1))
                        if u % NU == 0:
                            p.wait_ge(sb_linv, span(3 * (u // NU + 1), it, 3 * PPT))
                        if first and hd == 0:
                            n = 2 * (u // NU) + (1 - half)
                            if n:
                                p.wait_ge(sb_o, span(n, it, 2 * PPT))
                        nc.tensor.matmul(PS[SBD * hd:SBD * hd + SBD, 7, lo:H],
                                         VS[(u // NU) % 2][:, j, SBD * hd:SBD * hd + SBD], ZS[u % RZ][:, 0:w],
                                         start=first, stop=True, skip_group_check=True).then_inc(sb_pv, 1)
                    if s < BU and pp + 1 < PPT:
                        Stick.portion(p, it, pp + 1, (s % NU) // 8, s % 8)

        def act(a, link):
            wait_done(a, Stick.after)
            a.dma_start(TRI, ins["tri"].rearrange("i p n -> p i n")).then_inc(tri_in, 16)
            a.dma_start(spill, XT).then_inc(x2_spilled, 16)
            for k in range(KB):
                nc.scalar.activation(PTB[:, 0, k, :], XT[:, k, :], ACT.Identity).then_inc(xp_hi, 1)
            nc.scalar.preload_act_table_set("natural_log_exp_and_others")
            with a.Fori(0, 2) as it:
                v_ = lambda n: span(n, it, BU)
                link.enter(it, BU)
                a.wait_ge(sb_trip, span(1, it, 1))

                def linear(pp, i):
                    if i == 2:
                        return
                    j = 3 * pp + i
                    wait_sums(a, Stick.st, j, it, 3 * PPT)
                    if pp >= 2:
                        a.wait_ge(sb_z, v_((pp - 1) * NU))
                    nc.scalar.activation((QS, KS)[i][pp % 2], bank2(0), ACT.Identity,
                                         scale=SBD ** -0.5 if i == 0 else 1.0).then_inc(sb_linv, 1)

                for i in range(3):
                    linear(0, i)
                    round_ahead(a, Stick.st, i, it, 3 * PPT)
                for s in range(BU + 3):
                    if s < BU:
                        w = unit(s)[3]
                        a.wait_ge(sb_z, v_(s + 1))
                        if s >= RZ:
                            a.wait_ge(sb_pv, v_(s - RZ + 1))
                        nc.scalar.activation(ZS[s % RZ][:, 0:w], PS[:, 2 + s % 3, 0:w], ACT.Identity).then_inc(sb_zs, 1)
                    if 1 <= s < BU + 1:
                        u = s - 1
                        w = unit(u)[3]
                        a.wait_ge(sb_ab, v_(u + 1))
                        e = EL[u % RE][:, 0:w]
                        link(nc.scalar.activation(e, e, ACT.Exp))
                        nc.scalar.activation(e, e, ACT.Ln, bias=1.0).then_inc(sb_l, 1)
                    if s >= 3:
                        u = s - 3
                        w = unit(u)[3]
                        a.wait_ge(sb_tt, v_(u + 1))
                        z = ZS[u % RZ][:, 0:w]
                        nc.scalar.activation(z, z, ACT.Exp).then_inc(sb_w, 1)
                    if s < BU and s // NU + 1 < PPT and s % 8 == 7:
                        linear(s // NU + 1, (s % NU) // 8)
                    if s % 8 == 3 and 3 <= s // 8 + 2 < 3 * PPT:
                        round_ahead(a, Stick.st, s // 8 + 2, it, 3 * PPT)
                link.leave(2)

        def dve(v, link):
            wait_done(v, Stick.after)
            for k in range(KB):
                v.wait_ge(xp_hi, k + 1)
                nc.vector.tensor_tensor(PTB[:, 1, k, :], XT[:, k, :], PTB[:, 0, k, :].bitcast(F32),
                                        ALU.subtract).then_inc(xp_lo, 1)
            nc.vector.memset(FLAG[:, 0:1], 0.0).then_inc(sb_trip, 1)
            v.wait_ge(x2_spilled, 16)
            with v.Fori(0, 2) as it:
                v_ = lambda n: span(n, it, BU)

                def linear_v(pp):
                    wait_sums(v, Stick.st, 3 * pp + 2, it, 3 * PPT)
                    if pp >= 2:
                        v.wait_ge(sb_pv, v_((pp - 1) * NU))
                    nc.vector.tensor_copy(VS[pp % 2].rearrange("p b n -> p (b n)"), bank2(0)).then_inc(sb_linv, 1)

                def output(u):
                    v.wait_ge(sb_pv, v_(u + 1))
                    half, pp = unit(u)[0], u // NU
                    at_ = span(pp * T + half * H, it, PPT * T)
                    nc.vector.tensor_copy(XT_[:, bass.ds(at_, H)], PS[:, 7, :]).then_inc(sb_o, 1)

                v.wait_ge(sb_trip, span(1, it, 1))
                linear_v(0)
                for s in range(BU + 6):
                    if s >= 5 and s - 5 < BU and (unit(s - 5)[1], unit(s - 5)[2]) == (0, 1):
                        output(s - 5)
                    if s < BU:
                        w = unit(s)[3]
                        v.wait_ge(sb_zs, v_(s + 1))
                        if s >= RE:
                            v.wait_ge(sb_p, v_(s - RE + 1))
                        z = ZS[s % RZ][:, 0:w]
                        nc.vector.scalar_tensor_tensor(EL[s % RE][:, 0:w], z, -1.0, z, ALU.mult,
                                                       ALU.min).then_inc(sb_ab, 1)
                    if 1 <= s < BU + 1:
                        u = s - 1
                        w = unit(u)[3]
                        pb = PP[u % RP]
                        v.wait_ge(sb_l, v_(u + 1))
                        if u >= RP:
                            v.wait_ge(sb_t2, v_(u - RP + 1))
                        i_ = nc.vector.scalar_tensor_tensor(pb[:, 0:w], ZS[u % RZ][:, 0:w], 0.0, EL[u % RE][:, 0:w],
                                                            ALU.max, ALU.add)
                        if diagonal(u):
                            i_.then_inc(sb_pd, 1)
                            n_diag = sum(diagonal(x) for x in range(u + 1))
                            v.wait_ge(sb_pd, span(n_diag, it, N_DIAG))
                            i_ = nc.vector.tensor_tensor(pb[:, 0:P], pb[:, 0:P], STRICT, ALU.mult)
                        i_.then_inc(sb_p, 1)
                    if 2 <= s < BU + 2:
                        u = s - 2
                        half, j, hd, w, lo = unit(u)
                        z = ZS[u % RZ]
                        v.wait_ge(sb_t1, v_(u + 1))
                        i_ = nc.vector.tensor_tensor(z[:, 0:w], z[:, 0:w], PS[:, 5 + hd, lo:H], ALU.subtract)
                        if diagonal(u):
                            i_.then_inc(sb_td, 1)
                            n_diag = sum(diagonal(x) for x in range(u + 1))
                            v.wait_ge(sb_td, span(n_diag, it, N_DIAG))
                            i_ = nc.vector.tensor_tensor(z[:, 0:P], z[:, 0:P], CAP, ALU.min)
                        i_.then_inc(sb_tt, 1)
                    if s < BU and s // NU + 1 < PPT and s % NU == NU - 1:
                        linear_v(s // NU + 1)
                v.wait_ge(sb_o, span(2 * PPT, it, 2 * PPT))
                nc.vector.memset(FLAG[:, 0:1], 0.0).then_inc(sb_trip, 1)

    xp_hi, xp_lo, x2_spilled, x2_back = sem("xp_hi"), sem("xp_lo"), sem("x2_spilled"), sem("x2_back")
    o_hi, o_lo = sem("o_hi"), sem("o_lo")
    sb_trip = sem("sb_trip")
    sb_pd, sb_td = sem("sb_p_diag"), sem("sb_t_diag")
    N_DIAG = sum(diagonal(u) for u in range(BU))
    S.append(Stick)

    class OutputParts(Stage):
        name = "sb_parts"

        def act(a, link):
            wait_done(a, Stick.done)
            a.dma_start(HT, spill).then_inc(x2_back, 16)
            for k in range(KB):
                nc.scalar.activation(PTA[:, 0, k, :], XT[:, k, :], ACT.Identity).then_inc(o_hi, 1)

        def dve(v, link):
            wait_done(v, Stick.done)
            for k in range(KB):
                v.wait_ge(o_hi, k + 1)
                nc.vector.tensor_tensor(PTA[:, 1, k, :], XT[:, k, :], PTA[:, 0, k, :].bitcast(F32),
                                        ALU.subtract).then_inc(o_lo, 1)

    S.append(OutputParts)
    done = split_residual("sb_out", "ln1", PTA, (o_lo, 0), HT, [(x2_back, 16)])
    done = norm_stage("ln1", "layer", XT, XT, T, LN_EPS, lambda k: vec("ln_mix_g", 8 + k),
                      lambda k: vec("ln_mix_b", 8 + k), done,
                      summed=KB - 1)
    done = ffn(1, done)

    out_done = sem("out_done")

    stages = S if stop is None else S[:[s.name for s in S].index(stop) + 1]
    runs = []
    for st in (PLAN[n] for n in PLAN if n in [s.name for s in stages] or n in [s.also for s in stages]):
        if runs and runs[-1][1] == st.t0 and runs[-1][2] + st.t0 - runs[-1][0] == st.dram:
            runs[-1][1] = st.t0 + st.tiles
        else:
            runs.append([st.t0, st.t0 + st.tiles, st.dram])
    n_tiles = runs[-1][1]
    if stop is not None:
        runs[-1][1] += RING

    block = ctx.enter_context(nc.Block())

    @block.sync
    def _(sp):
        Setup.sp(sp)
        EvIn.sp(sp)
        for s in range(RING):
            sp.dma_start(W[:, s], ins["weights"][s].rearrange("p (k n) -> p k n", k=KB)).then_inc(w_full[s], 16)
        for t0, t1, dram in runs:
            with sp.Fori(1 if t0 == 0 else 0, (t1 - t0) // RING) as it:
                for s in range(RING):
                    sp.wait_ge(w_done[s], it if t0 == 0 else span(t0 // RING, it, 1))
                    sp.dma_start(W[:, s], ins["weights"][bass.ds(span(dram + s, it, RING), 1)]
                                 .rearrange("a p (k n) -> p (a k) n", k=KB)).then_inc(w_full[s], 16)
        result = out.rearrange("(k p) t -> p k t", p=P)
        if stop is not None:
            wait_done(sp, stages[-1].done)
            sp.dma_start(result, XT).then_inc(out_done, 16)
            sp.wait_ge(out_done, 16)
        else:
            for i in range(4):
                sp.wait_ge(n_sem["shifted"], n_count["shifted"] - 2 * KB + 4 * (i + 1))
                ks, ts = slice(4 * (i % 2), 4 * (i % 2) + 4), slice(i // 2 * H, (i // 2 + 1) * H)
                sp.dma_start(result[:, ks, ts], XT[:, ks, ts]).then_inc(out_done, 16)
            sp.wait_ge(out_done, 64)

    @block.tensor
    def _(pe):
        for s in stages:
            if s.pe is not None:
                s.pe(pe)

    @block.scalar
    def _(act):
        link = Link(act, "act")
        for s in stages:
            if s.act is not None:
                s.act(act, link)

    @block.vector
    def _(dve):
        link = Link(dve, "dve")
        for s in stages:
            if s.dve is not None:
                s.dve(dve, link)

    @block.gpsimd
    def _(pool):
        link = Link(pool, "pool")
        for s in stages:
            if s.pool is not None:
                s.pool(pool, link)
        if n_tiles > G0:
            with pool.Fori(0, (n_tiles - G0) // RING) as it:
                for j in range(RING):
                    g = G0 + j
                    pool.wait_ge(w_hi, span(j + 1, it, RING))
                    nc.gpsimd.tensor_tensor(WP[:, g % 2, 1, :], WR[:, (g % RING) * TILE:(g % RING + 1) * TILE],
                                            WP[:, g % 2, 0, :].bitcast(F32), ALU.subtract).then_inc(w_lo, 1)


def tiles_of(w):
    k, n = w.shape
    kb = k // P
    t = w.reshape(kb, P, n // P, P).transpose(2, 1, 0, 3)
    pieces = []
    for a in range(0, kb, KB):
        piece = np.zeros((n // P, P, KB, P), np.float32)
        piece[:, :, :min(KB, kb - a)] = t[:, :, a:a + KB]
        pieces.append(piece.reshape(n // P, P, TILE))
    return np.stack(pieces, 1)


def pack_weights(x):
    m0, m1 = (tiles_of(x["w_mod"][i]) for i in range(2))
    out = [m0]
    ev = tiles_of(x["ev_w_in"][0])[:, 0]
    out.append(ev[[0, 1, 2, 3, 10, 11, 10, 11, 12, 13, 12, 13, 4, 5, 6, 7, 8, 9, 14, 15, 16, 17, 18, 19]])
    out.append(np.concatenate([m1.reshape(8, 3, P, TILE), tiles_of(x["ev_w_out"][0])], 1))
    od = tiles_of(x["od_w_in"][0])[:, 0]
    out.append(od[24:28])
    for c in range(3):
        out.append(od[[g + 2 * c + i for g in (0, 6, 12, 18) for i in range(2)]])
    out.append(tiles_of(x["od_w_out"][0])[:, 0])
    glu = tiles_of(x["ssm_w_glu_2"][0])[:, 0]
    out.append(glu[[i // 2 + 8 * (i % 2) for i in range(16)]])
    out.append(tiles_of(x["ssm_w_out_2"][0])[:, 0])

    def ffn(i):
        gu = tiles_of(x["ffn_w_gu_2"][i])[:, 0]
        return [gu[[n // 2 + FB * (n % 2) for n in range(2 * FB)]],
                tiles_of(x["ffn_w_down_2"][i]).reshape(-1, P, TILE)]

    out += ffn(0)
    qkv = tiles_of(x["sb_w_qkv_2"][0])[:, 0]
    out.append(qkv[[n for pr in range(8) for n in (pr, 8 + pr, 16 + pr)]])
    out.append(tiles_of(x["sb_w_o_2"][0])[:, 0])
    out += ffn(1)
    return np.concatenate([o.reshape(-1, P, TILE) for o in out])


def pack_vectors(x):
    cols = {
        "cond": np.stack([x["c"][0], x["c_ctx"]], 1).reshape(KB, P, 2).transpose(1, 0, 2).reshape(P, 16),
        "conv_w": x["hy_conv_w"][0].reshape(3, 18, P).transpose(2, 1, 0).reshape(P, 54),
    }
    plain = {"b_mod": x["b_mod"], "norm_g": x["norm_g"], "pool_scale": x["pool_scale"], "q_g": x["q_norm_g"],
             "k_g": x["k_norm_g"], "conv_b": x["hy_conv_b"], "final_g": x["final_g"], "ssm_d": x["ssm_d_2"],
             "ln_mix_g": x["ln_mix_g_2"], "ln_mix_b": x["ln_mix_b_2"], "ln_ffn_g": x["ln_ffn_g_2"],
             "ln_ffn_b": x["ln_ffn_b_2"]}
    for name, a in plain.items():
        cols[name] = a.reshape(-1, P).T
    for name in ("hy_b1", "hy_b2", "hy_freq"):
        col = np.zeros((P, 1), np.float32)
        col[0:64, 0] = x[name][0]
        cols[name] = col
    return np.concatenate([cols[name] for name in VECS], 1)


def shape_tables():
    t = np.arange(T)
    inv_freq = 10000.0 ** (-np.arange(32) / 32)
    p = np.arange(P)
    pos = np.where((p // 64)[:, None] == 0, (t // 64)[None], (t % 64)[None])
    ang = pos * inv_freq[p % 32][:, None]
    swap = np.zeros((P, P))
    for m in range(P):
        if (m // 32) % 2 == 0:
            swap[m + 32, m] = -1.0
        else:
            swap[m - 32, m] = 1.0
    inv = np.zeros((2, P, T))
    for g, w in enumerate((2, 4, 8, 16)):
        cnt = np.clip(t + w // 2, 0, T) - np.clip(t - w // 2, 0, T)
        inv[g // 2, (g % 2) * 64:(g % 2) * 64 + 64] = 1.0 / cnt
    return {"rope": np.stack([np.cos(ang), np.sin(ang)]), "rope_swap": swap, "invcnt": inv, "ident": np.eye(P)}


def pack(inputs):
    x = {k: np.asarray(v) for k, v in inputs.items()}
    arrays = {k: np.ascontiguousarray(v, np.float32) for k, v in shape_tables().items()}
    arrays["xT"] = np.ascontiguousarray(x["x"][0].T)
    arrays["ctxT"] = np.ascontiguousarray(x["ctx"][0].T)
    arrays["weights"] = pack_weights(x)
    arrays["vecs"] = np.ascontiguousarray(pack_vectors(x))
    pool_w = np.zeros((2, P, P), np.float32)
    for g in range(4):
        lo = (g % 2) * 64
        pool_w[g // 2, lo:lo + 64, lo:lo + 64] = x["pool_w"][0, g]
    arrays["pool_w"] = pool_w
    more_arrays(x, arrays)
    return arrays


def more_arrays(x, arrays):
    f32 = np.float32
    arrays["hy_w1"] = np.ascontiguousarray(x["hy_w1"][0])
    arrays["hy_w2"] = np.ascontiguousarray(x["hy_w2"][0])
    arrays["hy_w3"] = np.ascontiguousarray(
        x["hy_w3"][0].reshape(64, 2, 2, 3, 256).transpose(3, 1, 0, 2, 4).reshape(6, 64, 512))
    arrays["fn_w"] = np.ascontiguousarray(x["fn_w"][0])
    deltas = np.abs(np.linspace(np.log(1e-2) / 1.5, np.log(1e-2) / 0.3, HYW))
    rows = np.concatenate([deltas.astype(f32).reshape(1, 3, 256), x["hy_skip"][0].reshape(2, 3, 256)])
    arrays["hy_rows"] = np.ascontiguousarray(
        np.broadcast_to(rows.transpose(1, 0, 2).reshape(3, 1, 768), (3, P, 768)))
    lin = np.linspace(0.0, 1.0, T)
    w = 2 * np.pi * np.arange(T) / T
    f = np.linspace(1e-4, 15, 16)
    ang = f[:, None] * w[None]
    arrays["hy_emb"] = np.concatenate([lin[None], np.cos(ang), -np.sin(ang)]).astype(f32)
    tok = np.arange(8)[None] // 4 + 2 * ((np.arange(8)[None] % 4) * P + np.arange(P)[:, None])
    first = np.ones((P, 1))
    first[0] = 0.0
    alt = 1.0 - 2.0 * (np.arange(P)[:, None] % 2)
    arrays["hy_cols"] = np.concatenate([-lin[tok], first, -first, alt], 1).astype(f32)
    u, m = np.arange(H)[:, None], np.arange(H)[None]
    even, odd = 2 * np.pi * (m + 0.5) * (2 * u) / 2048, 2 * np.pi * (m + 0.5) * (2 * u + 1) / 2048
    arrays["hy_dft"] = np.stack([np.cos(even), np.cos(odd), np.sin(even), np.sin(odd),
                                 np.cos(even).T, np.sin(even).T]).astype(f32)
    st = np.outer(np.arange(T), np.arange(H)) % T
    arrays["fn_seq"] = np.stack([np.cos(2 * np.pi * st / T), np.sin(2 * np.pi * st / T)]).astype(f32)
    cc = np.outer(np.arange(256), np.arange(256)) % 256
    arrays["fn_ch"] = (np.stack([np.cos(2 * np.pi * cc / 256), np.sin(2 * np.pi * cc / 256)]) / 512).astype(f32)
    yet_more(x, arrays)


def yet_more(x, arrays):
    def by_state(a):
        a = a.reshape((32, 2, 64) + a.shape[2:])
        return np.moveaxis(a, 0, 2).reshape((P, 32) + a.shape[3:])

    a_re, a_im = by_state(x["ssm_a_re_2"][0]), by_state(x["ssm_a_im_2"][0])
    ldt = by_state(np.repeat(x["ssm_log_dt_2"][0][:, None], 64, 1))
    arrays["s5_par"] = np.ascontiguousarray(np.stack([a_re, a_im, ldt], 1).reshape(P, 96))
    b = [by_state(x[n][0]) for n in ("ssm_b_re_2", "ssm_b_im_2")]
    c = [by_state(x[n][0].transpose(0, 2, 1)) for n in ("ssm_c_re_2", "ssm_c_im_2")]
    arrays["s5_bc"] = np.ascontiguousarray(np.stack(b + c, 1).reshape(P, 2048))
    r, s = np.arange(P)[:, None], np.arange(P)[None]
    arrays["tri"] = np.stack([r >= s, r < s, np.where(r < s, 3e38, -1e30)]).astype(np.float32)


def kernel(**inputs):
    import concourse.bacc as _bacc
    from concourse.bass_utils import run_bass_kernel_spmd as _run

    arrays = pack(inputs)
    nc = _bacc.Bacc("TRN2", target_bir_lowering=False, num_devices=1)
    ins = {n: nc.dram_tensor("in_" + n, a.shape, F32, kind="ExternalInput").ap() for n, a in arrays.items()}
    out = nc.dram_tensor("out", (D, T), F32, kind="ExternalOutput").ap()
    build(nc, ins, out)
    r = _run(nc, [{"in_" + n: a for n, a in arrays.items()}], core_ids=[0])
    return np.ascontiguousarray(r.results[0]["out"].T).reshape(1, T, D)
```
